# Optimizing a Trainium2 kernel written in Bass

```python
import functools
import jax, jax.numpy as jnp
from jax import lax
import numpy as np

D_MODEL = 1024
BATCH = 1
SEQ = 1024
DEPTH = 1
DEC_BATCH = 8
DEC_SEQ = 8
PAST_LEN = 2048
PAGE_SIZE = 128

D_MIX = D_MODEL
HEAD_DIM = 64
NSA_WIDTH = D_MIX // 2
NSA_HEADS = NSA_WIDTH // HEAD_DIM
NSA_KV = 2
NSA_G = NSA_HEADS // NSA_KV
CMP_BLOCK = 64
SEL_BLOCK = 64
TOP_K = 16
WINDOW = 512
Q_BLOCK = 128
GLA_WIDTH = D_MIX // 4
GLA_HEADS = 4
GLA_DV = GLA_WIDTH // GLA_HEADS
GLA_DK = GLA_DV // 2
GLA_RANK = 16
GLA_TAU = 16.0
GLA_CHUNK = 64
CONV_WIDTH = D_MIX - NSA_WIDTH - GLA_WIDTH
CONV_K = 3
EPS = 1e-6
NEG = -1e30
FORCE = 1e4

PROJ_LAYOUT = (
    ('nsa_q', NSA_WIDTH),
    ('nsa_cmp', 2 * NSA_KV * HEAD_DIM),
    ('nsa_slc', 2 * NSA_KV * HEAD_DIM),
    ('nsa_win', 2 * NSA_KV * HEAD_DIM),
    ('nsa_gate', 3 * NSA_HEADS),
    ('nsa_z', NSA_WIDTH),
    ('gla_q', GLA_HEADS * GLA_DK),
    ('gla_k', GLA_HEADS * GLA_DK),
    ('gla_v', GLA_WIDTH),
    ('gla_a', GLA_RANK),
    ('gla_z', GLA_WIDTH),
    ('conv_b', CONV_WIDTH),
    ('conv_c', CONV_WIDTH),
    ('conv_h', CONV_WIDTH),
    ('conv_z', CONV_WIDTH),
)
PROJ_COLS = sum(w for _, w in PROJ_LAYOUT)

kernel_name = 'hymba_nsa_gla_shortconv_step'

def rmsnorm(x, g):
    xf = x.astype(jnp.float32)
    xf = xf * lax.rsqrt(jnp.mean(xf * xf, axis=-1, keepdims=True) + EPS)
    return xf.astype(x.dtype) * g

def masked_softmax(s, mask):
    s = jnp.where(mask, s.astype(jnp.float32), NEG)
    return jax.nn.softmax(s, axis=-1) * mask

def in_proj(h, w_in):
    p = jnp.einsum('btd,dc->btc', h, w_in)
    out, off = {}, 0
    for name, width in PROJ_LAYOUT:
        out[name] = p[..., off:off + width]
        off += width
    return out

def compress_blocks(kv, w_ck, w_cv):
    b_, t_ = kv.shape[:2]
    kb = kv.reshape(b_, t_ // CMP_BLOCK, CMP_BLOCK, 2, NSA_KV, HEAD_DIM)
    w = jnp.stack([w_ck, w_cv], axis=-1)
    return jnp.einsum('bnlchd,lc->bnchd', kb, w)

def nsa_core(q, qpos, gates, kv_cmp, gather_sel, kv_band, band_pos, n_blocks):
    dt = q.dtype
    qs = q * (HEAD_DIM ** -0.5)
    nc = kv_cmp.shape[1]
    cmp_end = (jnp.arange(nc) + 1) * CMP_BLOCK - 1
    m_c = (cmp_end[None, :] <= qpos[:, None])[None, :, None, None, :]
    p_c = masked_softmax(jnp.einsum('bqhgd,bchd->bqhgc', qs, kv_cmp[:, :, 0]), m_c)
    o_c = jnp.einsum('bqhgc,bchd->bqhgd', p_c.astype(dt), kv_cmp[:, :, 1])
    imp = jnp.pad(p_c.sum(axis=3), ((0, 0), (0, 0), (0, 0), (0, n_blocks - nc)))
    blk = jnp.arange(n_blocks)[None, :]
    cur = (qpos // SEL_BLOCK)[:, None]
    forced = ((blk == 0) | (blk == cur) | (blk == cur - 1))[None, :, None, :]
    visible = (blk <= cur)[None, :, None, :]
    score = jnp.where(forced, FORCE, jnp.where(visible, imp, -1.0))
    _, idx = lax.top_k(score, min(TOP_K, n_blocks))
    b_, q_, h_, j_ = idx.shape
    kv_sel = gather_sel(idx).reshape(b_, q_, h_, j_ * SEL_BLOCK, 2, HEAD_DIM)
    tok = (idx[..., None] * SEL_BLOCK + jnp.arange(SEL_BLOCK)).reshape(b_, q_, h_, j_ * SEL_BLOCK)
    m_s = (tok <= qpos[None, :, None, None])[:, :, :, None, :]
    p_s = masked_softmax(jnp.einsum('bqhgd,bqhkd->bqhgk', qs, kv_sel[..., 0, :]), m_s)
    o_s = jnp.einsum('bqhgk,bqhkd->bqhgd', p_s.astype(dt), kv_sel[..., 1, :])
    dpos = qpos[:, None] - band_pos[None, :]
    m_w = ((dpos >= 0) & (dpos < WINDOW) & (band_pos[None, :] >= 0))[None, :, None, None, :]
    p_w = masked_softmax(jnp.einsum('bqhgd,bkhd->bqhgk', qs, kv_band[:, :, 0]), m_w)
    o_w = jnp.einsum('bqhgk,bkhd->bqhgd', p_w.astype(dt), kv_band[:, :, 1])
    return gates[..., 0:1] * o_c + gates[..., 1:2] * o_s + gates[..., 2:3] * o_w

def nsa_prompt(q, gates, kv_c, kv_s, kv_w, w_ck, w_cv):
    b_, s_ = q.shape[:2]
    nb = s_ // SEL_BLOCK
    kv_cmp = compress_blocks(kv_c[:, :(s_ // CMP_BLOCK) * CMP_BLOCK], w_ck, w_cv)
    kb = kv_s.reshape(b_, nb, SEL_BLOCK, 2, NSA_KV, HEAD_DIM)
    bi = jnp.arange(b_)[:, None, None, None]
    gi = jnp.arange(NSA_KV)[None, None, :, None]

    def gather_sel(idx):
        return kb[bi, idx, :, :, gi]

    kvw_pad = jnp.pad(kv_w, ((0, 0), (WINDOW, 0), (0, 0), (0, 0), (0, 0)))
    qb = min(Q_BLOCK, s_)

    def block(i):
        q0 = i * qb
        qpos = q0 + jnp.arange(qb)
        band = lax.dynamic_slice_in_dim(kvw_pad, q0, qb + WINDOW, axis=1)
        band_pos = q0 - WINDOW + jnp.arange(qb + WINDOW)
        return nsa_core(lax.dynamic_slice_in_dim(q, q0, qb, axis=1), qpos,
                        lax.dynamic_slice_in_dim(gates, q0, qb, axis=1),
                        kv_cmp, gather_sel, band, band_pos, nb)

    o = lax.map(block, jnp.arange(s_ // qb))
    o = jnp.moveaxis(o, 0, 1).reshape(b_, s_, NSA_KV, NSA_G, HEAD_DIM)
    w_keep = min(WINDOW, s_)
    return o, (kv_c, kv_s, kv_w[:, s_ - w_keep:])

def nsa_sample(q, gates, kv_c, kv_s, kv_w, l, w_ck, w_cv, cache_cmp_kv, cache_slc_kv, win_buf, page_table):
    bd, t_new = q.shape[:2]
    past = cache_cmp_kv[l, page_table].reshape(bd, PAST_LEN, 2, NSA_KV, HEAD_DIM)
    total = PAST_LEN + t_new
    nc = total // CMP_BLOCK
    full = jnp.concatenate([past, kv_c], axis=1)[:, :nc * CMP_BLOCK]
    kv_cmp = compress_blocks(full, w_ck, w_cv)
    n_past_blk = PAST_LEN // SEL_BLOCK
    n_new_blk = -(-t_new // SEL_BLOCK)
    nb = n_past_blk + n_new_blk
    sub = PAGE_SIZE // SEL_BLOCK
    new_blk = jnp.pad(kv_s, ((0, 0), (0, n_new_blk * SEL_BLOCK - t_new), (0, 0), (0, 0), (0, 0)))
    new_blk = new_blk.reshape(bd, n_new_blk, SEL_BLOCK, 2, NSA_KV, HEAD_DIM)
    bi = jnp.arange(bd)[:, None, None, None]
    gi = jnp.arange(NSA_KV)[None, None, :, None]

    def gather_sel(idx):
        jp = jnp.minimum(idx, n_past_blk - 1)
        phys = page_table[bi, jp // sub]
        rows = (jp % sub)[..., None] * SEL_BLOCK + jnp.arange(SEL_BLOCK)
        from_pool = cache_slc_kv[l, phys[..., None], rows, :, gi[..., None]]
        jn = jnp.clip(idx - n_past_blk, 0, n_new_blk - 1)
        from_new = new_blk[bi, jn, :, :, gi]
        return jnp.where((idx < n_past_blk)[..., None, None, None], from_pool, from_new)

    w_buf = win_buf.shape[1]
    band = jnp.concatenate([win_buf, kv_w], axis=1)
    band_pos = PAST_LEN - w_buf + jnp.arange(w_buf + t_new)
    qpos = PAST_LEN + jnp.arange(t_new)
    o = nsa_core(q, qpos, gates, kv_cmp, gather_sel, band, band_pos, nb)
    return o, (kv_c, kv_s, band[:, band.shape[1] - w_buf:])

def gla_chunked(q, k, v, log_a, s0):
    b_, t_ = q.shape[:2]
    c = min(GLA_CHUNK, t_)
    n = -(-t_ // c)
    pad = n * c - t_

    def to_chunks(a):
        a = jnp.pad(a, ((0, 0), (0, pad), (0, 0), (0, 0)))
        return a.reshape(b_, n, c, a.shape[2], a.shape[3]).transpose(1, 0, 3, 2, 4)

    causal = jnp.tril(jnp.ones((c, c), dtype=bool))[:, :, None]

    def step(s, xs):
        qi, ki, vi, ai = (a.astype(jnp.float32) for a in xs)
        bcum = jnp.cumsum(ai, axis=2)
        inter = jnp.einsum('bhtk,bhkv->bhtv', qi * jnp.exp(bcum), s)
        diff = bcum[:, :, :, None, :] - bcum[:, :, None, :, :]
        decay = jnp.exp(jnp.where(causal, diff, -jnp.inf))
        att = jnp.einsum('bhtk,bhsk,bhtsk->bhts', qi, ki, decay)
        o = inter + jnp.einsum('bhts,bhsv->bhtv', att, vi)
        blast = bcum[:, :, -1:, :]
        s = jnp.exp(blast[:, :, 0, :])[..., None] * s + jnp.einsum('bhsk,bhsv->bhkv', ki * jnp.exp(blast - bcum), vi)
        return s, o

    s, o = lax.scan(step, s0.astype(jnp.float32), (to_chunks(q), to_chunks(k), to_chunks(v), to_chunks(log_a)))
    o = o.transpose(1, 0, 3, 2, 4).reshape(b_, n * c, q.shape[2], v.shape[3])[:, :t_]
    return o.astype(v.dtype), s

def short_conv(u, buf, w):
    t_ = u.shape[1]
    up = jnp.concatenate([buf.astype(u.dtype), u], axis=1)
    y = sum(up[:, i:i + t_] * w[i] for i in range(CONV_K))
    return y, up[:, up.shape[1] - (CONV_K - 1):]

def layer_forward(x, l, W, nsa_fn, gla_s0, conv_buf):
    b_, t_ = x.shape[:2]
    p = in_proj(rmsnorm(x, W['norm_pre'][l]), W['w_in'][l])
    q = p['nsa_q'].reshape(b_, t_, NSA_KV, NSA_G, HEAD_DIM)
    gates = jax.nn.sigmoid(p['nsa_gate'].reshape(b_, t_, NSA_KV, NSA_G, 3))
    kv_c = p['nsa_cmp'].reshape(b_, t_, 2, NSA_KV, HEAD_DIM)
    kv_s = p['nsa_slc'].reshape(b_, t_, 2, NSA_KV, HEAD_DIM)
    kv_w = p['nsa_win'].reshape(b_, t_, 2, NSA_KV, HEAD_DIM)
    o_nsa, (new_c, new_s, new_w) = nsa_fn(q, gates, kv_c, kv_s, kv_w)
    o_nsa = o_nsa.reshape(b_, t_, NSA_WIDTH) * jax.nn.silu(p['nsa_z'])
    gq = p['gla_q'].reshape(b_, t_, GLA_HEADS, GLA_DK) * (GLA_DK ** -0.5)
    gk = p['gla_k'].reshape(b_, t_, GLA_HEADS, GLA_DK)
    gv = p['gla_v'].reshape(b_, t_, GLA_HEADS, GLA_DV)
    a_logit = jnp.einsum('btr,rk->btk', p['gla_a'], W['gla_a2'][l]) + W['gla_ab'][l]
    log_a = (jax.nn.log_sigmoid(a_logit.astype(jnp.float32)) / GLA_TAU).reshape(b_, t_, GLA_HEADS, GLA_DK)
    o_gla, s_gla = gla_chunked(gq, gk, gv, log_a, gla_s0)
    o_gla = rmsnorm(o_gla, W['gla_norm'][l]).reshape(b_, t_, GLA_WIDTH) * jax.nn.silu(p['gla_z'])
    y_conv, new_buf = short_conv(p['conv_c'] * p['conv_h'], conv_buf, W['conv_w'][l])
    o_conv = p['conv_b'] * y_conv * jax.nn.silu(p['conv_z'])
    mix = jnp.concatenate([o_nsa, o_gla, o_conv], axis=-1)
    out = jnp.einsum('btc,cd->btd', mix, W['w_out'][l])
    x = x + rmsnorm(out, W['norm_post'][l])
    return x, (new_c, new_s, new_w, s_gla.astype(x.dtype), new_buf)

def setup_inputs(seed: int = 0) -> dict:
    key = jax.random.key(seed)
    ks = jax.random.split(key, 20)
    nrm = jax.random.normal
    n_pages = PAST_LEN // PAGE_SIZE
    n_pool = (DEC_BATCH * n_pages * 5) // 4
    w_buf = min(WINDOW, PAST_LEN)
    kv_tail = (2, NSA_KV, HEAD_DIM)
    page_table = jax.random.permutation(ks[7], n_pool)[:DEC_BATCH * n_pages]
    return {
        'x_prompt': nrm(ks[0], (BATCH, SEQ, D_MODEL), jnp.float32),
        'x_sample': nrm(ks[1], (DEC_BATCH, DEC_SEQ, D_MODEL), jnp.float32),
        'cache_cmp_kv': nrm(ks[2], (DEPTH, n_pool, PAGE_SIZE) + kv_tail, jnp.float32),
        'cache_slc_kv': nrm(ks[3], (DEPTH, n_pool, PAGE_SIZE) + kv_tail, jnp.float32),
        'cache_win_kv': nrm(ks[4], (DEPTH, DEC_BATCH, w_buf) + kv_tail, jnp.float32),
        'state_gla': 0.5 * nrm(ks[5], (DEPTH, DEC_BATCH, GLA_HEADS, GLA_DK, GLA_DV), jnp.float32),
        'state_conv': nrm(ks[6], (DEPTH, DEC_BATCH, CONV_K - 1, CONV_WIDTH), jnp.float32),
        'page_table': page_table.reshape(DEC_BATCH, n_pages).astype(jnp.int32),
        'norm_pre': 1.0 + 0.1 * nrm(ks[8], (DEPTH, D_MODEL), jnp.float32),
        'norm_post': 1.0 + 0.1 * nrm(ks[9], (DEPTH, D_MODEL), jnp.float32),
        'w_in': nrm(ks[10], (DEPTH, D_MODEL, PROJ_COLS), jnp.float32) * D_MODEL ** -0.5,
        'w_out': nrm(ks[11], (DEPTH, D_MIX, D_MODEL), jnp.float32) * D_MIX ** -0.5,
        'w_cmp_k': (1.0 + 0.1 * nrm(ks[12], (DEPTH, CMP_BLOCK), jnp.float32)) / CMP_BLOCK,
        'w_cmp_v': (1.0 + 0.1 * nrm(ks[13], (DEPTH, CMP_BLOCK), jnp.float32)) / CMP_BLOCK,
        'gla_a2': nrm(ks[14], (DEPTH, GLA_RANK, GLA_HEADS * GLA_DK), jnp.float32) * GLA_RANK ** -0.5,
        'gla_ab': 0.1 * nrm(ks[15], (DEPTH, GLA_HEADS * GLA_DK), jnp.float32),
        'gla_norm': 1.0 + 0.1 * nrm(ks[16], (DEPTH, GLA_DV), jnp.float32),
        'conv_w': nrm(ks[17], (DEPTH, CONV_K, CONV_WIDTH), jnp.float32) * CONV_K ** -0.5,
    }

def reference(x_prompt, x_sample, cache_cmp_kv, cache_slc_kv, cache_win_kv, state_gla, state_conv, page_table,
              norm_pre, norm_post, w_in, w_out, w_cmp_k, w_cmp_v, gla_a2, gla_ab, gla_norm, conv_w):
    W = {'norm_pre': norm_pre, 'norm_post': norm_post, 'w_in': w_in, 'w_out': w_out,
         'gla_a2': gla_a2, 'gla_ab': gla_ab, 'gla_norm': gla_norm, 'conv_w': conv_w}
    xp, xs = x_prompt, x_sample
    st_p, st_s = [], []
    for l in range(DEPTH):
        nsa_p = functools.partial(nsa_prompt, w_ck=w_cmp_k[l], w_cv=w_cmp_v[l])
        gla0 = jnp.zeros((xp.shape[0], GLA_HEADS, GLA_DK, GLA_DV), jnp.float32)
        conv0 = jnp.zeros((xp.shape[0], CONV_K - 1, CONV_WIDTH), xp.dtype)
        xp, sp = layer_forward(xp, l, W, nsa_p, gla0, conv0)
        nsa_s = functools.partial(nsa_sample, l=l, w_ck=w_cmp_k[l], w_cv=w_cmp_v[l],
                                  cache_cmp_kv=cache_cmp_kv, cache_slc_kv=cache_slc_kv,
                                  win_buf=cache_win_kv[l], page_table=page_table)
        xs, ss = layer_forward(xs, l, W, nsa_s, state_gla[l], state_conv[l])
        st_p.append(sp)
        st_s.append(ss)
    new_cmp_p = jnp.stack([s[0] for s in st_p])
    new_cmp_s = jnp.stack([s[0] for s in st_s])
    new_slc_p = jnp.stack([s[1] for s in st_p])
    new_slc_s = jnp.stack([s[1] for s in st_s])
    new_win_p = jnp.stack([s[2] for s in st_p])
    new_win_s = jnp.stack([s[2] for s in st_s])
    new_gla_p = jnp.stack([s[3] for s in st_p])
    new_gla_s = jnp.stack([s[3] for s in st_s])
    new_conv_p = jnp.stack([s[4] for s in st_p])
    new_conv_s = jnp.stack([s[4] for s in st_s])
    return (xp, xs, new_cmp_p, new_cmp_s, new_slc_p, new_slc_s, new_win_p, new_win_s,
            new_gla_p, new_gla_s, new_conv_p, new_conv_s)


_drawn_inputs = setup_inputs


def setup_inputs(seed=0):
    import zlib

    import numpy as np

    out = dict(_drawn_inputs(seed))
    spreads = {}
    factors = {'cache_cmp_kv': 3.149, 'w_cmp_k': 8.0, 'w_cmp_v': 8.0, 'cache_slc_kv': 4.013}
    for name, (base, spread) in spreads.items():
        noise = np.random.default_rng([zlib.crc32(name.encode()), seed]).standard_normal(out[name].shape)
        drawn = base * np.exp(spread * noise) if base else spread * noise
        out[name] = __import__('jax').numpy.asarray(drawn.astype(out[name].dtype))
    for name, factor in factors.items():
        out[name] = (out[name] * factor).astype(out[name].dtype)
    return out
```

```python
from contextlib import ExitStack

import numpy as np

import concourse.bass as bass
from concourse import mybir

ALU = mybir.AluOpType
ACT = mybir.ActivationFunctionType
F32 = mybir.dt.float32
F32R = mybir.dt.float32r
I32 = mybir.dt.int32
AX = mybir.AxisListType.X

P = 128
D = 1024
KD = D // P
SEQ = 1024
NT = SEQ // P
DB, DS = 8, 8
NS = DB * DS
TOK = SEQ + NS
HD = 64
NKV, NG = 2, 4
PAST, PAGE = 2048, 128
NPG = PAST // PAGE
CB = 64
NBLK = PAST // CB
WIN = 512
EPS = 1e-6
NEG = -1e30
SCALE = HD ** -0.5
GH, GK, GV, GR = 4, 32, 64, 16
TAU = 16.0
CW, CK = 256, 3

C_Q, C_CMP, C_SLC, C_WIN, C_GATE, C_Z = 0, 512, 768, 1024, 1280, 1304
C_GQ, C_GA, C_GZ = 1816, 2328, 2344
C_B, C_C, C_H, C_ZC = 2600, 2856, 3112, 3368
NRES = C_Z
WR = NRES // 4
WZ = (512 + 256) // 2
WG = (C_GZ - C_GQ) // 2
WMAX = max(WR, WZ, WG)
NGL = C_GZ - C_GQ
DVE_PER_KV = 111
DVE_PER_PAIRS = 72
CH3 = ((0, 364), (364, 362), (726, 362))


class Order:

    def __init__(self, eng, sem, base=0):
        self.eng, self.sem, self.base, self.it, self.per, self.n = eng, sem, base, None, 0, 0

    def loop(self, it, per, first=0):
        self.base, self.it, self.per, self.n = self.base + self.n - first * per, it, per, 0
        self.first = first

    def end_loop(self, iterations):
        assert self.n == self.per, f"this loop signals {self.n}, not {self.per}"
        self.base, self.it, self.n = self.base + (self.first + iterations) * self.per, None, 0

    def did(self, ins):
        self.n += 1
        ins.then_inc(self.sem, 1)

    def wait(self):
        at = self.base + self.n
        self.eng.wait_ge(self.sem, at if self.it is None else self.it * self.per + at)


def hybrid_step(nc, x_prompt, x_sample, cache_cmp_kv, cache_slc_kv, cache_win_kv, state_gla, state_conv,
                page_table, norm_pre, norm_post, w_in, w_out, w_cmp_k, w_cmp_v, gla_a2, gla_ab, gla_norm,
                conv_w, y_prompt, y_sample, new_cmp_p, new_cmp_s, new_slc_p, new_slc_s, new_win_p, new_win_s,
                new_gla_p, new_gla_s, new_conv_p, new_conv_s):
    z_dram = nc.dram_tensor("z_scratch", (TOK, 2, WZ), F32, kind="Internal").ap()
    gla_dram = nc.dram_tensor("gla_scratch", (TOK, 2, WG), F32, kind="Internal").ap()
    attn_dram = nc.dram_tensor("attn_scratch", (DB, NKV, NG, DS, HD), F32, kind="Internal").ap()
    gate_dram = nc.dram_tensor("gate_scratch", (NS, 3 * NKV * NG), F32, kind="Internal").ap()
    with ExitStack() as ctx:
        sem = lambda name: ctx.enter_context(nc.semaphore(name))
        sb = lambda name, shape, dt=F32: ctx.enter_context(nc.sbuf_tensor(name, shape, dt))
        ident = sb("ident", [P, P])
        pres = sb("pres", [P, NT + 1, NRES])
        cmix_hi = sb("cmix_hi", [P, 2, TOK], F32R)
        cmix_lo = sb("cmix_lo", [P, 2, TOK], F32R)
        ps = ctx.enter_context(nc.psum_tensor("ps", [P, 8, 512], F32))
        project(nc, sem, ident, pres, cmix_hi, cmix_lo, ps, z_dram, gla_dram, x_prompt, x_sample, norm_pre,
                w_in, conv_w, state_conv, cache_win_kv, new_win_s, new_conv_p, new_conv_s)
        o_nsa = sb("o_nsa", [P, NT + 1, 512])
        attend_prompt(nc, sem, ident, pres, o_nsa, ps, w_cmp_k, w_cmp_v, new_cmp_p, new_cmp_s, new_slc_p,
                      new_slc_s, new_win_p, new_win_s)
        attend_sample(nc, sem, ident, pres, o_nsa, ps, attn_dram, gate_dram, cache_cmp_kv, cache_slc_kv, cache_win_kv,
                      page_table, w_cmp_k, w_cmp_v)
        finish_rows(nc, sem, ident, pres, cmix_hi, cmix_lo, o_nsa, ps, z_dram, gla_dram, x_prompt, x_sample,
                    norm_post, w_out, gla_a2, gla_ab, gla_norm, state_gla, y_prompt, y_sample, new_gla_p,
                    new_gla_s)


def project(nc, sem, ident, pres, cmix_hi, cmix_lo, ps, z_dram, gla_dram, x_prompt, x_sample, norm_pre, w_in,
            conv_w, state_conv, cache_win_kv, new_win_s, new_conv_p, new_conv_s):
    with ExitStack() as ctx:
        sb = lambda name, shape, dt=F32: ctx.enter_context(nc.sbuf_tensor(name, shape, dt))
        h_hi = sb("h_hi", [P, KD, TOK], F32R)
        h_lo = sb("h_lo", [P, KD, TOK], F32R)
        w_raw = sb("w_raw", [P, KD * WMAX])
        w_hi = sb("w_hi", [P, 2, KD * WMAX], F32R)
        w_lo = sb("w_lo", [P, 2, KD * WMAX], F32R)
        stage = sb("stage", [P, 3, WZ])
        g_col = sb("g_col", [P, KD])
        stat = sb("stat", [P, 4])
        eps = sb("eps", [P, 1])
        start = sb("start", [P, 1])
        cw = sb("cw", [P, 2, CK])
        cstate = sb("cstate", [P, 2, DB, 2])
        cnew_p = sb("cnew_p", [P, 2, 2])
        cnew_s = sb("cnew_s", [P, 2, DB, 2])
        flat = pres[:, :, :].rearrange("p a b -> p (a b)")
        at = [0]

        def part(n):
            at[0] += n
            return flat[:, at[0] - n:at[0]]

        xt = [part(D), part(D)]
        xn = part(D)
        xg = [part(512), part(512)]
        b_t, c_t, h_t, z_t, y_t = part(TOK), part(TOK), part(TOK), part(TOK), part(TOK)
        u_p = part(2 + SEQ)
        u_s = part(DB * (2 + DS)).rearrange("p (b t) -> p b t", b=DB)
        assert at[0] <= (NT + 1) * NRES

        s_small = sem("small_loaded")
        s_x = [sem("x_loaded_0"), sem("x_loaded_1")]
        s_w = sem("w_loaded")
        s_st = [sem(f"stage_stored_{i}") for i in range(3)]
        s_ident = sem("ident_ready")
        s_split = sem("w_split")
        s_rt = sem("row_rms_ready")
        s_xn = sem("x_normed")
        s_xT = sem("x_transposed")
        s_xg = sem("x_scaled")
        s_hi = sem("h_hi_ready")
        s_lo = sem("h_lo_ready")
        s_pj = sem("projected")
        s_ev = sem("projection_copied")
        s_conv = sem("conv_done")
        a_done, v_done, g_done = sem("act_done_a"), sem("dve_done_a"), sem("pool_done_a")
        s_out = sem("copied_out_a")

        def w_cols(c, n):
            return w_in[0, :, bass.ds(c, n)].rearrange("(k p) c -> p k c", p=P)

        def raw(w, a=0, n=None):
            v = w_raw[:, 0:KD * w].rearrange("p (k c) -> p k c", k=KD)
            return v[:, :, a:a + (n or w)]

        with nc.Block() as block:

            @block.sync
            def _(sp):
                sp.dma_start(g_col[:, :], norm_pre[0].rearrange("(k p) -> p k", p=P)).then_inc(s_small, 16)
                sp.dma_start(xt[0], x_prompt[0, 0:P, :]).then_inc(s_x[0], 16)
                sp.dma_start(xt[1], x_prompt[0, P:2 * P, :]).then_inc(s_x[1], 16)
                sp.dma_start(raw(P), w_cols(C_C, P)).then_inc(s_w, 16)
                for h in range(2):
                    sp.dma_start(cw[:, h, :], conv_w[0, :, h * P:(h + 1) * P].rearrange("j p -> p j")
                                 ).then_inc(s_small, 16)
                    sp.dma_start(cstate[:, h, :, :], state_conv[0, :, :, h * P:(h + 1) * P].rearrange(
                        "b r p -> p b r")).then_inc(s_small, 16)
                with sp.Fori(0, 3) as i:
                    for s in range(2):
                        sp.wait_ge(s_xn, 2 * i + s + 1)
                        sp.dma_start(xt[s], x_prompt[0, bass.ds((2 * i + s + 2) * P, P), :]).then_inc(s_x[s], 16)
                sp.wait_ge(s_xn, 7)
                sp.dma_start(xt[0][0:NS, :], x_sample.rearrange("b t d -> (b t) d")).then_inc(s_x[0], 16)
                sp.dma_start(new_win_s[0, :, 0:WIN - DS].rearrange("b w c h d -> b (w c h d)"),
                             cache_win_kv[0, :, DS:WIN].rearrange("b w c h d -> b (w c h d)")).then_inc(s_out, 16)

                for n, c in enumerate((C_H, C_B, C_ZC, C_C + P, C_H + P, C_B + P, C_ZC + P)):
                    sp.wait_ge(s_split, n + 1)
                    sp.dma_start(raw(P), w_cols(c, P)).then_inc(s_w, 16)
                with sp.Fori(0, 4) as i:
                    sp.wait_ge(s_split, 8 + i)
                    sp.dma_start(raw(WR), w_cols(i * WR, WR)).then_inc(s_w, 16)
                for j in range(2):
                    sp.wait_ge(s_split, 12 + 2 * j)
                    sp.dma_start(raw(WZ, 0, 256), w_cols(C_Z + 256 * j, 256)).then_inc(s_w, 16)
                    sp.dma_start(raw(WZ, 256, 128), w_cols(C_GZ + 128 * j, 128)).then_inc(s_w, 16)
                    sp.wait_ge(s_split, 13 + 2 * j)
                    sp.dma_start(raw(WG), w_cols(C_GQ + WG * j, WG)).then_inc(s_w, 16)
                sp.wait_ge(s_conv, 3)
                for h in range(2):
                    sp.dma_start(new_conv_p[0, 0, :, h * P:(h + 1) * P].rearrange("r p -> p r"),
                                 cnew_p[:, h, :]).then_inc(s_out, 16)
                    sp.dma_start(new_conv_s[0, :, :, h * P:(h + 1) * P].rearrange("b r p -> p b r"),
                                 cnew_s[:, h, :, :]).then_inc(s_out, 16)
                sp.wait_ge(s_out, 80)

            @block.gpsimd
            def _(pool):
                g = Order(pool, g_done)
                g.did(nc.gpsimd.memset(ident[:, :], 0.0))
                g.wait()
                nc.gpsimd.affine_select(out=ident[:, :], in_=ident[:, :], compare_op=ALU.not_equal, fill=1.0,
                                        base=0, pattern=[[-1, P]], channel_multiplier=1).then_inc(s_ident, 1)

                def split(slot, w):
                    n = KD * w
                    g.did(nc.gpsimd.tensor_copy(w_hi[:, slot, 0:n], w_raw[:, 0:n]))
                    g.wait()
                    nc.gpsimd.tensor_tensor(w_lo[:, slot, 0:n], w_raw[:, 0:n],
                                            w_hi[:, slot, 0:n].bitcast(F32), ALU.subtract).then_inc(s_split, 1)

                for n in range(8):
                    pool.wait_ge(s_w, 16 * (n + 1))
                    if n >= 2:
                        pool.wait_ge(s_pj, 3 * (n - 1))
                    split(n % 2, P)
                for c in range(8):
                    w = WR if c < 4 else (WZ, WG)[c % 2]
                    pool.wait_ge(s_w, 16 * (9 + c) if c < 4 else (224, 240, 272, 288)[c - 4])
                    pool.wait_ge(s_pj, 21 + 3 * c if c < 2 else 24 + 9 * (c - 1))
                    split(c % 2, w)

            @block.scalar
            def _(act):
                a = Order(act, a_done)

                def norm(i, s, rows):
                    act.wait_ge(s_x[s], 16 * (i + 1))
                    a.did(nc.scalar.activation(ps[0:rows, 0:2, :].rearrange("p a b -> p (a b)"), xt[s][0:rows, :],
                                               ACT.Square, accum_out=stat[0:rows, s:s + 1]))
                    a.wait()
                    nc.scalar.activation(stat[0:rows, 2 + s:3 + s], stat[0:rows, s:s + 1], ACT.Sqrt,
                                         scale=1.0 / D, bias=eps[0:rows, :]).then_inc(s_rt, 1)

                def halves(t, s, rows, col):
                    for f in range(2):
                        act.wait_ge(s_xg, t * 2 + f + 1)
                        nc.scalar.activation(
                            h_hi[:, 4 * f:4 * f + 4, bass.ds(col, rows)],
                            xg[f][:, 0:4 * rows].rearrange("p (k c) -> p k c", k=4), ACT.Copy).then_inc(s_hi, 1)

                act.wait_ge(s_ident, 2)
                with act.Fori(0, 4) as i:
                    a.loop(i, 2)
                    for s in range(2):
                        norm(i, s, P)
                        halves(2 * i + s, s, P, (2 * i + s) * P)
                a.end_loop(4)
                norm(4, 0, NS)
                halves(8, 0, NS, SEQ)
                nc.scalar.activation(start[:, 0:1], eps[:, :], ACT.Copy).then_inc(s_ev, 1)
                with act.Fori(0, 2) as h:
                    for m, (dst, fn) in enumerate(((c_t, ACT.Copy), (h_t, ACT.Copy), (b_t, ACT.Copy),
                                                   (z_t, ACT.Silu))):
                        for c, (t0, tn) in enumerate(CH3):
                            act.wait_ge(s_pj, 12 * h + 3 * m + c + 1)
                            if m == 0 and c == 0:
                                act.wait_ge(s_conv, h + 1)
                            nc.scalar.activation(dst[:, t0:t0 + tn], ps[:, (3 * m + c) % 6, 0:tn],
                                                 fn).then_inc(s_ev, 1)
                act.wait_ge(s_conv, 3)
                with act.Fori(0, 2) as i:
                    for s in range(2):
                        for t in range(NT + 1):
                            rows = P if t < NT else NS
                            n = 9 * s + t
                            act.wait_ge(s_pj, 18 * i + 25 + n)
                            nc.scalar.activation(pres[0:rows, t, bass.ds((2 * i + s) * WR, WR)],
                                                 ps[0:rows, n % 6, 0:WR], ACT.Copy).then_inc(s_ev, 1)
                for j in range(2):
                    for s in range(2):
                        w = (WZ, WG)[s]
                        for t in range(NT + 1):
                            rows = P if t < NT else NS
                            n = 9 * s + t
                            use = 6 * j + n // 3
                            act.wait_ge(s_pj, 61 + 18 * j + n)
                            if use > 0:
                                act.wait_ge(s_st[n % 3], 16 * use)
                            nc.scalar.activation(stage[0:rows, n % 3, 0:w], ps[0:rows, n % 6, 0:w],
                                                 (ACT.Silu, ACT.Copy)[s]).then_inc(s_ev, 1)
                            act.wait_ge(s_ev, 62 + 18 * j + n)
                            dst = (z_dram, gla_dram)[s]
                            act.dma_start(dst[t * P:t * P + rows, j, :], stage[0:rows, n % 3, 0:w]
                                          ).then_inc(s_st[n % 3], 16)
                for q in s_st:
                    act.wait_ge(q, 16 * 12)

            @block.vector
            def _(dve):
                v = Order(dve, v_done)

                def tile(t, s, rows, col):
                    dve.wait_ge(s_rt, t + 1)
                    v.did(nc.vector.reciprocal(stat[0:rows, s:s + 1], stat[0:rows, 2 + s:3 + s]))
                    v.wait()
                    nc.vector.tensor_scalar(xn[0:rows, :], xt[s][0:rows, :], stat[0:rows, s:s + 1], None,
                                            ALU.mult).then_inc(s_xn, 1)
                    for f in range(2):
                        dve.wait_ge(s_xT, 2 * t + f + 1)
                        nc.vector.tensor_tensor(
                            xg[f][:, 0:4 * rows].rearrange("p (k c) -> p k c", k=4),
                            ps[:, 6 + f, 0:4 * rows].rearrange("p (k c) -> p k c", k=4),
                            g_col[:, 4 * f:4 * f + 4].unsqueeze(2).to_broadcast([P, 4, rows]),
                            ALU.mult).then_inc(s_xg, 1)
                    for f in range(2):
                        dve.wait_ge(s_hi, 2 * t + f + 1)
                        nc.vector.tensor_tensor(
                            h_lo[:, 4 * f:4 * f + 4, bass.ds(col, rows)],
                            xg[f][:, 0:4 * rows].rearrange("p (k c) -> p k c", k=4),
                            h_hi[:, 4 * f:4 * f + 4, bass.ds(col, rows)].bitcast(F32),
                            ALU.subtract).then_inc(s_lo, 1)

                nc.vector.memset(eps[:, :], EPS).then_inc(s_ident, 1)
                dve.wait_ge(s_small, 80)
                with dve.Fori(0, 4) as i:
                    v.loop(i, 2)
                    for s in range(2):
                        tile(2 * i + s, s, P, (2 * i + s) * P)
                v.end_loop(4)
                tile(8, 0, NS, SEQ)
                nc.vector.memset(u_p[:, 0:2], 0.0).then_inc(s_conv, 1)
                dve.wait_ge(s_conv, 1)
                with dve.Fori(0, 2) as h:
                    v.loop(h, 12)
                    dve.wait_ge(s_ev, 12 * h + 13)
                    one = lambda w: w[:, bass.ds(h, 1)]
                    v.did(nc.vector.tensor_tensor(u_p[:, 2:2 + SEQ], c_t[:, 0:SEQ], h_t[:, 0:SEQ], ALU.mult))
                    v.did(nc.vector.tensor_tensor(
                        u_s[:, :, 2:2 + DS], c_t[:, SEQ:TOK].rearrange("p (b t) -> p b t", b=DB),
                        h_t[:, SEQ:TOK].rearrange("p (b t) -> p b t", b=DB), ALU.mult))
                    v.did(nc.vector.tensor_copy(u_s[:, :, 0:2],
                                                one(cstate).rearrange("p h b r -> p (h b) r")))
                    v.wait()
                    y_s = y_t[:, SEQ:TOK].rearrange("p (b t) -> p b t", b=DB)
                    for j in range(CK):
                        wj = cw[:, bass.ds(h, 1), j]
                        if j == 0:
                            v.did(nc.vector.tensor_scalar(y_t[:, 0:SEQ], u_p[:, 0:SEQ], wj, None, ALU.mult))
                            v.did(nc.vector.tensor_scalar(y_s, u_s[:, :, 0:DS], wj, None, ALU.mult))
                        else:
                            v.did(nc.vector.scalar_tensor_tensor(y_t[:, 0:SEQ], u_p[:, j:j + SEQ], wj,
                                                                 y_t[:, 0:SEQ], ALU.mult, ALU.add))
                            v.did(nc.vector.scalar_tensor_tensor(y_s, u_s[:, :, j:j + DS], wj, y_s,
                                                                 ALU.mult, ALU.add))
                        v.wait()
                    nc.vector.tensor_copy(one(cnew_p), u_p[:, SEQ:SEQ + 2].unsqueeze(1))
                    nc.vector.tensor_copy(one(cnew_s), u_s[:, :, DS:DS + 2].unsqueeze(1))
                    v.did(nc.vector.tensor_tensor(y_t, y_t, b_t, ALU.mult))
                    v.wait()
                    v.did(nc.vector.tensor_tensor(y_t, y_t, z_t, ALU.mult))
                    v.wait()
                    v.did(nc.vector.tensor_copy(one(cmix_hi), y_t.unsqueeze(1)))
                    v.wait()
                    nc.vector.tensor_tensor(one(cmix_lo), y_t.unsqueeze(1), one(cmix_hi).bitcast(F32),
                                            ALU.subtract).then_inc(s_conv, 1)
                v.end_loop(2)

            @block.tensor
            def _(pe):
                def transposes(t, rows):
                    pe.wait_ge(s_xn, t + 1)
                    for f in range(2):
                        if not isinstance(t, int) or t > 0:
                            pe.wait_ge(s_xg, 2 * t + f - 1)
                        for k in range(4):
                            mm = nc.tensor.transpose(ps[:, 6 + f, k * rows:(k + 1) * rows],
                                                     xn[0:rows, (4 * f + k) * P:(4 * f + k + 1) * P],
                                                     ident[0:rows, 0:rows])
                        mm.then_inc(s_xT, 1)

                pe.wait_ge(s_ident, 2)
                transposes(0, P)
                with pe.Fori(1, NT) as t:
                    transposes(t, P)
                transposes(8, NS)
                pe.wait_ge(s_hi, 18)
                pe.wait_ge(s_lo, 18)

                def wv(buf, slot, w):
                    return buf[:, slot, 0:KD * w].rearrange("p (k c) -> p k c", k=KD)

                def product(out, slot, w, stationary_w, tok):
                    n, mm = 0, None
                    t0, tn = tok
                    for k in range(KD):
                        for ww, hh in ((w_hi, h_hi), (w_hi, h_lo), (w_lo, h_hi)) if stationary_w else (
                                (w_hi, h_hi), (w_lo, h_hi), (w_hi, h_lo)):
                            wk, hk = wv(ww, slot, w)[:, k, :], hh[:, k, t0:t0 + tn]
                            lhs, rhs = (wk, hk) if stationary_w else (hk, wk)
                            mm = nc.tensor.matmul(out, lhs, rhs, start=(n == 0), stop=(n == 3 * KD - 1))
                            n += 1
                    mm.then_inc(s_pj, 1)

                with pe.Fori(0, 2) as h:
                    for m in range(4):
                        pe.wait_ge(s_split, 4 * h + m + 1)
                        for c, tok in enumerate(CH3):
                            n = 3 * m + c
                            pe.wait_ge(s_ev, 12 * h + max(n - 5, 0) + 1)
                            product(ps[:, n % 6, 0:tok[1]], m % 2, P, True, tok)
                with pe.Fori(0, 2) as i:
                    for s in range(2):
                        pe.wait_ge(s_split, 2 * i + s + 9)
                        for t in range(NT + 1):
                            rows = P if t < NT else NS
                            n = 9 * s + t
                            pe.wait_ge(s_ev, 18 * i + n + 20)
                            product(ps[0:rows, n % 6, 0:WR], s, WR, False, (t * P, rows))
                with pe.Fori(0, 2) as j:
                    for s in range(2):
                        pe.wait_ge(s_split, 2 * j + s + 13)
                        w = (WZ, WG)[s]
                        for t in range(NT + 1):
                            rows = P if t < NT else NS
                            n = 9 * s + t
                            pe.wait_ge(s_ev, 18 * j + n + 56)
                            product(ps[0:rows, n % 6, 0:w], s, w, False, (t * P, rows))


def attend_prompt(nc, sem, ident, pres, o_nsa, ps, w_cmp_k, w_cmp_v, new_cmp_p, new_cmp_s, new_slc_p,
                  new_slc_s, new_win_p, new_win_s):
    NB = SEQ // CB
    BR = ((C_SLC, 1), (C_WIN, 2))

    def span(u):
        i, br = u // 2, u % 2
        return (0 if br == 0 else max(0, i - WIN // P)), i

    HIDDEN = 2.0 ** 100
    UNITS = 2 * NT
    LAG, PTS = 2, 3
    BEHIND, PRS = 1, 3
    tiles_of = [span(u)[1] - span(u)[0] + 1 for u in range(UNITS)]
    first_tile = [sum(tiles_of[:u]) for u in range(UNITS + 1)]
    TILES = first_tile[UNITS]
    HEADS = NG * UNITS

    def schedule():
        turned, summed = [], []

        def sums(keep):
            while len(turned) > keep:
                x, t = turned.pop(0)
                yield "sum", x, t
                while summed:
                    yield "output", summed.pop(0), 0
                if t == tiles_of[x] - 1:
                    summed.append(x)

        ahead = ("query", "c_scores", "c_exp", "c_turn", "c_values")
        for what in ahead:
            yield what, 0, 0
        for h in range(HEADS + NG + BEHIND):
            u, y = h // NG, h % NG
            if u < UNITS:
                yield "scores", u, y
            x, g = (h - BEHIND) // NG - 1, (h - BEHIND) % NG
            n = tiles_of[x] if 0 <= x < UNITS else 0
            t0, t1 = -(-n * g // NG), -(-n * (g + 1) // NG)
            for t in range(t0, t1):
                yield "turn", x, t
                if u < UNITS and t == t0:
                    yield "least", u, y
                turned.append((x, t))
                yield from sums(LAG)
            if u < UNITS:
                if t0 == t1:
                    yield "least", u, y
                yield "exp", u, y
                i = (u + 1) // 2
                if u % 2 == 1 and i < NT:
                    yield ahead[y], i, 0
                elif u % 2 == 0 and y == 2 and u > 0:
                    yield ahead[NG], u // 2, 0
        yield from sums(0)
        yield "output", summed.pop(0), 0

    steps = list(schedule())
    for i in range(2, NT):
        assert steps.index(("c_values", i, 0)) > steps.index(("output", 2 * i - 3, 0))
    uses = [(k, x) for what, x, _ in steps
            for k in {"query": ("q",), "c_scores": ("cs",), "c_turn": ("ct",), "c_values": ("co",), "output": ("z",)}.get(what, ())]
    USES = len(uses)
    place = {x: n for n, x in enumerate(uses)}

    with ExitStack() as ctx:
        sb = lambda name, shape, dt=F32: ctx.enter_context(nc.sbuf_tensor(name, shape, dt))
        q_st = sb("q_st", [P, NT, NG, 2, HD])
        k_st = sb("k_st", [P, 3, NT, 2, HD])
        g_st = sb("g_st", [P, NT, NG, 3])
        kT = sb("kT", [P, 2, SEQ], F32R)
        vs = sb("vs", [P, 2, NT, 2, HD], F32R)
        kcT = sb("kcT", [P, NB], F32R)
        vc = sb("vc", [P, NG, HD])
        q_hi = sb("q_hi", [P, 2, NG * P], F32R)
        q_lo = sb("q_lo", [P, 2, NG * P], F32R)
        prob = sb("prob", [P, PRS, NG, SEQ])
        pt_hi = sb("pt_hi", [P, PTS, NG * P], F32R)
        pt_lo = sb("pt_lo", [P, PTS, NG * P], F32R)
        oT = sb("oT", [P, NG * P])
        scaled = sb("scaled", [P, NG, HD])
        o_acc = sb("o_acc", [P, 2, NG, HD])
        gate = sb("gate", [P, NT + 1, 3 * NKV * NG])
        least = sb("least", [P, HEADS])
        rowsum = sb("rowsum", [P, HEADS])
        factor = sb("factor", [P, 2, NG])
        ident2 = sb("ident2", [P, HD])
        pen = sb("pen", [P, 2, P])
        pen_r = sb("pen_r", [P, 2, P], F32R)
        ident_r = sb("ident_r", [P, P], F32R)
        c_mask = sb("c_mask", [P, NT, NB])
        c_pen = sb("c_pen", [P, NT, NB])
        c_s = sb("c_s", [P, NG, NB])
        c_e = sb("c_e", [P, NG, NB])
        c_p = sb("c_p", [P, NG, 32])
        c_pT = sb("c_pT", [P, P])
        c_stat = sb("c_stat", [P, 3, NG])
        wk2 = sb("wk2", [P, 2])
        wv2 = sb("wv2", [P, 2])
        wv4 = sb("wv4", [P, NB - 2 + NG * 32])

        s_stored = sem("rows_stored")
        s_w2z, s_w2, s_const = sem("w2_zeroed"), sem("w2_loaded"), sem("consts_b")
        s_gate = sem("gates_ready")
        s_stg = sem("kv_staged")
        s_kt, s_khi, s_klo = sem("k_transposed"), sem("k_hi"), sem("k_lo")
        s_vhi, s_vlo = sem("v_hi"), sem("v_lo")
        s_sp = sem("spare_written")
        s_spr = sem("spare_read")
        s_qhi = sem("q_hi_ready")
        s_cs, s_ce, s_cp = sem("c_scores"), sem("c_exp"), sem("c_probs")
        s_qk, s_mx, s_exp = sem("scores"), sem("maxed"), sem("exped")
        s_pt, s_pth, s_ptl, s_pv = sem("p_transposed"), sem("pt_hi"), sem("pt_lo"), sem("pv_done")
        s_ot, s_otc = sem("out_summed"), sem("out_copied")
        v_done, g_done = sem("dve_done_b"), sem("pool_done_b")

        def S(g, n):
            return ps[:, 2 * (g % 2):2 * (g % 2) + 2, :].rearrange("p a b -> p (a b)")[:, 0:n]

        with nc.Block() as block:

            @block.sync
            def _(sp):
                for dst_p, dst_s, c in ((new_cmp_p, new_cmp_s, C_CMP), (new_slc_p, new_slc_s, C_SLC)):
                    sp.dma_start(dst_p[0, 0].rearrange("(t p) c h d -> p t (c h d)", p=P),
                                 pres[:, 0:NT, c:c + 256]).then_inc(s_stored, 16)
                    sp.dma_start(dst_s[0].rearrange("b t c h d -> (b t) (c h d)"),
                                 pres[0:NS, NT, c:c + 256]).then_inc(s_stored, 16)
                sp.dma_start(new_win_p[0, 0].rearrange("(t p) c h d -> p t (c h d)", p=P),
                             pres[:, NT // 2:NT, C_WIN:C_WIN + 256]).then_inc(s_stored, 16)
                for b in range(DB):
                    sp.dma_start(new_win_s[0, b, WIN - DS:WIN].rearrange("t c h d -> t (c h d)"),
                                 pres[b * DS:(b + 1) * DS, NT, C_WIN:C_WIN + 256]).then_inc(s_stored, 16)
                sp.wait_ge(s_w2z, 2)
                for w, dst in ((w_cmp_k, wk2), (w_cmp_v, wv2)):
                    for b in range(2):
                        sp.dma_start(dst[b * CB:(b + 1) * CB, b:b + 1],
                                     w[0].rearrange("(l o) -> l o", o=1)).then_inc(s_w2, 16)
                sp.wait_ge(s_stored, 16 * 13)

            @block.gpsimd
            def _(pool):
                g = Order(pool, g_done)
                nc.gpsimd.memset(wk2[:, :], 0.0).then_inc(s_w2z, 1)
                nc.gpsimd.memset(wv2[:, :], 0.0).then_inc(s_w2z, 1)
                for m, x in ((pen, 0.0), (c_pen, 0.0), (c_mask, 1.0), (wv4, 0.0), (vc, 0.0),
                             (c_p, 0.0)):
                    g.did(nc.gpsimd.memset(m[:], x))
                g.wait()
                g.did(nc.gpsimd.affine_select(out=pen[:, 0, :], in_=pen[:, 0, :], compare_op=ALU.is_ge,
                                              fill=HIDDEN, base=0, pattern=[[-1, P]], channel_multiplier=1))
                g.did(nc.gpsimd.affine_select(out=pen[:, 1, :], in_=pen[:, 1, :], compare_op=ALU.is_gt,
                                              fill=HIDDEN, base=0, pattern=[[1, P]], channel_multiplier=-1))
                g.wait()
                g.did(nc.gpsimd.tensor_copy(pen_r[:, :, :], pen[:, :, :]))
                g.did(nc.gpsimd.tensor_copy(ident_r[:, :], ident[:, :]))
                g.did(nc.gpsimd.tensor_tensor(ident2[:, :], ident[:, 0:HD], ident[:, HD:P], ALU.add))
                for m, x in ((c_pen, -NEG), (c_mask, 0.0)):
                    g.did(nc.gpsimd.affine_select(out=m[:, :, :], in_=m[:, :, :], compare_op=ALU.is_ge, fill=x,
                                                  base=-(CB - 1), pattern=[[P, NT], [-CB, NB]],
                                                  channel_multiplier=1))
                pool.wait_ge(s_w2, 64)
                for h in range(NG):
                    g.did(nc.gpsimd.tensor_copy(wv4[:, NB - 2 + 32 * h:NB + 32 * h], wv2[:, :]))
                g.wait()
                nc.gpsimd.memset(c_stat[:], 0.0).then_inc(s_const, 1)

            @block.tensor
            def _(pe):
                pe.wait_ge(s_const, 1)
                with pe.Fori(0, NKV) as kv:
                    K = lambda n, per: kv * per + n

                    def spare(x):
                        if place[x] > 0:
                            pe.wait_ge(s_spr, K(place[x], USES))
                        return ps[:, 7, :]

                    pe.wait_ge(s_stg, kv + 1)
                    for b in range(4):
                        if b >= 2:
                            pe.wait_ge(s_klo, K(b - 1, 6))
                        for t in range(4):
                            mm = nc.tensor.transpose(
                                ps[:, 4 + b % 2, t * P:(t + 1) * P],
                                k_st[:, b // 2, 4 * (b % 2) + t, :, :].rearrange("p a d -> p (a d)"),
                                ident[:, :])
                        mm.then_inc(s_kt, 1)
                    pe.wait_ge(s_klo, K(3, 6))
                    for j in range(NT):
                        mm = nc.tensor.matmul(ps[:, 4, 2 * j:2 * j + 2],
                                              k_st[:, 2, j, :, :].rearrange("p a d -> p (a d)"), wk2[:, :],
                                              start=True, stop=True)
                    mm.then_inc(s_kt, 1)
                    pe.wait_ge(s_klo, K(4, 6))
                    for j in range(NT):
                        mm = nc.tensor.matmul(ps[:, 5, 0:HD], wv4[:, NB - 2 - 2 * j:NB - 2 - 2 * j + NG * 32],
                                              pres[:, j, bass.ds(kv * HD + C_CMP + P, HD)],
                                              start=(j == 0), stop=(j == NT - 1))
                    mm.then_inc(s_kt, 1)
                    pe.wait_ge(s_klo, K(6, 6))
                    pe.wait_ge(s_vlo, K(2, 2))
                    for what, x, y in steps:
                        if what == "query":
                            out = spare(("q", x))
                            for g in range(NG):
                                mm = nc.tensor.transpose(
                                    out[:, g * P:(g + 1) * P],
                                    q_st[:, x, g, :, :].rearrange("p a d -> p (a d)"), ident[:, :])
                            mm.then_inc(s_sp, 1)
                        elif what == "c_scores":
                            out = spare(("cs", x))
                            for g in range(NG):
                                for q in (q_hi, q_lo):
                                    mm = nc.tensor.matmul(out[:, g * NB:(g + 1) * NB],
                                                          q[:, x % 2, g * P:(g + 1) * P], kcT[:, :],
                                                          start=(q is q_hi), stop=(q is q_lo))
                            mm.then_inc(s_sp, 1)
                        elif what == "scores":
                            i, br = x // 2, x % 2
                            j0, j1 = span(x)
                            h = NG * x + y
                            if h >= 2:
                                pe.wait_ge(s_exp, K(h - 1, HEADS))
                            for c in range(j0, j1 + 1, 4):
                                n = min(4, j1 + 1 - c) * P
                                bank = 2 * (y % 2) + (c - j0) // 4
                                edges = []
                                if c + n // P > j1:
                                    edges.append((n - P, 0))
                                if c == j0 and br == 1 and i >= WIN // P:
                                    edges.append((0, 1))
                                for q in (q_hi, q_lo):
                                    mm = nc.tensor.matmul(ps[:, bank, 0:n], q[:, i % 2, y * P:(y + 1) * P],
                                                          kT[:, br, c * P:c * P + n],
                                                          start=(q is q_hi), stop=(q is q_lo and not edges))
                                for at, edge in edges:
                                    mm = nc.tensor.matmul(ps[:, bank, at:at + P], ident_r[:, :],
                                                          pen_r[:, edge, :], start=False,
                                                          stop=((at, edge) == edges[-1]))
                            mm.then_inc(s_qk, 1)
                        elif what == "turn":
                            t = first_tile[x] + y
                            if y == 0:
                                pe.wait_ge(s_exp, K(NG * (x + 1), HEADS))
                            if t >= 2:
                                pe.wait_ge(s_ptl, K(t - 1, TILES))
                            for g in range(NG):
                                mm = nc.tensor.transpose(ps[:, 4 + t % 2, g * P:(g + 1) * P],
                                                         prob[:, x % PRS, g, y * P:(y + 1) * P], ident[:, :])
                            mm.then_inc(s_pt, 1)
                        elif what == "sum":
                            t = first_tile[x] + y
                            if y == 0 and x > 0:
                                pe.wait_ge(s_otc, K(x, UNITS))
                            for s, buf in ((s_pth, pt_hi), (s_ptl, pt_lo)):
                                pe.wait_ge(s, K(t + 1, TILES))
                                mm = nc.tensor.matmul(
                                    ps[:, 6, :],
                                    vs[:, x % 2, span(x)[0] + y, :, :].rearrange("p a d -> p (a d)"),
                                    buf[:, t % PTS, :], start=(y == 0 and buf is pt_hi),
                                    stop=(y == tiles_of[x] - 1 and buf is pt_lo))
                            mm.then_inc(s_pv, 1)
                        elif what == "output":
                            out = spare(("z", x))
                            pe.wait_ge(s_otc, K(x + 1, UNITS))
                            for g in range(NG):
                                mm = nc.tensor.matmul(out[:, g * HD:(g + 1) * HD], oT[:, g * P:(g + 1) * P],
                                                      ident2[:, :], start=True, stop=True)
                            mm.then_inc(s_sp, 1)
                        elif what == "c_turn":
                            out = spare(("ct", x))
                            pe.wait_ge(s_cp, K(x + 1, NT))
                            nc.tensor.transpose(out[:, 0:P], c_p[:, :, :].rearrange("p g n -> p (g n)"),
                                                ident[:, :]).then_inc(s_sp, 1)
                        elif what == "c_values":
                            out = spare(("co", x))
                            nc.tensor.matmul(out[:, 0:NG * HD], c_pT[:, :],
                                             vc[:, :, :].rearrange("p g d -> p (g d)"),
                                             start=True, stop=True).then_inc(s_sp, 1)

            @block.scalar
            def _(act):
                nc.scalar.activation(gate[:, 0:NT, :], pres[:, 0:NT, C_GATE:C_Z], ACT.Sigmoid)
                nc.scalar.activation(gate[0:NS, NT, :], pres[0:NS, NT, C_GATE:C_Z], ACT.Sigmoid
                                     ).then_inc(s_gate, 1)
                with act.Fori(0, NKV) as kv:
                    K = lambda n, per: kv * per + n
                    act.wait_ge(s_stg, kv + 1)
                    for br, (c, _) in enumerate(BR):
                        nc.scalar.activation(vs[:, br, :, 0, :], pres[:, 0:NT, bass.ds(kv * HD + c + P, HD)],
                                             ACT.Copy).then_inc(s_vhi, 1)
                    for b in range(5):
                        act.wait_ge(s_kt, K(b + 1, 6))
                        dst = kT[:, b // 2, 512 * (b % 2):512 * (b % 2) + 512] if b < 4 else kcT[:, :]
                        nc.scalar.activation(dst, ps[:, 4 + b % 2, 0:512 if b < 4 else NB],
                                             ACT.Copy).then_inc(s_khi, 1)
                    for what, x, y in steps:
                        if what == "query":
                            act.wait_ge(s_sp, K(place["q", x] + 1, USES))
                            nc.scalar.activation(q_hi[:, x % 2, :], ps[:, 7, :], ACT.Copy).then_inc(s_qhi, 1)
                        elif what == "c_exp":
                            act.wait_ge(s_cs, K(x + 1, NT))
                            nc.scalar.activation(c_e[:, :, :], c_s[:, :, :], ACT.Exp, scale=-1.0
                                                 ).then_inc(s_ce, 1)
                        elif what == "exp":
                            h = NG * x + y
                            n = tiles_of[x] * P
                            act.wait_ge(s_mx, K(h + 1, HEADS))
                            nc.scalar.activation(prob[:, x % PRS, y, 0:n], S(y, n), ACT.Exp, scale=-1.0,
                                                 bias=least[:, h:h + 1],
                                                 accum_out=rowsum[:, h:h + 1]).then_inc(s_exp, 1)
                        elif what == "turn":
                            t = first_tile[x] + y
                            act.wait_ge(s_pt, K(t + 1, TILES))
                            if t >= PTS:
                                act.wait_ge(s_pv, K(t - PTS + 1, TILES))
                            nc.scalar.activation(pt_hi[:, t % PTS, :], ps[:, 4 + t % 2, :],
                                                 ACT.Copy).then_inc(s_pth, 1)
                        elif what == "sum":
                            t = first_tile[x] + y
                            if y == tiles_of[x] - 1:
                                act.wait_ge(s_pv, K(t + 1, TILES))
                                if x > 0:
                                    act.wait_ge(s_sp, K(place["z", x - 1] + 1, USES))
                                nc.scalar.activation(oT[:, :], ps[:, 6, :], ACT.Copy).then_inc(s_otc, 1)

            @block.vector
            def _(dve):
                v = Order(dve, v_done)
                dve.wait_ge(s_gate, 1)
                dve.wait_ge(s_const, 1)
                with dve.Fori(0, NKV) as kv:
                    K = lambda n, per: kv * per + n
                    v.loop(kv, DVE_PER_KV)
                    for a in range(2):
                        for g in range(NG):
                            v.did(nc.vector.tensor_scalar(
                                q_st[:, :, g, a, :], pres[:, 0:NT, bass.ds(kv * NG * HD + g * HD, HD)], -SCALE,
                                None, ALU.mult))
                        for n, c in enumerate((C_SLC, C_WIN, C_CMP)):
                            v.did(nc.vector.tensor_copy(k_st[:, n, :, a, :],
                                                        pres[:, 0:NT, bass.ds(kv * HD + c, HD)]))
                    v.did(nc.vector.tensor_copy(g_st[:, :, :, :].rearrange("p i g c -> p i (g c)"),
                                                gate[:, 0:NT, bass.ds(kv * NG * 3, NG * 3)]))
                    v.wait()
                    nc.vector.memset(factor[:, 0, :], 0.0).then_inc(s_stg, 1)
                    for br, (c, _) in enumerate(BR):
                        dve.wait_ge(s_vhi, K(br + 1, 2))
                        nc.vector.tensor_tensor(vs[:, br, :, 1, :], pres[:, 0:NT, bass.ds(kv * HD + c + P, HD)],
                                                vs[:, br, :, 0, :].bitcast(F32), ALU.subtract).then_inc(s_vlo, 1)
                    for b in range(5):
                        dve.wait_ge(s_khi, K(b + 1, 5))
                        dst = kT[HD:P, b // 2, 512 * (b % 2):512 * (b % 2) + 512] if b < 4 else kcT[HD:P, :]
                        nc.vector.tensor_tensor(dst, ps[HD:P, 4 + b % 2, 0:512 if b < 4 else NB],
                                                dst.bitcast(F32), ALU.subtract).then_inc(s_klo, 1)
                    dve.wait_ge(s_kt, K(6, 6))
                    for g in range(NG):
                        last = nc.vector.tensor_copy(vc[32 * g:32 * g + NB, g, :], ps[32 * g:32 * g + NB, 5, 0:HD])
                    last.then_inc(s_klo, 1)
                    for what, x, y in steps:
                        if what == "query":
                            dve.wait_ge(s_qhi, K(x + 1, NT))
                            nc.vector.tensor_tensor(q_lo[:, x % 2, :], ps[:, 7, :],
                                                    q_hi[:, x % 2, :].bitcast(F32), ALU.subtract
                                                    ).then_inc(s_spr, 1)
                        elif what == "c_scores":
                            dve.wait_ge(s_sp, K(place["cs", x] + 1, USES))
                            nc.vector.tensor_tensor(
                                c_s[:, :, :], ps[:, 7, 0:NG * NB].rearrange("p (g n) -> p g n", g=NG),
                                c_pen[:, x, :].unsqueeze(1).to_broadcast([P, NG, NB]), ALU.add
                            ).then_inc(s_spr, 1)
                            dve.wait_ge(s_spr, K(place["cs", x] + 1, USES))
                            v.did(nc.vector.tensor_reduce(c_stat[:, 0, :], c_s[:, :, :], AX, ALU.min))
                            v.wait()
                            nc.vector.tensor_tensor(c_s[:, :, :], c_s[:, :, :],
                                                    c_stat[:, 0, :].unsqueeze(2).to_broadcast([P, NG, NB]),
                                                    ALU.subtract).then_inc(s_cs, 1)
                        elif what == "least":
                            h = NG * x + y
                            n = tiles_of[x] * P
                            dve.wait_ge(s_qk, K(h + 1, HEADS))
                            nc.vector.tensor_reduce(least[:, h:h + 1], S(y, n), AX, ALU.min).then_inc(s_mx, 1)
                        elif what == "turn":
                            t = first_tile[x] + y
                            dve.wait_ge(s_pth, K(t + 1, TILES))
                            nc.vector.tensor_tensor(pt_lo[:, t % PTS, :], ps[:, 4 + t % 2, :],
                                                    pt_hi[:, t % PTS, :].bitcast(F32), ALU.subtract
                                                    ).then_inc(s_ptl, 1)
                        elif what == "output":
                            i, br = x // 2, x % 2
                            v.did(nc.vector.reciprocal(factor[:, 0, :], rowsum[:, NG * x:NG * x + NG]))
                            v.wait()
                            v.did(nc.vector.tensor_tensor(factor[:, 0, :], factor[:, 0, :], g_st[:, i, :, br + 1],
                                                          ALU.mult))
                            v.wait()
                            dve.wait_ge(s_sp, K(place["z", x] + 1, USES))
                            nc.vector.tensor_tensor(
                                scaled[:, :, :], ps[:, 7, 0:NG * HD].rearrange("p (g e) -> p g e", g=NG),
                                factor[:, 0, :].unsqueeze(2).to_broadcast([P, NG, HD]), ALU.mult
                            ).then_inc(s_spr, 1)
                            dve.wait_ge(s_spr, K(place["z", x] + 1, USES))
                            acc = o_acc[:, i % 2, :, :]
                            out = acc if br == 0 else o_nsa[:, i, bass.ds(kv * NG * HD, NG * HD)].rearrange(
                                "p (g d) -> p g d", g=NG)
                            v.did(nc.vector.tensor_tensor(out, acc, scaled[:, :, :], ALU.add))
                            v.wait()
                        elif what == "c_exp":
                            dve.wait_ge(s_ce, K(x + 1, NT))
                            v.did(nc.vector.tensor_tensor(
                                c_e[:, :, :], c_e[:, :, :], c_mask[:, x, :].unsqueeze(1).to_broadcast([P, NG, NB]),
                                ALU.mult))
                            v.wait()
                            v.did(nc.vector.tensor_reduce(c_stat[:, 1, :], c_e[:, :, :], AX, ALU.add))
                            nc.vector.tensor_copy(c_p[:, :, 0:NB], c_e[:, :, :]).then_inc(s_cp, 1)
                            v.wait()
                            v.did(nc.vector.tensor_scalar(c_stat[:, 1, :], c_stat[:, 1, :], 0.5, None, ALU.max))
                            v.wait()
                            v.did(nc.vector.reciprocal(c_stat[:, 2, :], c_stat[:, 1, :]))
                            v.wait()
                            v.did(nc.vector.tensor_tensor(factor[:, 1, :], c_stat[:, 2, :], g_st[:, x, :, 0],
                                                          ALU.mult))
                            v.wait()
                        elif what == "c_turn":
                            dve.wait_ge(s_sp, K(place["ct", x] + 1, USES))
                            nc.vector.tensor_copy(c_pT[:, :], ps[:, 7, 0:P]).then_inc(s_spr, 1)
                        elif what == "c_values":
                            dve.wait_ge(s_sp, K(place["co", x] + 1, USES))
                            nc.vector.tensor_tensor(
                                o_acc[:, x % 2, :, :], ps[:, 7, 0:NG * HD].rearrange("p (g d) -> p g d", g=NG),
                                factor[:, 1, :].unsqueeze(2).to_broadcast([P, NG, HD]), ALU.mult
                            ).then_inc(s_spr, 1)
                            dve.wait_ge(s_spr, K(place["co", x] + 1, USES))
                v.end_loop(NKV)

def attend_sample(nc, sem, ident, pres, o_nsa, ps, attn_dram, gate_dram, cache_cmp_kv, cache_slc_kv,
                  cache_win_kv, page_table, w_cmp_k, w_cmp_v):
    PAIRS = DB // 2
    CHT = 8
    NCH = PAGE // CHT
    RINGC = 3
    KEEP = 16 - 1
    FORCE = 1e4
    ROW = NKV * HD
    NBAT = 2 * NPG // 4
    WT = WIN // P
    TB = [("k", b) for b in range(NBAT)] + [("p", b) for b in range(NPG // 4)] + [("pn", 0)] + \
         [("wk", 0), ("wk", 1), ("wp", 0), ("wpn", 0), ("cp", 0)]
    tb = {x: n for n, x in enumerate(TB)}
    NTB = len(TB)

    with ExitStack() as ctx:
        sb = lambda name, shape, dt=F32: ctx.enter_context(nc.sbuf_tensor(name, shape, dt))
        free = pres[:, 0:NT, :].rearrange("p a b -> p (a b)")
        chunk = [free[:, n * 2048:(n + 1) * 2048] for n in range(RINGC)]
        prod = [free[:, (RINGC + n) * 2048:(RINGC + n + 1) * 2048] for n in range(2)]
        same = free[:, (RINGC + 2) * 2048:(RINGC + 2) * 2048 + P]
        new = pres[0:NS, NT, :]
        kv = sb("kv_pages", [P, 2, 2, NPG, 2, ROW])
        wkv = sb("kv_window", [P, 2, 2, WT, 2, ROW])
        kT = sb("kT_s", [P, 2, 512])
        pT = sb("pT_s", [P, 2, 4, P])
        prob = sb("prob_s", [P, PAST + P])
        probw = sb("probw_s", [P, WIN + P])
        q_nat = sb("q_nat", [NS, NG, NKV, HD])
        q_bd = sb("q_bd", [P, DB, NKV, NG, DS])
        q_pair = sb("q_pair", [P, P])
        k_new = sb("k_new", [P, 2, NS])
        wb = sb("wb", [P, 2, CB])
        pages = sb("pages", [P, 1], I32)
        page16 = sb("page16", [P, 1], I32)
        chunk_no = sb("chunk_no", [P, NCH], I32)
        rows16 = sb("rows16", [P, NCH], I32)
        part = sb("part", [P, 2, ROW])
        kc = sb("kc", [P, 2, 2, ROW])
        kcT = sb("kcT_s", [P, 2, P])
        gates = sb("gates_s", [P, PAIRS, 3])
        row_i = sb("row_i", [P, 1], I32)
        row_t = sb("row_t", [P, 1])
        col_i = sb("col_i", [P, P], I32)
        col_t = sb("col_t", [P, P])
        quad = sb("quad", [P, P])
        causal8 = sb("causal8", [P, DS])
        own = sb("own", [P, PAIRS, DB])
        own_pen = sb("own_pen", [P, PAIRS, DB])
        new_pen = sb("new_pen", [P, PAIRS, DB, DS])
        wpen = sb("wpen", [P, DS])
        kvsel = sb("kvsel", [P, 2])
        before = sb("before", [P, NBLK, NBLK])
        c_s = sb("cs_s", [P, 2, DB, NPG])
        c_e = sb("ce_s", [P, 2 * P])
        imp = sb("imp", [P, NBLK])
        above = sb("above", [P, NBLK, NBLK])
        ties = sb("ties", [P, NBLK, NBLK])
        rank = sb("rank", [P, NBLK])
        selpen = sb("selpen", [P, NBLK])
        st = sb("st_s", [P, 24])
        o_row = sb("o_row", [P, HD])

        s_misc, s_gl = sem("misc_loaded_c"), sem("gates_loaded")
        s_gst = sem("gates_stored")
        s_ch = [sem(f"chunk_loaded_{n}") for n in range(RINGC)]
        s_idx, s_prod, s_part = sem("indices_ready"), sem("product_ready"), sem("chunk_summed")
        s_int = sem("int_consts")
        s_const = sem("consts_c")
        s_qn, s_qt, s_qbd = sem("q_natural"), sem("q_turned"), sem("q_blockdiag")
        s_kc, s_kct, s_kce = sem("kc_done"), sem("kc_turned"), sem("kc_copied")
        s_kv = [[sem(f"pages_{s}{b}") for b in range(2)] for s in range(2)]
        s_wn = [sem(f"window_{s}") for s in range(2)]
        s_qp = sem("q_pair_ready")
        s_csc, s_cmx, s_cex, s_cpn = sem("c_scored"), sem("c_maxed"), sem("c_exped"), sem("c_normed")
        s_imp = sem("importance")
        s_tb, s_tbe = sem("bank_turned"), sem("bank_copied")
        s_sc, s_mx, s_ex = sem("s_scored"), sem("s_maxed"), sem("s_exped")
        s_pv = sem("s_values")
        s_comb = sem("s_combined")
        s_ost, s_fin = sem("o_stored"), sem("o_back")
        v_done, g_done, a_done = sem("dve_done_c"), sem("pool_done_c"), sem("act_done_c")

        with nc.Block() as block:

            @block.sync
            def _(sp):
                sp.dma_start(pages[:, :], page_table.rearrange("b (j o) -> (b j) o", o=1)).then_inc(s_misc, 16)
                for n, w in enumerate((w_cmp_k, w_cmp_v)):
                    sp.dma_start(wb[:, n, :], w[0:1, :].to_broadcast([P, CB])).then_inc(s_misc, 16)
                sp.dma_start(gate_dram, new[:, C_GATE:C_Z]).then_inc(s_gst, 16)
                sp.wait_ge(s_gst, 16)
                for b in range(DB):
                    sp.dma_start(gates[(b % 2) * HD:(b % 2) * HD + HD, b // 2, :],
                                 gate_dram[b * DS:(b + 1) * DS, :].rearrange("t (k c) -> k t c", c=3)
                                 ).then_inc(s_gl, 16)

                def load_pair(it, s, first):
                    pi = 2 * it + s
                    for b in range(2):
                        for j in range(NPG):
                            page = sp.value_load(page_table[bass.ds(pi * 2 + b, 1), j:j + 1], min_val=0,
                                                 max_val=cache_slc_kv.shape[1] - 1)
                            if b == 0 and j == 0 and not first:
                                sp.wait_ge(s_pv, (it - 1) * 6 + 3 * s + 3)
                            sp.dma_start(kv[:, s, b, j, :, :].rearrange("p c r -> p (c r)"),
                                         cache_slc_kv[0, bass.ds(page, 1)].rearrange(
                                             "o t c h d -> t (o c h d)")).then_inc(s_kv[s][b], 16)
                    sp.dma_start(wkv[:, s, :, :, :, :].rearrange("p b w c r -> p b w (c r)"),
                                 cache_win_kv[0, bass.ds(2 * pi, 2)].rearrange(
                                     "b (w p) c h d -> p b w (c h d)", p=P)).then_inc(s_wn[s], 16)

                for s in range(2):
                    load_pair(0, s, True)
                with sp.Fori(1, PAIRS // 2) as it:
                    for s in range(2):
                        load_pair(it, s, False)
                sp.wait_ge(s_ost, 16 * PAIRS)
                for b in range(DB):
                    sp.dma_start(o_nsa[b * DS:(b + 1) * DS, NT, :].rearrange("t (k d) -> t k d", d=HD),
                                 attn_dram[b].rearrange("h g t d -> t (h g) d")).then_inc(s_fin, 16)
                sp.wait_ge(s_fin, 16 * DB)

            @block.gpsimd
            def _(pool):
                g = Order(pool, g_done)
                g.did(nc.gpsimd.iota(row_i[:, :], pattern=[[0, 1]], base=0, channel_multiplier=1))
                g.did(nc.gpsimd.iota(chunk_no[:, :], pattern=[[1, NCH]], base=0, channel_multiplier=0))
                g.wait()
                nc.gpsimd.iota(col_i[:, :], pattern=[[0, 16], [1, 8]], base=0,
                               channel_multiplier=0).then_inc(s_int, 1)
                for m, x in ((q_bd, 0.0), (quad, 0.0), (own, 1.0), (own_pen, 0.0), (before, 1.0), (kvsel, 0.0),
                             (prob[:, PAST + NS:], 0.0), (probw[:, WIN + NS:], 0.0)):
                    g.did(nc.gpsimd.memset(m[:], x))
                g.wait()
                for n in range(4):
                    g.did(nc.gpsimd.memset(quad[32 * n:32 * n + 32, 32 * n:32 * n + 32], 1.0))
                    g.did(nc.gpsimd.memset(kvsel[32 * n:32 * n + 32, n % 2:n % 2 + 1], 1.0))
                    g.wait()
                for b2 in range(2):
                    for m, fill in ((own, 0.0), (own_pen, NEG)):
                        v = m[b2 * HD:b2 * HD + HD]
                        g.did(nc.gpsimd.affine_select(out=v, in_=v, compare_op=ALU.is_equal, fill=fill, base=-b2,
                                                      pattern=[[-2, PAIRS], [1, DB]], channel_multiplier=0))
                    g.wait()
                g.did(nc.gpsimd.affine_select(out=before[:], in_=before[:], compare_op=ALU.is_gt, fill=0.0,
                                              base=0, pattern=[[1, NBLK], [-1, NBLK]], channel_multiplier=0))
                g.wait()
                nc.gpsimd.memset(st[:, 23:24], 0.0).then_inc(s_const, 1)
                pool.wait_ge(s_idx, 1)
                src = cache_cmp_kv.rearrange("o n (c t) k h d -> (o n c) (t k h d)", t=CHT)

                def gather(c):
                    nc.gpsimd.indirect_dma_start(chunk[c % RINGC], None, src,
                                                 bass.IndirectOffsetOnAxis(ap=rows16[:, c:c + 1], axis=0)
                                                 ).then_inc(s_ch[c % RINGC], 16)

                for c in range(RINGC - 1):
                    gather(c)
                for c in range(NCH):
                    if c + RINGC - 1 < NCH:
                        if c > 0:
                            pool.wait_ge(s_prod, c)
                        gather(c + RINGC - 1)
                    pool.wait_ge(s_ch[c % RINGC], 16 * (c // RINGC + 1))
                    if c >= 2:
                        pool.wait_ge(s_part, c - 1)
                    l0 = CHT * (c % (CB // CHT))
                    nc.gpsimd.tensor_tensor(
                        prod[c % 2].rearrange("p (t k r) -> p t k r", t=CHT, k=2),
                        chunk[c % RINGC].rearrange("p (t k r) -> p t k r", t=CHT, k=2),
                        wb[:, :, l0:l0 + CHT].rearrange("p k t -> p t k").unsqueeze(3).to_broadcast(
                            [P, CHT, 2, ROW]), ALU.mult).then_inc(s_prod, 1)

            @block.tensor
            def _(pe):
                pe.wait_ge(s_qn, 1)
                for g in range(NG):
                    mm = nc.tensor.transpose(ps[:, 5, g * NS:(g + 1) * NS],
                                             q_nat[:, g, :, :].rearrange("p h d -> p (h d)"), ident[0:NS, 0:NS])
                for n, c in enumerate((C_SLC, C_WIN)):
                    mm = nc.tensor.transpose(ps[:, 5, (NG + n) * NS:(NG + n + 1) * NS], new[:, c:c + ROW],
                                             ident[0:NS, 0:NS])
                mm.then_inc(s_qt, 1)
                pe.wait_ge(s_kc, 1)
                for half in range(2):
                    mm = nc.tensor.transpose(ps[:, 7, half * P:(half + 1) * P], kc[:, half, 0, :], ident[:, :])
                mm.then_inc(s_kct, 1)
                pe.wait_ge(s_qbd, 1)
                pe.wait_ge(s_kce, 1)
                pe.wait_ge(s_const, 2)
                with pe.Fori(0, PAIRS // 2) as it:
                    for s in range(2):
                        pi = 2 * it + s
                        K = lambda n, per: pi * per + n

                        def turn(x, ins):
                            n = tb[x]
                            if n >= 2:
                                pe.wait_ge(s_tbe, K(n - 1, NTB))
                            for k, (src, w) in enumerate(ins):
                                mm = nc.tensor.transpose(ps[0:w, 5 + n % 2, k * P:(k + 1) * P], src, ident[:, :])
                            mm.then_inc(s_tb, 1)

                        def turned(x):
                            pe.wait_ge(s_tbe, K(tb[x] + 1, NTB))

                        pe.wait_ge(s_qp, pi + 1)
                        nc.tensor.matmul(ps[:, 7, 0:2 * P], q_pair[:, :], kcT[:, :, :].rearrange("p a b -> p (a b)"),
                                         start=True, stop=True).then_inc(s_csc, 1)
                        nc.tensor.matmul(ps[:, 4, 0:NS], q_pair[:, :], k_new[:, 0, :], start=True, stop=True)
                        for n in range(NBAT):
                            b, c = n % 2, n // 2
                            if c == 0:
                                pe.wait_ge(s_kv[s][b], 256 * it + 256)
                            turn(("k", n), [(kv[:, s, b, 4 * c + k, 0, :], P) for k in range(4)])
                            turned(("k", n))
                            mm = nc.tensor.matmul(ps[b * HD:b * HD + HD, c, :], q_pair[:, b * HD:b * HD + HD],
                                                  kT[:, tb["k", n] % 2, :], start=True, stop=True)
                        mm.then_inc(s_sc, 1)
                        pe.wait_ge(s_cpn, pi + 1)
                        nc.tensor.matmul(ps[:, 7, 0:2 * P], same[:, :], c_e[:, :], start=True,
                                         stop=True).then_inc(s_imp, 1)
                        pe.wait_ge(s_ex, K(1, 2))
                        turn(("p", 0), [(prob[:, k * P:(k + 1) * P], P) for k in range(4)])

                        def values(lhs, rhs, rows, first, last):
                            return nc.tensor.matmul(ps[rows, 7, 0:ROW], lhs, rhs, start=first, stop=last,
                                                    skip_group_check=True)

                        for c in range(NPG // 4):
                            if c + 1 < NPG // 4:
                                turn(("p", c + 1), [(prob[:, (4 * c + 4 + k) * P:(4 * c + 5 + k) * P], P)
                                                    for k in range(4)])
                            else:
                                turn(("pn", 0), [(prob[:, PAST:PAST + P], P)])
                            turned(("p", c))
                            for k in range(4):
                                for b in range(2):
                                    values(pT[:, tb["p", c] % 2, k, b * HD:b * HD + HD],
                                           kv[:, s, b, 4 * c + k, 1, :], slice(b * HD, b * HD + HD),
                                           c == 0 and k == 0, False)
                        turned(("pn", 0))
                        values(pT[0:NS, tb["pn", 0] % 2, 0, :], new[:, C_SLC + ROW:C_SLC + 2 * ROW], slice(0, P),
                               False, True).then_inc(s_pv, 1)
                        pe.wait_ge(s_wn[s], 16 * it + 16)
                        for b in range(2):
                            turn(("wk", b), [(wkv[:, s, b, k, 0, :], P) for k in range(WT)])
                            turned(("wk", b))
                            nc.tensor.matmul(ps[b * HD:b * HD + HD, 0, :], q_pair[:, b * HD:b * HD + HD],
                                             kT[:, tb["wk", b] % 2, :], start=True, stop=True)
                        nc.tensor.matmul(ps[:, 1, 0:NS], q_pair[:, :], k_new[:, 1, :], start=True,
                                         stop=True).then_inc(s_sc, 1)
                        pe.wait_ge(s_ex, K(2, 2))
                        turn(("wp", 0), [(probw[:, k * P:(k + 1) * P], P) for k in range(WT)])
                        turn(("wpn", 0), [(probw[:, WIN:WIN + P], P)])
                        turned(("wp", 0))
                        pe.wait_ge(s_comb, K(1, 3))
                        for k in range(WT):
                            for b in range(2):
                                values(pT[:, tb["wp", 0] % 2, k, b * HD:b * HD + HD], wkv[:, s, b, k, 1, :],
                                       slice(b * HD, b * HD + HD), k == 0, False)
                        turned(("wpn", 0))
                        values(pT[0:NS, tb["wpn", 0] % 2, 0, :], new[:, C_WIN + ROW:C_WIN + 2 * ROW], slice(0, P),
                               False, True).then_inc(s_pv, 1)
                        turn(("cp", 0), [(c_e[:, k * P:(k + 1) * P], P) for k in range(2)])
                        turned(("cp", 0))
                        pe.wait_ge(s_comb, K(2, 3))
                        for half in range(2):
                            mm = nc.tensor.matmul(ps[:, 7, 0:ROW], pT[:, tb["cp", 0] % 2, half, :],
                                                  kc[:, half, 1, :], start=(half == 0), stop=(half == 1))
                        mm.then_inc(s_pv, 1)

            @block.scalar
            def _(act):
                a = Order(act, a_done)
                act.wait_ge(s_gl, 16 * DB)
                a.did(nc.scalar.activation(gates[:, :, :], gates[:, :, :], ACT.Sigmoid))
                with act.Fori(0, PAIRS // 2) as it:
                    for s in range(2):
                        pi = 2 * it + s
                        K = lambda n, per: pi * per + n

                        def copy(x, w, n, rows=P):
                            act.wait_ge(s_tb, K(tb[x] + 1, NTB))
                            dst = (kT[:, tb[x] % 2, :] if x[0] in ("k", "wk") else
                                   pT[0:rows, tb[x] % 2, :, :].rearrange("p k r -> p (k r)")[:, 0:n])
                            nc.scalar.activation(dst, ps[0:rows, 5 + tb[x] % 2, 0:n], ACT.Copy).then_inc(s_tbe, 1)

                        act.wait_ge(s_cmx, pi + 1)
                        nc.scalar.activation(c_e[:, :], c_s[:].rearrange("p a b c -> p (a b c)"), ACT.Exp,
                                             scale=SCALE, bias=st[:, 1:2], accum_out=st[:, 2:3]
                                             ).then_inc(s_cex, 1)
                        for n in range(NBAT):
                            copy(("k", n), P, 512)
                        act.wait_ge(s_mx, K(1, 2))
                        nc.scalar.activation(prob[:, 0:PAST], ps[:, 0:4, :].rearrange("p a b -> p (a b)"), ACT.Exp,
                                             scale=SCALE, bias=st[:, 6:7], accum_out=st[:, 7:8])
                        nc.scalar.activation(prob[:, PAST:PAST + NS], ps[:, 4, 0:NS], ACT.Exp, scale=SCALE,
                                             bias=st[:, 6:7], accum_out=st[:, 8:9]).then_inc(s_ex, 1)
                        for c in range(NPG // 4):
                            copy(("p", c), P, 512)
                        copy(("pn", 0), NS, P, NS)
                        for b in range(2):
                            copy(("wk", b), P, 512)
                        act.wait_ge(s_mx, K(2, 2))
                        nc.scalar.activation(probw[:, 0:WIN], ps[:, 0, :], ACT.Exp, scale=SCALE, bias=st[:, 12:13],
                                             accum_out=st[:, 13:14])
                        nc.scalar.activation(probw[:, WIN:WIN + NS], ps[:, 1, 0:NS], ACT.Exp, scale=SCALE,
                                             bias=st[:, 12:13], accum_out=st[:, 14:15]).then_inc(s_ex, 1)
                        copy(("wp", 0), P, 512)
                        copy(("wpn", 0), NS, P, NS)
                        copy(("cp", 0), P, 2 * P)
                        act.wait_ge(s_comb, K(3, 3))
                        act.dma_start(attn_dram.rearrange("b h g t d -> (b h g t) d")[bass.ds(pi * P, P), :],
                                      o_row[:, :]).then_inc(s_ost, 16)
                        act.wait_ge(s_ost, 16 * pi + 16)

            @block.vector
            def _(dve):
                v = Order(dve, v_done)
                dve.wait_ge(s_misc, 48)
                dve.wait_ge(s_int, 1)
                v.did(nc.vector.tensor_scalar(page16[:, :], pages[:, :], float(NCH), None, ALU.mult))
                v.wait()
                nc.vector.tensor_tensor(rows16[:, :], chunk_no[:, :], page16[:, :].to_broadcast([P, NCH]),
                                        ALU.add).then_inc(s_idx, 1)
                v.did(nc.vector.tensor_single_scalar(row_i[:, :], row_i[:, :], 7, ALU.bitwise_and))
                v.wait()
                v.did(nc.vector.tensor_copy(row_t[:, :], row_i[:, :]))
                v.did(nc.vector.tensor_copy(col_t[:, :], col_i[:, :]))
                v.wait()
                v.did(nc.vector.tensor_scalar(same[:, :], col_t[:, :], row_t[:, :], None, ALU.is_equal))
                v.did(nc.vector.tensor_scalar(causal8[:, :], col_t[:, 0:DS], row_t[:, :], None, ALU.is_le))
                v.wait()
                dve.wait_ge(s_const, 1)
                v.did(nc.vector.tensor_tensor(same[:, :], same[:, :], quad[:, :], ALU.mult))
                v.did(nc.vector.tensor_scalar(wpen[:, :], causal8[:, :], NEG, None, ALU.mult))
                v.did(nc.vector.tensor_tensor(
                    new_pen[:], own[:].unsqueeze(3).to_broadcast([P, PAIRS, DB, DS]),
                    causal8[:].unsqueeze(1).unsqueeze(1).to_broadcast([P, PAIRS, DB, DS]), ALU.mult))
                v.wait()
                v.did(nc.vector.tensor_scalar(new_pen[:], new_pen[:], -NEG, NEG, ALU.mult, ALU.add))
                v.did(nc.vector.memset(kc[:], 0.0))
                for g in range(NG):
                    last = nc.vector.tensor_copy(q_nat[:, g, :, :],
                                                 new[:, 0:512].rearrange("p (h g d) -> p h g d", h=NKV, g=NG)[:, :, g, :])
                last.then_inc(s_qn, 1)
                dve.wait_ge(s_qt, 1)
                for h in range(NKV):
                    r = slice(h * HD, (h + 1) * HD)
                    nc.vector.tensor_copy(q_bd[r, :, h, :, :],
                                          ps[r, 5, 0:NG * NS].rearrange("p (g b t) -> p b g t", g=NG, b=DB))
                nc.vector.tensor_copy(k_new[:], ps[:, 5, NG * NS:(NG + 2) * NS].rearrange("p (n c) -> p n c", n=2)
                                      ).then_inc(s_qbd, 1)
                dve.wait_ge(s_qbd, 1)
                v.wait()
                nc.vector.memset(st[:, 22:23], 0.0).then_inc(s_const, 1)
                for c in range(NCH):
                    half = c * CHT // CB
                    dve.wait_ge(s_prod, c + 1)
                    v.did(nc.vector.tensor_reduce(part[:], prod[c % 2].rearrange("p (t k r) -> p k r t", t=CHT, k=2),
                                                  AX, ALU.add))
                    v.wait()
                    nc.vector.tensor_tensor(kc[:, half, :, :], kc[:, half, :, :], part[:], ALU.add
                                            ).then_inc(s_part, 1)
                    dve.wait_ge(s_part, c + 1)
                nc.vector.memset(st[:, 21:22], 0.0).then_inc(s_kc, 1)
                dve.wait_ge(s_kct, 1)
                nc.vector.tensor_copy(kcT[:], ps[:, 7, 0:2 * P].rearrange("p (a b) -> p a b", a=2)
                                      ).then_inc(s_kce, 1)
                with dve.Fori(0, PAIRS // 2) as it:
                    v.loop(it, DVE_PER_PAIRS)
                    for s in range(2):
                        pi = 2 * it + s
                        K = lambda n, per: pi * per + n
                        S4 = ps[:, 0:4, :].rearrange("p a b -> p (a b)")

                        def did(ins):
                            v.did(ins)
                            v.wait()

                        nc.vector.tensor_copy(q_pair[:, :], q_bd[:].rearrange("p b h g t -> p (b h g t)")[
                            :, bass.ds(pi * P, P)]).then_inc(s_qp, 1)
                        dve.wait_ge(s_csc, pi + 1)
                        did(nc.vector.tensor_tensor(
                            c_s[:],
                            ps[:, 7, 0:2 * P].rearrange("p (a b j) -> p a b j", a=2, b=DB),
                            own_pen[:, bass.ds(pi, 1), :].rearrange("p o b -> p (o b)").unsqueeze(1).unsqueeze(3)
                            .to_broadcast([P, 2, DB, NPG]), ALU.add))
                        did(nc.vector.tensor_reduce(st[:, 0:1], c_s[:].rearrange("p a b j -> p (a b j)"), AX, ALU.max))
                        nc.vector.tensor_scalar(st[:, 1:2], st[:, 0:1], -SCALE, None, ALU.mult).then_inc(s_cmx, 1)
                        dve.wait_ge(s_cex, pi + 1)
                        did(nc.vector.reciprocal(st[:, 3:4], st[:, 2:3]))
                        nc.vector.tensor_scalar(c_e[:, :], c_e[:, :], st[:, 3:4], None, ALU.mult).then_inc(s_cpn, 1)
                        dve.wait_ge(s_imp, pi + 1)
                        did(nc.vector.tensor_reduce(
                            imp[:, :].rearrange("p (j a) -> p a j", a=2),
                            ps[:, 7, 0:2 * P].rearrange("p (a b j) -> p a j b", a=2, b=DB), AX, ALU.add))
                        did(nc.vector.memset(imp[:, 0:1], FORCE))
                        did(nc.vector.memset(imp[:, NBLK - 1:NBLK], FORCE))
                        i_m = imp[:, :].unsqueeze(1).to_broadcast([P, NBLK, NBLK])
                        i_n = imp[:, :].unsqueeze(2).to_broadcast([P, NBLK, NBLK])
                        v.did(nc.vector.tensor_tensor(above[:], i_m, i_n, ALU.is_gt))
                        did(nc.vector.tensor_tensor(ties[:], i_m, i_n, ALU.is_equal))
                        did(nc.vector.tensor_tensor(ties[:], ties[:], before[:], ALU.mult))
                        did(nc.vector.tensor_tensor(above[:], above[:], ties[:], ALU.add))
                        did(nc.vector.tensor_reduce(rank[:, :], above[:], AX, ALU.add))
                        did(nc.vector.tensor_scalar(selpen[:, :], rank[:, :], KEEP - 0.5, NEG, ALU.is_gt, ALU.mult))
                        dve.wait_ge(s_sc, K(1, 2))
                        v.did(nc.vector.tensor_tensor(S4.rearrange("p (n l) -> p n l", l=CB),
                                                      S4.rearrange("p (n l) -> p n l", l=CB),
                                                      selpen[:, :].unsqueeze(2).to_broadcast([P, NBLK, CB]), ALU.add))
                        did(nc.vector.tensor_tensor(ps[:, 4, 0:NS], ps[:, 4, 0:NS],
                                                    new_pen[:, bass.ds(pi, 1)].rearrange("p o b t -> p (o b t)"),
                                                    ALU.add))
                        v.did(nc.vector.tensor_reduce(st[:, 4:5], S4, AX, ALU.max))
                        did(nc.vector.tensor_reduce(st[:, 5:6], ps[:, 4, 0:NS], AX, ALU.max))
                        did(nc.vector.tensor_tensor(st[:, 4:5], st[:, 4:5], st[:, 5:6], ALU.max))
                        nc.vector.tensor_scalar(st[:, 6:7], st[:, 4:5], -SCALE, None, ALU.mult).then_inc(s_mx, 1)

                        def factors(branch, sums):
                            if len(sums) == 2:
                                did(nc.vector.tensor_tensor(st[:, 16:17], st[:, sums[0]:sums[0] + 1],
                                                            st[:, sums[1]:sums[1] + 1], ALU.add))
                                did(nc.vector.reciprocal(st[:, 17:18], st[:, 16:17]))
                            else:
                                did(nc.vector.memset(st[:, 17:18], 1.0))
                            did(nc.vector.tensor_tensor(st[:, 17:18], st[:, 17:18],
                                                        gates[:, bass.ds(pi, 1), branch], ALU.mult))
                            did(nc.vector.tensor_scalar(st[:, 18:20], kvsel[:, :], st[:, 17:18], None, ALU.mult))

                        def combine(n):
                            if n == 0:
                                did(nc.vector.tensor_scalar(o_row[:, :], ps[:, 7, 0:HD], st[:, 18:19], None,
                                                            ALU.mult))
                            else:
                                did(nc.vector.scalar_tensor_tensor(o_row[:, :], ps[:, 7, 0:HD], st[:, 18:19],
                                                                   o_row[:, :], ALU.mult, ALU.add))
                            nc.vector.scalar_tensor_tensor(o_row[:, :], ps[:, 7, HD:ROW], st[:, 19:20],
                                                           o_row[:, :], ALU.mult, ALU.add).then_inc(s_comb, 1)
                            dve.wait_ge(s_comb, K(n + 1, 3))

                        dve.wait_ge(s_ex, K(1, 2))
                        factors(1, (7, 8))
                        dve.wait_ge(s_pv, K(1, 3))
                        combine(0)
                        dve.wait_ge(s_sc, K(2, 2))
                        v.did(nc.vector.tensor_tensor(ps[:, 0, 0:DS], ps[:, 0, 0:DS], wpen[:, :], ALU.add))
                        did(nc.vector.tensor_tensor(ps[:, 1, 0:NS], ps[:, 1, 0:NS],
                                                    new_pen[:, bass.ds(pi, 1)].rearrange("p o b t -> p (o b t)"),
                                                    ALU.add))
                        v.did(nc.vector.tensor_reduce(st[:, 10:11], ps[:, 0, :], AX, ALU.max))
                        did(nc.vector.tensor_reduce(st[:, 11:12], ps[:, 1, 0:NS], AX, ALU.max))
                        did(nc.vector.tensor_tensor(st[:, 10:11], st[:, 10:11], st[:, 11:12], ALU.max))
                        nc.vector.tensor_scalar(st[:, 12:13], st[:, 10:11], -SCALE, None, ALU.mult).then_inc(s_mx, 1)
                        dve.wait_ge(s_ex, K(2, 2))
                        factors(2, (13, 14))
                        dve.wait_ge(s_pv, K(2, 3))
                        combine(1)
                        factors(0, ())
                        dve.wait_ge(s_pv, K(3, 3))
                        combine(2)
                v.end_loop(PAIRS // 2)

def finish_rows(nc, sem, ident, pres, cmix_hi, cmix_lo, o_nsa, ps, z_dram, gla_dram, x_prompt, x_sample, norm_post,
                w_out, gla_a2, gla_ab, gla_norm, state_gla, y_prompt, y_sample, new_gla_p, new_gla_s):
    LEVELS = (64, 32, 16, 8)
    NL = len(LEVELS)
    BASE = 8
    LOG_A_MIN = -21.0
    E_BK, E_KD, E_BQ, E_IN = NL, NL + 1, NL + 2, NL + 3
    NE = NL + 4
    CHN = GH * GK
    LAST = NT

    with ExitStack() as ctx:
        sb = lambda name, shape, dt=F32: ctx.enter_context(nc.sbuf_tensor(name, shape, dt))
        flat = pres[:, :, :].rearrange("p a b -> p (a b)")
        at = [0]

        def part(*dims):
            n = int(np.prod(dims))
            at[0] += n
            assert at[0] <= (NT + 1) * NRES
            v = flat[:, at[0] - n:at[0]]
            if len(dims) == 2:
                v = v.rearrange("p (a b) -> p a b", a=dims[0])
            elif len(dims) == 3:
                v = v.rearrange("p (a b c) -> p a b c", a=dims[0], b=dims[1])
            return v

        s0, s1 = part(DB, GH * GV), part(DB, GH * GV)
        qE = part(NL + 1, GH, P)
        kE = part(NL + 2, P)
        post, xr, sq, yt = part(D), part(D), part(D), part(D)
        wo_raw = sb("wo_raw", [P, 2, D])
        wo_hi = sb("wo_hi", [P, KD, D], F32R)
        wo_lo = sb("wo_lo", [P, KD, D], F32R)
        gnorm = sb("gnorm", [P, GV])
        a2 = sb("a2", [GR, CHN])
        a_bias = sb("a_bias", [1, CHN])
        ones = sb("ones", [1, P])
        qka = sb("qka", [P, 2 * CHN + GR])
        vt = sb("vt", [P, GH * GV])
        zt = sb("zt", [P, 2, WZ])
        qT = sb("qT_g", [P, P])
        q_bd = sb("q_bd_g", [P, GH, P])
        kT = sb("kT_g", [P, P])
        aT = sb("aT_g", [GR, P])
        lg = sb("lg", [P, CHN])
        lneg = sb("lneg", [P, CHN])
        lu = sb("lu", [P, CHN])
        log_a = sb("log_a", [P, CHN])
        bT = sb("bT", [P, P])
        dec = sb("dec", [P, NE, P])
        qi = sb("qi", [P, P])
        att = sb("att", [P, GH, P])
        kd = sb("kd", [P, CHN])
        state = sb("state", [P, GH * GV])
        upd = sb("upd", [P, GH * GV])
        bdm = sb("bdm", [P, GH, GV])
        o_g = sb("o_g", [P, GH, GV])
        o_sq = sb("o_sq", [P, GH, GV])
        st = sb("st_d", [P, 16])
        mix = sb("mix", [P, 6 * P])
        m_hi = sb("m_hi", [P, KD, P], F32R)
        m_lo = sb("m_lo", [P, KD, P], F32R)
        eps = sb("eps_d", [P, 1])
        one = sb("one_d", [P, 1])
        upper = sb("upper", [P, P])
        masks = sb("masks", [P, NL, P], I32)
        base_m = sb("base_m", [P, P])
        mk = sb("mk", [P, P])
        ri = sb("ri", [P, 1], I32)
        rj = sb("rj", [P, 2], I32)
        rf = sb("rf", [P, 3])
        ci = sb("ci", [P, P], I32)
        cj = sb("cj", [P, P], I32)
        cf = sb("cf", [P, P])
        qi_b = sb("qi_b", [P, DB * (NS + DS)])
        kd_b = sb("kd_b", [NS, DB, CHN])
        seq_m = sb("seq_m", [NS, DB])

        s_wr = [sem("wo_loaded_0"), sem("wo_loaded_1")]
        s_wh, s_wl = sem("wo_hi_ready"), sem("wo_lo_ready")
        s_cst = sem("small_loaded_d")
        s_s0z, s_s0 = sem("s0_zeroed"), sem("s0_loaded")
        s_qka, s_v, s_z, s_x = sem("qka_loaded"), sem("v_loaded"), sem("z_loaded"), sem("x_loaded_d")
        s_int, s_mask = sem("int_consts_d"), sem("masks_ready")
        s_t1, s_aT, s_qT = sem("qka_turned"), sem("a_turned"), sem("q_turned_d")
        s_lg, s_lgc, s_ls, s_la = sem("logits"), sem("logits_copied"), sem("log1p_done"), sem("log_a_ready")
        s_cs, s_bT, s_D, s_E, s_kq = sem("b_summed"), sem("b_copied"), sem("exponents"), sem("decays"), \
            sem("kq_decayed")
        s_at, s_atr = sem("att_product"), sem("att_taken")
        s_kd, s_kdc, s_o, s_on = sem("kd_turned"), sem("kd_copied"), sem("o_summed"), sem("o_taken")
        s_up, s_st = sem("update_product"), sem("state_ready")
        s_sq, s_ms, s_r4 = sem("o_squared"), sem("o_mean"), sem("o_rms")
        s_mix, s_mt, s_mh, s_ml, s_cm = sem("mix_ready"), sem("mix_turned"), sem("mix_hi"), sem("mix_lo"), \
            sem("conv_mixed")
        s_op, s_rr, s_y, s_ys = sem("out_product"), sem("out_rms"), sem("y_ready"), sem("y_stored")
        s_new = sem("states_stored")
        s_kdm = sem("kd_masked")
        v_done, a_done, g_done = sem("dve_done_d"), sem("act_done_d"), sem("pool_done_d")

        def ge(eng, s, n):
            if not isinstance(n, int) or n > 0:
                eng.wait_ge(s, n)

        def steps(order, gla, out):
            for x in order:
                tile = out if x.startswith("out") else gla
                if tile is not None:
                    yield x, tile

        def rounds(eng, order, run, own=None, per=0):
            for x, t in steps(order, 0, None):
                run(x, t, P, False)
            with eng.Fori(1, NT) as i:
                if own:
                    own.loop(i, per, 1)
                for x, t in steps(order, i, i - 1):
                    run(x, t, P, False)
            if own:
                own.end_loop(NT - 1)
            for x, t in steps(order, LAST, LAST - 1):
                out = x.startswith("out")
                run(x, t, P if out else NS, not out)
            for x, t in steps(order, None, LAST):
                run(x, t, NS, True)

        with nc.Block() as block:

            @block.sync
            def _(sp):
                sp.dma_start(wo_raw[:, 0, :], w_out[0, 0:P, :]).then_inc(s_wr[0], 16)
                sp.dma_start(wo_raw[:, 1, :], w_out[0, P:2 * P, :]).then_inc(s_wr[1], 16)
                sp.dma_start(a2[:, :], gla_a2[0]).then_inc(s_cst, 16)
                sp.dma_start(a_bias[:, :], gla_ab[0:1, :]).then_inc(s_cst, 16)
                sp.dma_start(gnorm[:, :], gla_norm[0:1, :].to_broadcast([P, GV])).then_inc(s_cst, 16)
                sp.dma_start(post[:, :], norm_post[0:1, :].to_broadcast([P, D])).then_inc(s_cst, 16)

                def qk(t, rows):
                    g = gla_dram.rearrange("r a c -> r (a c)")[bass.ds(t * P, rows), :]
                    ge(sp, s_t1, t)
                    sp.dma_start(qka[0:rows, 0:2 * CHN], g[:, 0:2 * CHN]).then_inc(s_qka, 16)
                    sp.dma_start(qka[0:rows, 2 * CHN:], g[:, C_GA - C_GQ:NGL]).then_inc(s_qka, 16)

                def later(t, rows):
                    g = gla_dram.rearrange("r a c -> r (a c)")[bass.ds(t * P, rows), :]
                    ge(sp, s_up, t)
                    sp.dma_start(vt[0:rows, :], g[:, 2 * CHN:2 * CHN + GH * GV]).then_inc(s_v, 16)
                    ge(sp, s_mix, t)
                    sp.dma_start(zt[0:rows, :, :], z_dram[bass.ds(t * P, rows), :, :]).then_inc(s_z, 16)

                def resid(t, rows):
                    ge(sp, s_y, t + 1)
                    src = x_sample.rearrange("b t d -> (b t) d") if t is LAST else x_prompt[0, bass.ds(t * P, P), :]
                    sp.dma_start(xr[0:rows, :], src).then_inc(s_x, 16)

                def store(t, rows):
                    sp.wait_ge(s_y, t + 2)
                    dst = y_sample.rearrange("b t d -> (b t) d") if t is LAST else y_prompt[0, bass.ds(t * P, P), :]
                    sp.dma_start(dst, yt[0:rows, :]).then_inc(s_ys, 16)

                qk(0, P)
                later(0, P)
                for k in range(2, KD):
                    sp.wait_ge(s_wl, k - 1)
                    sp.dma_start(wo_raw[:, k % 2, :], w_out[0, k * P:(k + 1) * P, :]).then_inc(s_wr[k % 2], 16)
                sp.wait_ge(s_s0z, 1)
                for h in range(GH):
                    sp.dma_start(s0[h * GK:(h + 1) * GK, :, h * GV:(h + 1) * GV],
                                 state_gla[0, :, h].rearrange("b k v -> k b v")).then_inc(s_s0, 16)
                with sp.Fori(1, NT) as i:
                    qk(i, P)
                    resid(i - 1, P)
                    later(i, P)
                    store(i - 1, P)
                qk(LAST, NS)
                resid(LAST - 1, P)
                later(LAST, NS)
                store(LAST - 1, P)
                resid(LAST, NS)
                store(LAST, NS)
                for h in range(GH):
                    r, c = slice(h * GK, (h + 1) * GK), slice(h * GV, (h + 1) * GV)
                    sp.dma_start(new_gla_p[0, 0, h], state[r, c]).then_inc(s_new, 16)
                    sp.dma_start(new_gla_s[0, :, h].rearrange("b k v -> k b v"), s1[r, :, c]).then_inc(s_new, 16)
                sp.wait_ge(s_new, 16 * 2 * GH)
                sp.wait_ge(s_ys, 16 * (NT + 1) + 1)

            @block.gpsimd
            def _(pool):
                g = Order(pool, g_done)
                g.did(nc.gpsimd.memset(s0, 0.0))
                g.wait()
                g.did(nc.gpsimd.iota(ri[:, :], pattern=[[0, 1]], base=0, channel_multiplier=1))
                g.did(nc.gpsimd.iota(ci[:, :], pattern=[[1, P]], base=0, channel_multiplier=0))
                for m, x in ((upper, 1.0), (q_bd, 0.0), (bdm, 0.0), (state, 0.0), (ones, 1.0), (qi_b, 0.0),
                             (seq_m, 1.0)):
                    g.did(nc.gpsimd.memset(m[:], x))
                g.wait()
                nc.gpsimd.memset(one[:, :], 1.0).then_inc(s_s0z, 1)
                g.did(nc.gpsimd.affine_select(out=upper[:, :], in_=upper[:, :], compare_op=ALU.is_ge, fill=0.0,
                                              base=0, pattern=[[1, P]], channel_multiplier=-1))
                g.did(nc.gpsimd.affine_select(out=seq_m[:, :], in_=seq_m[:, :], compare_op=ALU.is_ge, fill=0.0,
                                              base=0, pattern=[[-DS, DB]], channel_multiplier=1))
                g.wait()
                g.did(nc.gpsimd.affine_select(out=seq_m[:, :], in_=seq_m[:, :], compare_op=ALU.is_ge, fill=0.0,
                                              base=DS - 1, pattern=[[DS, DB]], channel_multiplier=-1))
                for h in range(GH):
                    g.did(nc.gpsimd.memset(bdm[h * GK:(h + 1) * GK, h, :], 1.0))
                    g.wait()
                nc.gpsimd.memset(eps[:, :], EPS).then_inc(s_int, 1)

                def run(x, t, rows, sample):
                    ge(pool, s_op, 2 * t)
                    for src, dst in ((cmix_hi, m_hi), (cmix_lo, m_lo)):
                        nc.gpsimd.tensor_copy(dst[:, 6:KD, 0:rows],
                                              src[:, :, bass.ds(t * P, rows)].bitcast(F32)).then_inc(s_cm, 1)

                rounds(pool, ("conv",), run)

            @block.tensor
            def _(pe):
                def run(x, t, rows, sample):
                    R = rows
                    if x == "turn":
                        pe.wait_ge(s_qka, 32 * t + 32)
                        ge(pe, s_ml, t)
                        for n, (c, w) in enumerate(((0, CHN), (CHN, CHN), (2 * CHN, GR))):
                            mm = nc.tensor.transpose(ps[0:w, 0, n * P:n * P + R], qka[0:R, c:c + w], ident[0:R, 0:R])
                        mm.then_inc(s_t1, 1)
                    elif x == "logits":
                        pe.wait_ge(s_aT, t + 1)
                        ge(pe, s_bT, t)
                        nc.tensor.matmul(ps[0:R, 1, 0:CHN], aT[:, 0:R], a2[:, :], start=True, stop=False)
                        nc.tensor.matmul(ps[0:R, 1, 0:CHN], ones[:, 0:R], a_bias[:, :], start=False,
                                         stop=True).then_inc(s_lg, 1)
                    elif x in ("out0", "out1"):
                        half = int(x[3])
                        if half == 0:
                            pe.wait_ge(s_ml, t + 1)
                            pe.wait_ge(s_cm, 2 * t + 2)
                            ge(pe, s_y, t + 1)
                        n = 0
                        for k in range(KD):
                            for l, w in ((m_hi, wo_hi), (m_hi, wo_lo), (m_lo, wo_hi)):
                                mm = nc.tensor.matmul(ps[0:R, 2 + half, :], l[:, k, 0:R],
                                                      w[:, k, half * 512:(half + 1) * 512], start=(n == 0),
                                                      stop=(n == 3 * KD - 1))
                                n += 1
                        mm.then_inc(s_op, 1)
                    elif x == "sum":
                        pe.wait_ge(s_la, t + 1)
                        nc.tensor.matmul(ps[:, 1, 0:R], log_a[0:R, :], (base_m if sample else upper)[0:R, 0:R],
                                         start=True, stop=True).then_inc(s_cs, 1)
                    elif x == "att":
                        pe.wait_ge(s_kq, t + 1)
                        base = (NL + 1) * t
                        for e in range(1 if sample else NL + 1):
                            ge(pe, s_atr, base + e - 1 if not isinstance(t, int) or t > 0 or e > 1 else 0)
                            k = E_BK if e == 0 else e - 1
                            mm = nc.tensor.matmul(ps[0:R, 4 + e % 2, :].rearrange("p (h t) -> p h t", h=GH)[:, :, 0:R],
                                                  kE[:, k, 0:R], qE[:, e, :, 0:R], start=True, stop=True)
                            mm.then_inc(s_at, 1)
                    elif x == "kd":
                        nc.tensor.transpose(ps[0:R, 0, 0:CHN], kE[:, E_KD, 0:R], ident[:, :]).then_inc(s_kd, 1)
                    elif x == "o":
                        pe.wait_ge(s_atr, (NL + 1) * t + (1 if sample else NL + 1))
                        ge(pe, s_on, t)
                        pe.wait_ge(s_v, 16 * t + 16)
                        if sample:
                            pe.wait_ge(s_s0, 16 * GH)
                            for b in range(DB):
                                nc.tensor.matmul(ps[0:R, 6, 0:GH * GV], qi_b[:, b * NS:(b + 1) * NS], s0[:, b, :],
                                                 start=(b == 0), stop=False, skip_group_check=True)
                        else:
                            ge(pe, s_st, t)
                            nc.tensor.matmul(ps[0:R, 6, 0:GH * GV], qi[:, 0:R], state[:, :], start=True,
                                             stop=False, skip_group_check=True)
                        for h in range(GH):
                            mm = nc.tensor.matmul(ps[0:R, 6, h * GV:(h + 1) * GV], att[0:R, h, 0:R],
                                                  vt[0:R, h * GV:(h + 1) * GV], start=False, stop=(h == GH - 1),
                                                  skip_group_check=True)
                        mm.then_inc(s_o, 1)
                    elif x == "update":
                        pe.wait_ge(s_kdc, t + 1)
                        if not sample:
                            nc.tensor.matmul(ps[:, 7, 0:GH * GV], kd[0:R, :], vt[0:R, :], start=True,
                                             stop=True).then_inc(s_up, 1)
                        else:
                            pe.wait_ge(s_kdm, 1)
                            for b in range(DB):
                                if b > 0:
                                    pe.wait_ge(s_st, NT + b)
                                nc.tensor.matmul(ps[:, 7, 0:GH * GV], kd_b[:, b, :], vt[0:R, :], start=True,
                                                 stop=True).then_inc(s_up, 1)
                    elif x == "mixturn":
                        pe.wait_ge(s_mix, t + 1)
                        pe.wait_ge(s_st, t + (DB if sample else 1))
                        for n in range(6):
                            mm = nc.tensor.transpose(ps[:, 0 if n < 4 else 7, (n % 4) * P:(n % 4) * P + R],
                                                     mix[0:R, n * P:(n + 1) * P], ident[0:R, 0:R])
                        mm.then_inc(s_mt, 1)

                pe.wait_ge(s_mask, 1)
                pe.wait_ge(s_cst, 64)
                pe.wait_ge(s_wl, KD)
                rounds(pe, ("turn", "logits", "out0", "sum", "out1", "att", "kd", "o", "update", "mixturn"), run)

            @block.scalar
            def _(act):
                a = Order(act, a_done)

                def did(ins):
                    a.did(ins)
                    a.wait()

                def run(x, t, rows, sample):
                    R = rows
                    if x == "turn":
                        act.wait_ge(s_t1, t + 1)
                        nc.scalar.activation(kT[:, 0:R], ps[:, 0, P:P + R], ACT.Copy)
                        nc.scalar.activation(aT[:, 0:R], ps[0:GR, 0, 2 * P:2 * P + R], ACT.Copy).then_inc(s_aT, 1)
                    elif x == "softplus":
                        act.wait_ge(s_lgc, t + 1)
                        did(nc.scalar.activation(lu[0:R, :], lg[0:R, :], ACT.Abs))
                        did(nc.scalar.activation(lu[0:R, :], lu[0:R, :], ACT.Exp, scale=-1.0))
                        nc.scalar.activation(lu[0:R, :], lu[0:R, :], ACT.Ln, bias=one[0:R, :]).then_inc(s_ls, 1)
                    elif x == "decay":
                        act.wait_ge(s_D, t + 1)
                        n0 = E_BK if sample else 0
                        nc.scalar.activation(dec[:, n0:NE, 0:R], dec[:, n0:NE, 0:R], ACT.Exp).then_inc(s_E, 1)
                    elif x == "out":
                        act.wait_ge(s_op, 2 * t + 2)
                        did(nc.scalar.activation(sq[0:R, :], ps[0:R, 2:4, :].rearrange("p a b -> p (a b)"),
                                                 ACT.Square, accum_out=st[0:R, 8:9]))
                        did(nc.scalar.activation(st[0:R, 9:10], st[0:R, 8:9], ACT.Ln, scale=1.0 / D,
                                                 bias=eps[0:R, :]))
                        nc.scalar.activation(st[0:R, 10:11], st[0:R, 9:10], ACT.Exp, scale=-0.5).then_inc(s_rr, 1)
                    elif x == "kd":
                        act.wait_ge(s_kd, t + 1)
                        nc.scalar.activation(kd[0:R, :], ps[0:R, 0, 0:CHN], ACT.Copy).then_inc(s_kdc, 1)
                    elif x == "rms":
                        act.wait_ge(s_on, t + 1)
                        nc.scalar.activation(o_sq[0:R], o_g[0:R], ACT.Square).then_inc(s_sq, 1)
                        act.wait_ge(s_ms, t + 1)
                        did(nc.scalar.activation(st[0:R, 4:8], st[0:R, 0:4], ACT.Ln, scale=1.0 / GV,
                                                 bias=eps[0:R, :]))
                        nc.scalar.activation(st[0:R, 4:8], st[0:R, 4:8], ACT.Exp, scale=-0.5).then_inc(s_r4, 1)
                    elif x == "mixhi":
                        act.wait_ge(s_mt, t + 1)
                        for bank, k0, k1 in ((0, 0, 4), (7, 4, 6)):
                            last = nc.scalar.activation(
                                m_hi[:, k0:k1, 0:R],
                                ps[:, bank, 0:(k1 - k0) * P].rearrange("p (k c) -> p k c", c=P)[:, :, 0:R], ACT.Copy)
                        last.then_inc(s_mh, 1)

                act.wait_ge(s_int, 1)
                for k in range(KD):
                    act.wait_ge(s_wr[k % 2], 16 * (k // 2) + 16)
                    nc.scalar.activation(wo_hi[:, k, :], wo_raw[:, k % 2, :], ACT.Copy).then_inc(s_wh, 1)
                act.wait_ge(s_cst, 64)
                rounds(act, ("turn", "softplus", "decay", "out", "kd", "rms", "mixhi"), run, a, 5)

            @block.vector
            def _(dve):
                v = Order(dve, v_done)

                def did(ins):
                    v.did(ins)
                    v.wait()

                def run(x, t, rows, sample):
                    R = rows
                    if x == "turn":
                        dve.wait_ge(s_aT, t + 1)
                        for h in range(GH):
                            r = slice(h * GK, (h + 1) * GK)
                            nc.vector.tensor_scalar(q_bd[r, h, 0:R], ps[r, 0, 0:R], GK ** -0.5, None, ALU.mult)
                        nc.vector.tensor_scalar(qT[:, 0:R], ps[:, 0, 0:R], GK ** -0.5, None,
                                                ALU.mult).then_inc(s_qT, 1)
                    elif x == "softplus":
                        dve.wait_ge(s_lg, t + 1)
                        nc.vector.tensor_copy(lg[0:R, :], ps[0:R, 1, 0:CHN]).then_inc(s_lgc, 1)
                        dve.wait_ge(s_lgc, t + 1)
                        v.did(nc.vector.tensor_scalar(lneg[0:R, :], lg[0:R, :], 0.0, None, ALU.min))
                        v.wait()
                        dve.wait_ge(s_ls, t + 1)
                        did(nc.vector.tensor_tensor(lneg[0:R, :], lneg[0:R, :], lu[0:R, :], ALU.subtract))
                        nc.vector.tensor_scalar(log_a[0:R, :], lneg[0:R, :], 1.0 / TAU, LOG_A_MIN, ALU.mult,
                                                ALU.max).then_inc(s_la, 1)
                    elif x == "decay":
                        dve.wait_ge(s_cs, t + 1)
                        nc.vector.tensor_copy(bT[:, 0:R], ps[:, 1, 0:R]).then_inc(s_bT, 1)
                        dve.wait_ge(s_bT, t + 1)
                        if not sample:
                            for e, L in enumerate(LEVELS):
                                b = bT[:, :].rearrange("p (n a l) -> p n a l", a=2, l=L)
                                d = dec[:, e, :].rearrange("p (n a l) -> p n a l", a=2, l=L)
                                n = P // (2 * L)
                                r = b[:, :, 0, L - 1:L].to_broadcast([P, n, L])
                                nc.vector.tensor_tensor(d[:, :, 0, :], r, b[:, :, 0, :], ALU.subtract)
                                nc.vector.tensor_tensor(d[:, :, 1, :], b[:, :, 1, :], r, ALU.subtract)
                        b8 = bT[:, 0:R].rearrange("p (n l) -> p n l", l=BASE)
                        c8 = b8[:, :, BASE // 2 - 1:BASE // 2].to_broadcast([P, R // BASE, BASE])
                        v8 = lambda e: dec[:, e, 0:R].rearrange("p (n l) -> p n l", l=BASE)
                        nc.vector.tensor_tensor(v8(E_BK), c8, b8, ALU.subtract)
                        nc.vector.tensor_tensor(v8(E_BQ), b8, c8, ALU.subtract)
                        nc.vector.tensor_copy(dec[:, E_IN, 0:R], bT[:, 0:R])
                        end = (b8[:, :, BASE - 1:BASE].to_broadcast([P, R // BASE, BASE]) if sample else
                               bT[:, P - 1:P].to_broadcast([P, P]))
                        nc.vector.tensor_tensor(v8(E_KD) if sample else dec[:, E_KD, :], end,
                                                b8 if sample else bT[:, :], ALU.subtract).then_inc(s_D, 1)
                        dve.wait_ge(s_E, t + 1)
                        dve.wait_ge(s_qT, t + 1)
                        n0 = E_BK if sample else 0
                        nc.vector.tensor_tensor(kE[:, n0:NL + 2, 0:R], dec[:, n0:NL + 2, 0:R],
                                                kT[:, 0:R].unsqueeze(1).to_broadcast([P, NL + 2 - n0, R]), ALU.mult)
                        for e in range(1 if sample else NL + 1):
                            nc.vector.tensor_tensor(
                                qE[:, e, :, 0:R], q_bd[:, :, 0:R],
                                dec[:, E_BQ if e == 0 else e - 1, 0:R].unsqueeze(1).to_broadcast([P, GH, R]),
                                ALU.mult)
                        if sample:
                            nc.vector.tensor_tensor(
                                qi_b[:, :].rearrange("p (b x) -> p b x", b=DB)[:, :, 0:DS],
                                qT[:, 0:R].rearrange("p (b t) -> p b t", b=DB),
                                dec[:, E_IN, 0:R].rearrange("p (b t) -> p b t", b=DB), ALU.mult).then_inc(s_kq, 1)
                        else:
                            nc.vector.tensor_tensor(qi[:, 0:R], qT[:, 0:R], dec[:, E_IN, 0:R],
                                                    ALU.mult).then_inc(s_kq, 1)
                    elif x == "out":
                        dve.wait_ge(s_rr, t + 1)
                        dve.wait_ge(s_x, 16 * t + 16)
                        dve.wait_ge(s_ys, 16 * t + 1)
                        did(nc.vector.scalar_tensor_tensor(
                            yt[0:R, :], ps[0:R, 2:4, :].rearrange("p a b -> p (a b)"), st[0:R, 10:11],
                            post[0:R, :], ALU.mult, ALU.mult))
                        nc.vector.tensor_tensor(yt[0:R, :], yt[0:R, :], xr[0:R, :], ALU.add).then_inc(s_y, 1)
                    elif x == "att":
                        base = (NL + 1) * t
                        for e in range(1 if sample else NL + 1):
                            dve.wait_ge(s_at, base + e + 1)
                            src = ps[0:R, 4 + e % 2, :].rearrange("p (h t) -> p h t", h=GH)[:, :, 0:R]
                            if e == 0:
                                ins = nc.vector.tensor_tensor(att[0:R, :, 0:R], src, base_m[0:R, 0:R].unsqueeze(
                                    1).to_broadcast([R, GH, R]), ALU.mult)
                            else:
                                dve.wait_ge(s_atr, base + e)
                                nc.vector.memset(st[:, 11:12], 0.0)
                                ins = nc.vector.copy_predicated(
                                    att[:, :, :], masks[:, e - 1, :].unsqueeze(1).to_broadcast([P, GH, P]), src)
                            ins.then_inc(s_atr, 1)
                    elif x == "o":
                        dve.wait_ge(s_o, t + 1)
                        nc.vector.tensor_copy(o_g[0:R], ps[0:R, 6, 0:GH * GV].rearrange("p (h v) -> p h v", h=GH)
                                              ).then_inc(s_on, 1)
                    elif x == "update":
                        if not sample:
                            dve.wait_ge(s_up, t + 1)
                            did(nc.vector.tensor_tensor(upd[:, :], ps[:, 7, 0:GH * GV],
                                                        bdm[:].rearrange("p h v -> p (h v)"), ALU.mult))
                            nc.vector.scalar_tensor_tensor(state[:, :], state[:, :], dec[:, E_IN, P - 1:P],
                                                           upd[:, :], ALU.mult, ALU.add).then_inc(s_st, 1)
                        else:
                            dve.wait_ge(s_kdc, t + 1)
                            nc.vector.tensor_tensor(
                                kd_b[:], kd[0:NS, :].unsqueeze(1).to_broadcast([NS, DB, CHN]),
                                seq_m[:, :].unsqueeze(2).to_broadcast([NS, DB, CHN]), ALU.mult).then_inc(s_kdm, 1)
                            for b in range(DB):
                                dve.wait_ge(s_up, NT + b + 1)
                                nc.vector.scalar_tensor_tensor(
                                    s1[:, b, :], s0[:, b, :], dec[:, E_IN, b * DS + DS - 1:b * DS + DS],
                                    ps[:, 7, 0:GH * GV], ALU.mult, ALU.add).then_inc(s_st, 1)
                    elif x == "rms":
                        dve.wait_ge(s_sq, t + 1)
                        nc.vector.tensor_reduce(st[0:R, 0:4], o_sq[0:R], AX, ALU.add).then_inc(s_ms, 1)
                        dve.wait_ge(s_z, 16 * t + 16)
                        nc.vector.tensor_tensor(
                            mix[0:R, 0:512].rearrange("p (a c) -> p a c", a=2),
                            o_nsa[0:R, bass.ds(t, 1), :].rearrange("p o (a c) -> p (o a) c", a=2),
                            zt[0:R, :, 0:256], ALU.mult)
                        dve.wait_ge(s_r4, t + 1)
                        did(nc.vector.tensor_tensor(o_g[0:R], o_g[0:R],
                                                    st[0:R, 4:8].unsqueeze(2).to_broadcast([R, GH, GV]), ALU.mult))
                        did(nc.vector.tensor_tensor(o_g[0:R], o_g[0:R],
                                                    gnorm[0:R, :].unsqueeze(1).to_broadcast([R, GH, GV]), ALU.mult))
                        nc.vector.tensor_tensor(
                            mix[0:R, 512:768].rearrange("p (a c) -> p a c", a=2),
                            o_g[0:R].rearrange("p (a h) v -> p a (h v)", a=2), zt[0:R, :, 256:WZ],
                            ALU.mult).then_inc(s_mix, 1)
                    elif x == "mixlo":
                        dve.wait_ge(s_mh, t + 1)
                        for bank, k0, k1 in ((0, 0, 4), (7, 4, 6)):
                            last = nc.vector.tensor_tensor(
                                m_lo[:, k0:k1, 0:R],
                                ps[:, bank, 0:(k1 - k0) * P].rearrange("p (k c) -> p k c", c=P)[:, :, 0:R],
                                m_hi[:, k0:k1, 0:R].bitcast(F32), ALU.subtract)
                        last.then_inc(s_ml, 1)

                for s in (s_y, s_ys):
                    nc.vector.memset(st[:, 11:12], 0.0).then_inc(s, 1)
                    dve.wait_ge(s, 1)
                dve.wait_ge(s_int, 1)
                for e, L in enumerate(LEVELS + (BASE,)):
                    sh = L.bit_length() - 1
                    v.did(nc.vector.tensor_single_scalar(rj[:, 0:1], ri[:, :], sh, ALU.logical_shift_right))
                    did(nc.vector.tensor_single_scalar(cj[:, :], ci[:, :], sh, ALU.logical_shift_right))
                    v.did(nc.vector.tensor_single_scalar(rj[:, 1:2], rj[:, 0:1], 1, ALU.bitwise_and))
                    did(nc.vector.tensor_copy(cf[:, :], cj[:, :]))
                    v.did(nc.vector.tensor_scalar(rf[:, 0:1], rj[:, 0:1], 0.0 if e == NL else 1.0, None, ALU.add))
                    did(nc.vector.tensor_scalar(rf[:, 1:2], rj[:, 1:2], -1.0, 1.0, ALU.mult, ALU.add))
                    if e < NL:
                        did(nc.vector.tensor_scalar(mk[:, :], cf[:, :], rf[:, 0:1], rf[:, 1:2], ALU.is_equal,
                                                    ALU.mult))
                        did(nc.vector.tensor_copy(masks[:, e, :], mk[:, :]))
                    else:
                        did(nc.vector.tensor_scalar(mk[:, :], cf[:, :], rf[:, 0:1], None, ALU.is_equal))
                        nc.vector.tensor_tensor(base_m[:, :], mk[:, :], upper[:, :], ALU.mult).then_inc(s_mask, 1)
                dve.wait_ge(s_mask, 1)
                for k in range(KD):
                    dve.wait_ge(s_wh, k + 1)
                    nc.vector.tensor_tensor(wo_lo[:, k, :], wo_raw[:, k % 2, :], wo_hi[:, k, :].bitcast(F32),
                                            ALU.subtract).then_inc(s_wl, 1)
                dve.wait_ge(s_cst, 64)
                rounds(dve, ("turn", "softplus", "decay", "out", "att", "o", "update", "rms", "mixlo"), run, v, 6)


_INS = ["x_prompt", "x_sample", "cache_cmp_kv", "cache_slc_kv", "cache_win_kv", "state_gla", "state_conv",
        "page_table", "norm_pre", "norm_post", "w_in", "w_out", "w_cmp_k", "w_cmp_v", "gla_a2", "gla_ab",
        "gla_norm", "conv_w"]
_OUTS = [(1, SEQ, D), (DB, DS, D), (1, 1, SEQ, 2, NKV, HD), (1, DB, DS, 2, NKV, HD), (1, 1, SEQ, 2, NKV, HD),
         (1, DB, DS, 2, NKV, HD), (1, 1, WIN, 2, NKV, HD), (1, DB, WIN, 2, NKV, HD), (1, 1, GH, GK, GV),
         (1, DB, GH, GK, GV), (1, 1, CK - 1, CW), (1, DB, CK - 1, CW)]


def kernel(**inputs):
    import concourse.bacc as bacc
    from concourse.bass_utils import run_bass_kernel_spmd

    nc = bacc.Bacc("TRN2", target_bir_lowering=False, num_devices=1)
    arrays, args = {}, []
    for name in _INS:
        a = np.ascontiguousarray(inputs[name])
        arrays[f"in_{name}"] = a
        args.append(nc.dram_tensor(f"in_{name}", a.shape, mybir.dt.from_np(a.dtype), kind="ExternalInput").ap())
    for i, shape in enumerate(_OUTS):
        args.append(nc.dram_tensor(f"out_{i}", shape, F32, kind="ExternalOutput").ap())
    with nc.allow_non_contiguous_dma(reason="small columns of weights and states"):
        hybrid_step(nc, *args)
    r = run_bass_kernel_spmd(nc, [arrays], core_ids=[0])
    return tuple(r.results[0][f"out_{i}"] for i in range(len(_OUTS)))
```

```python
from contextlib import ExitStack

import numpy as np

import concourse.bass as bass
from concourse import mybir

ALU = mybir.AluOpType
ACT = mybir.ActivationFunctionType
F32 = mybir.dt.float32
F32R = mybir.dt.float32r
I32 = mybir.dt.int32
AX = mybir.AxisListType.X

P = 128
D = 1024
KD = D // P
SEQ = 1024
NT = SEQ // P
DB, DS = 8, 8
NS = DB * DS
TOK = SEQ + NS
HD = 64
NKV, NG = 2, 4
PAST, PAGE = 2048, 128
NPG = PAST // PAGE
CB = 64
NBLK = PAST // CB
WIN = 512
EPS = 1e-6
NEG = -1e30
SCALE = HD ** -0.5
GH, GK, GV, GR = 4, 32, 64, 16
TAU = 16.0
CW, CK = 256, 3

C_Q, C_CMP, C_SLC, C_WIN, C_GATE, C_Z = 0, 512, 768, 1024, 1280, 1304
C_GQ, C_GA, C_GZ = 1816, 2328, 2344
C_B, C_C, C_H, C_ZC = 2600, 2856, 3112, 3368
NRES = C_Z
WR = NRES // 4
WZ = (512 + 256) // 2
WG = (C_GZ - C_GQ) // 2
WMAX = max(WR, WZ, WG)
NGL = C_GZ - C_GQ
DVE_PER_KV = 103
DVE_PER_PAIRS = 72
CH3 = ((0, 364), (364, 362), (726, 362))


class Order:

    def __init__(self, eng, sem, base=0):
        self.eng, self.sem, self.base, self.it, self.per, self.n = eng, sem, base, None, 0, 0

    def loop(self, it, per, first=0):
        self.base, self.it, self.per, self.n = self.base + self.n - first * per, it, per, 0
        self.first = first

    def end_loop(self, iterations):
        assert self.n == self.per, f"this loop signals {self.n}, not {self.per}"
        self.base, self.it, self.n = self.base + (self.first + iterations) * self.per, None, 0

    def did(self, ins):
        self.n += 1
        ins.then_inc(self.sem, 1)

    def wait(self):
        at = self.base + self.n
        self.eng.wait_ge(self.sem, at if self.it is None else self.it * self.per + at)


def hybrid_step(nc, x_prompt, x_sample, cache_cmp_kv, cache_slc_kv, cache_win_kv, state_gla, state_conv,
                page_table, norm_pre, norm_post, w_in, w_out, w_cmp_k, w_cmp_v, gla_a2, gla_ab, gla_norm,
                conv_w, y_prompt, y_sample, new_cmp_p, new_cmp_s, new_slc_p, new_slc_s, new_win_p, new_win_s,
                new_gla_p, new_gla_s, new_conv_p, new_conv_s):
    z_dram = nc.dram_tensor("z_scratch", (TOK, 2, WZ), F32, kind="Internal").ap()
    gla_dram = nc.dram_tensor("gla_scratch", (TOK, 2, WG), F32, kind="Internal").ap()
    attn_dram = nc.dram_tensor("attn_scratch", (DB, NKV, NG, DS, HD), F32, kind="Internal").ap()
    gate_dram = nc.dram_tensor("gate_scratch", (NS, 3 * NKV * NG), F32, kind="Internal").ap()
    with ExitStack() as ctx:
        sem = lambda name: ctx.enter_context(nc.semaphore(name))
        sb = lambda name, shape, dt=F32: ctx.enter_context(nc.sbuf_tensor(name, shape, dt))
        ident = sb("ident", [P, P])
        pres = sb("pres", [P, NT + 1, NRES])
        cmix_hi = sb("cmix_hi", [P, 2, TOK], F32R)
        cmix_lo = sb("cmix_lo", [P, 2, TOK], F32R)
        ps = ctx.enter_context(nc.psum_tensor("ps", [P, 8, 512], F32))
        project(nc, sem, ident, pres, cmix_hi, cmix_lo, ps, z_dram, gla_dram, x_prompt, x_sample, norm_pre,
                w_in, conv_w, state_conv, cache_win_kv, new_win_s, new_conv_p, new_conv_s)
        o_nsa = sb("o_nsa", [P, NT + 1, 512])
        with nc.sbuf_tensor("kc", [P, 2, 2, NKV * HD], F32) as kc:
            attend_prompt(nc, sem, ident, pres, o_nsa, kc, ps, cache_cmp_kv, page_table, w_cmp_k, w_cmp_v, new_cmp_p, new_cmp_s, new_slc_p,
                          new_slc_s, new_win_p, new_win_s)
            attend_sample(nc, sem, ident, pres, o_nsa, kc, ps, attn_dram, gate_dram, cache_slc_kv, cache_win_kv,
                          page_table)
        finish_rows(nc, sem, ident, pres, cmix_hi, cmix_lo, o_nsa, ps, z_dram, gla_dram, x_prompt, x_sample,
                    norm_post, w_out, gla_a2, gla_ab, gla_norm, state_gla, y_prompt, y_sample, new_gla_p,
                    new_gla_s)


def project(nc, sem, ident, pres, cmix_hi, cmix_lo, ps, z_dram, gla_dram, x_prompt, x_sample, norm_pre, w_in,
            conv_w, state_conv, cache_win_kv, new_win_s, new_conv_p, new_conv_s):
    with ExitStack() as ctx:
        sb = lambda name, shape, dt=F32: ctx.enter_context(nc.sbuf_tensor(name, shape, dt))
        h_hi = sb("h_hi", [P, KD, TOK], F32R)
        h_lo = sb("h_lo", [P, KD, TOK], F32R)
        w_raw = sb("w_raw", [P, KD * WMAX])
        w_hi = sb("w_hi", [P, 2, KD * WMAX], F32R)
        w_lo = sb("w_lo", [P, 2, KD * WMAX], F32R)
        stage = sb("stage", [P, 3, WZ])
        g_col = sb("g_col", [P, KD])
        stat = sb("stat", [P, 4])
        eps = sb("eps", [P, 1])
        start = sb("start", [P, 1])
        cw = sb("cw", [P, 2, CK])
        cstate = sb("cstate", [P, 2, DB, 2])
        cnew_p = sb("cnew_p", [P, 2, 2])
        cnew_s = sb("cnew_s", [P, 2, DB, 2])
        flat = pres[:, :, :].rearrange("p a b -> p (a b)")
        at = [0]

        def part(n):
            at[0] += n
            return flat[:, at[0] - n:at[0]]

        xt = [part(D), part(D)]
        xn = part(D)
        xg = [part(512), part(512)]
        b_t, c_t, h_t, z_t, y_t = part(TOK), part(TOK), part(TOK), part(TOK), part(TOK)
        u_p = part(2 + SEQ)
        u_s = part(DB * (2 + DS)).rearrange("p (b t) -> p b t", b=DB)
        assert at[0] <= (NT + 1) * NRES

        s_small = sem("small_loaded")
        s_x = [sem("x_loaded_0"), sem("x_loaded_1")]
        s_w = sem("w_loaded")
        s_st = [sem(f"stage_stored_{i}") for i in range(3)]
        s_ident = sem("ident_ready")
        s_split = sem("w_split")
        s_rt = sem("row_rms_ready")
        s_xn = sem("x_normed")
        s_xT = sem("x_transposed")
        s_xg = sem("x_scaled")
        s_hi = sem("h_hi_ready")
        s_lo = sem("h_lo_ready")
        s_pj = sem("projected")
        s_ev = sem("projection_copied")
        s_conv = sem("conv_done")
        a_done, v_done, g_done = sem("act_done_a"), sem("dve_done_a"), sem("pool_done_a")
        s_out = sem("copied_out_a")

        def w_cols(c, n):
            return w_in[0, :, bass.ds(c, n)].rearrange("(k p) c -> p k c", p=P)

        def raw(w, a=0, n=None):
            v = w_raw[:, 0:KD * w].rearrange("p (k c) -> p k c", k=KD)
            return v[:, :, a:a + (n or w)]

        with nc.Block() as block:

            @block.sync
            def _(sp):
                sp.dma_start(g_col[:, :], norm_pre[0].rearrange("(k p) -> p k", p=P)).then_inc(s_small, 16)
                sp.dma_start(xt[0], x_prompt[0, 0:P, :]).then_inc(s_x[0], 16)
                sp.dma_start(xt[1], x_prompt[0, P:2 * P, :]).then_inc(s_x[1], 16)
                sp.dma_start(raw(P), w_cols(C_C, P)).then_inc(s_w, 16)
                for h in range(2):
                    sp.dma_start(cw[:, h, :], conv_w[0, :, h * P:(h + 1) * P].rearrange("j p -> p j")
                                 ).then_inc(s_small, 16)
                    sp.dma_start(cstate[:, h, :, :], state_conv[0, :, :, h * P:(h + 1) * P].rearrange(
                        "b r p -> p b r")).then_inc(s_small, 16)
                with sp.Fori(0, 3) as i:
                    for s in range(2):
                        sp.wait_ge(s_xn, 2 * i + s + 1)
                        sp.dma_start(xt[s], x_prompt[0, bass.ds((2 * i + s + 2) * P, P), :]).then_inc(s_x[s], 16)
                sp.wait_ge(s_xn, 7)
                sp.dma_start(xt[0][0:NS, :], x_sample.rearrange("b t d -> (b t) d")).then_inc(s_x[0], 16)
                sp.dma_start(new_win_s[0, :, 0:WIN - DS].rearrange("b w c h d -> b (w c h d)"),
                             cache_win_kv[0, :, DS:WIN].rearrange("b w c h d -> b (w c h d)")).then_inc(s_out, 16)

                for n, c in enumerate((C_H, C_B, C_ZC, C_C + P, C_H + P, C_B + P, C_ZC + P)):
                    sp.wait_ge(s_split, n + 1)
                    sp.dma_start(raw(P), w_cols(c, P)).then_inc(s_w, 16)
                with sp.Fori(0, 4) as i:
                    sp.wait_ge(s_split, 8 + i)
                    sp.dma_start(raw(WR), w_cols(i * WR, WR)).then_inc(s_w, 16)
                for j in range(2):
                    sp.wait_ge(s_split, 12 + 2 * j)
                    sp.dma_start(raw(WZ, 0, 256), w_cols(C_Z + 256 * j, 256)).then_inc(s_w, 16)
                    sp.dma_start(raw(WZ, 256, 128), w_cols(C_GZ + 128 * j, 128)).then_inc(s_w, 16)
                    sp.wait_ge(s_split, 13 + 2 * j)
                    sp.dma_start(raw(WG), w_cols(C_GQ + WG * j, WG)).then_inc(s_w, 16)
                sp.wait_ge(s_conv, 3)
                for h in range(2):
                    sp.dma_start(new_conv_p[0, 0, :, h * P:(h + 1) * P].rearrange("r p -> p r"),
                                 cnew_p[:, h, :]).then_inc(s_out, 16)
                    sp.dma_start(new_conv_s[0, :, :, h * P:(h + 1) * P].rearrange("b r p -> p b r"),
                                 cnew_s[:, h, :, :]).then_inc(s_out, 16)
                sp.wait_ge(s_out, 80)

            @block.gpsimd
            def _(pool):
                g = Order(pool, g_done)
                g.did(nc.gpsimd.memset(ident[:, :], 0.0))
                g.wait()
                nc.gpsimd.affine_select(out=ident[:, :], in_=ident[:, :], compare_op=ALU.not_equal, fill=1.0,
                                        base=0, pattern=[[-1, P]], channel_multiplier=1).then_inc(s_ident, 1)

                def split(slot, w):
                    n = KD * w
                    g.did(nc.gpsimd.tensor_copy(w_hi[:, slot, 0:n], w_raw[:, 0:n]))
                    g.wait()
                    nc.gpsimd.tensor_tensor(w_lo[:, slot, 0:n], w_raw[:, 0:n],
                                            w_hi[:, slot, 0:n].bitcast(F32), ALU.subtract).then_inc(s_split, 1)

                for n in range(8):
                    pool.wait_ge(s_w, 16 * (n + 1))
                    if n >= 2:
                        pool.wait_ge(s_pj, 3 * (n - 1))
                    split(n % 2, P)
                for c in range(8):
                    w = WR if c < 4 else (WZ, WG)[c % 2]
                    pool.wait_ge(s_w, 16 * (9 + c) if c < 4 else (224, 240, 272, 288)[c - 4])
                    pool.wait_ge(s_pj, 21 + 3 * c if c < 2 else 24 + 9 * (c - 1))
                    split(c % 2, w)

            @block.scalar
            def _(act):
                a = Order(act, a_done)

                def norm(i, s, rows):
                    act.wait_ge(s_x[s], 16 * (i + 1))
                    a.did(nc.scalar.activation(ps[0:rows, 0:2, :].rearrange("p a b -> p (a b)"), xt[s][0:rows, :],
                                               ACT.Square, accum_out=stat[0:rows, s:s + 1]))
                    a.wait()
                    nc.scalar.activation(stat[0:rows, 2 + s:3 + s], stat[0:rows, s:s + 1], ACT.Sqrt,
                                         scale=1.0 / D, bias=eps[0:rows, :]).then_inc(s_rt, 1)

                def halves(t, s, rows, col):
                    for f in range(2):
                        act.wait_ge(s_xg, t * 2 + f + 1)
                        nc.scalar.activation(
                            h_hi[:, 4 * f:4 * f + 4, bass.ds(col, rows)],
                            xg[f][:, 0:4 * rows].rearrange("p (k c) -> p k c", k=4), ACT.Copy).then_inc(s_hi, 1)

                act.wait_ge(s_ident, 2)
                with act.Fori(0, 4) as i:
                    a.loop(i, 2)
                    for s in range(2):
                        norm(i, s, P)
                        halves(2 * i + s, s, P, (2 * i + s) * P)
                a.end_loop(4)
                norm(4, 0, NS)
                halves(8, 0, NS, SEQ)
                nc.scalar.activation(start[:, 0:1], eps[:, :], ACT.Copy).then_inc(s_ev, 1)
                with act.Fori(0, 2) as h:
                    for m, (dst, fn) in enumerate(((c_t, ACT.Copy), (h_t, ACT.Copy), (b_t, ACT.Copy),
                                                   (z_t, ACT.Silu))):
                        for c, (t0, tn) in enumerate(CH3):
                            act.wait_ge(s_pj, 12 * h + 3 * m + c + 1)
                            if m == 0 and c == 0:
                                act.wait_ge(s_conv, h + 1)
                            nc.scalar.activation(dst[:, t0:t0 + tn], ps[:, (3 * m + c) % 6, 0:tn],
                                                 fn).then_inc(s_ev, 1)
                act.wait_ge(s_conv, 3)
                with act.Fori(0, 2) as i:
                    for s in range(2):
                        for t in range(NT + 1):
                            rows = P if t < NT else NS
                            n = 9 * s + t
                            act.wait_ge(s_pj, 18 * i + 25 + n)
                            nc.scalar.activation(pres[0:rows, t, bass.ds((2 * i + s) * WR, WR)],
                                                 ps[0:rows, n % 6, 0:WR], ACT.Copy).then_inc(s_ev, 1)
                for j in range(2):
                    for s in range(2):
                        w = (WZ, WG)[s]
                        for t in range(NT + 1):
                            rows = P if t < NT else NS
                            n = 9 * s + t
                            use = 6 * j + n // 3
                            act.wait_ge(s_pj, 61 + 18 * j + n)
                            if use > 0:
                                act.wait_ge(s_st[n % 3], 16 * use)
                            nc.scalar.activation(stage[0:rows, n % 3, 0:w], ps[0:rows, n % 6, 0:w],
                                                 (ACT.Silu, ACT.Copy)[s]).then_inc(s_ev, 1)
                            act.wait_ge(s_ev, 62 + 18 * j + n)
                            dst = (z_dram, gla_dram)[s]
                            act.dma_start(dst[t * P:t * P + rows, j, :], stage[0:rows, n % 3, 0:w]
                                          ).then_inc(s_st[n % 3], 16)
                for q in s_st:
                    act.wait_ge(q, 16 * 12)

            @block.vector
            def _(dve):
                v = Order(dve, v_done)

                def tile(t, s, rows, col):
                    dve.wait_ge(s_rt, t + 1)
                    v.did(nc.vector.reciprocal(stat[0:rows, s:s + 1], stat[0:rows, 2 + s:3 + s]))
                    v.wait()
                    nc.vector.tensor_scalar(xn[0:rows, :], xt[s][0:rows, :], stat[0:rows, s:s + 1], None,
                                            ALU.mult).then_inc(s_xn, 1)
                    for f in range(2):
                        dve.wait_ge(s_xT, 2 * t + f + 1)
                        nc.vector.tensor_tensor(
                            xg[f][:, 0:4 * rows].rearrange("p (k c) -> p k c", k=4),
                            ps[:, 6 + f, 0:4 * rows].rearrange("p (k c) -> p k c", k=4),
                            g_col[:, 4 * f:4 * f + 4].unsqueeze(2).to_broadcast([P, 4, rows]),
                            ALU.mult).then_inc(s_xg, 1)
                    for f in range(2):
                        dve.wait_ge(s_hi, 2 * t + f + 1)
                        nc.vector.tensor_tensor(
                            h_lo[:, 4 * f:4 * f + 4, bass.ds(col, rows)],
                            xg[f][:, 0:4 * rows].rearrange("p (k c) -> p k c", k=4),
                            h_hi[:, 4 * f:4 * f + 4, bass.ds(col, rows)].bitcast(F32),
                            ALU.subtract).then_inc(s_lo, 1)

                nc.vector.memset(eps[:, :], EPS).then_inc(s_ident, 1)
                dve.wait_ge(s_small, 80)
                with dve.Fori(0, 4) as i:
                    v.loop(i, 2)
                    for s in range(2):
                        tile(2 * i + s, s, P, (2 * i + s) * P)
                v.end_loop(4)
                tile(8, 0, NS, SEQ)
                nc.vector.memset(u_p[:, 0:2], 0.0).then_inc(s_conv, 1)
                dve.wait_ge(s_conv, 1)
                with dve.Fori(0, 2) as h:
                    v.loop(h, 12)
                    dve.wait_ge(s_ev, 12 * h + 13)
                    one = lambda w: w[:, bass.ds(h, 1)]
                    v.did(nc.vector.tensor_tensor(u_p[:, 2:2 + SEQ], c_t[:, 0:SEQ], h_t[:, 0:SEQ], ALU.mult))
                    v.did(nc.vector.tensor_tensor(
                        u_s[:, :, 2:2 + DS], c_t[:, SEQ:TOK].rearrange("p (b t) -> p b t", b=DB),
                        h_t[:, SEQ:TOK].rearrange("p (b t) -> p b t", b=DB), ALU.mult))
                    v.did(nc.vector.tensor_copy(u_s[:, :, 0:2],
                                                one(cstate).rearrange("p h b r -> p (h b) r")))
                    v.wait()
                    y_s = y_t[:, SEQ:TOK].rearrange("p (b t) -> p b t", b=DB)
                    for j in range(CK):
                        wj = cw[:, bass.ds(h, 1), j]
                        if j == 0:
                            v.did(nc.vector.tensor_scalar(y_t[:, 0:SEQ], u_p[:, 0:SEQ], wj, None, ALU.mult))
                            v.did(nc.vector.tensor_scalar(y_s, u_s[:, :, 0:DS], wj, None, ALU.mult))
                        else:
                            v.did(nc.vector.scalar_tensor_tensor(y_t[:, 0:SEQ], u_p[:, j:j + SEQ], wj,
                                                                 y_t[:, 0:SEQ], ALU.mult, ALU.add))
                            v.did(nc.vector.scalar_tensor_tensor(y_s, u_s[:, :, j:j + DS], wj, y_s,
                                                                 ALU.mult, ALU.add))
                        v.wait()
                    nc.vector.tensor_copy(one(cnew_p), u_p[:, SEQ:SEQ + 2].unsqueeze(1))
                    nc.vector.tensor_copy(one(cnew_s), u_s[:, :, DS:DS + 2].unsqueeze(1))
                    v.did(nc.vector.tensor_tensor(y_t, y_t, b_t, ALU.mult))
                    v.wait()
                    v.did(nc.vector.tensor_tensor(y_t, y_t, z_t, ALU.mult))
                    v.wait()
                    v.did(nc.vector.tensor_copy(one(cmix_hi), y_t.unsqueeze(1)))
                    v.wait()
                    nc.vector.tensor_tensor(one(cmix_lo), y_t.unsqueeze(1), one(cmix_hi).bitcast(F32),
                                            ALU.subtract).then_inc(s_conv, 1)
                v.end_loop(2)

            @block.tensor
            def _(pe):
                def transposes(t, rows):
                    pe.wait_ge(s_xn, t + 1)
                    for f in range(2):
                        if not isinstance(t, int) or t > 0:
                            pe.wait_ge(s_xg, 2 * t + f - 1)
                        for k in range(4):
                            mm = nc.tensor.transpose(ps[:, 6 + f, k * rows:(k + 1) * rows],
                                                     xn[0:rows, (4 * f + k) * P:(4 * f + k + 1) * P],
                                                     ident[0:rows, 0:rows])
                        mm.then_inc(s_xT, 1)

                pe.wait_ge(s_ident, 2)
                transposes(0, P)
                with pe.Fori(1, NT) as t:
                    transposes(t, P)
                transposes(8, NS)
                pe.wait_ge(s_hi, 18)
                pe.wait_ge(s_lo, 18)

                def wv(buf, slot, w):
                    return buf[:, slot, 0:KD * w].rearrange("p (k c) -> p k c", k=KD)

                def product(out, slot, w, stationary_w, tok):
                    n, mm = 0, None
                    t0, tn = tok
                    for k in range(KD):
                        for ww, hh in ((w_hi, h_hi), (w_hi, h_lo), (w_lo, h_hi)) if stationary_w else (
                                (w_hi, h_hi), (w_lo, h_hi), (w_hi, h_lo)):
                            wk, hk = wv(ww, slot, w)[:, k, :], hh[:, k, t0:t0 + tn]
                            lhs, rhs = (wk, hk) if stationary_w else (hk, wk)
                            mm = nc.tensor.matmul(out, lhs, rhs, start=(n == 0), stop=(n == 3 * KD - 1))
                            n += 1
                    mm.then_inc(s_pj, 1)

                with pe.Fori(0, 2) as h:
                    for m in range(4):
                        pe.wait_ge(s_split, 4 * h + m + 1)
                        for c, tok in enumerate(CH3):
                            n = 3 * m + c
                            pe.wait_ge(s_ev, 12 * h + max(n - 5, 0) + 1)
                            product(ps[:, n % 6, 0:tok[1]], m % 2, P, True, tok)
                with pe.Fori(0, 2) as i:
                    for s in range(2):
                        pe.wait_ge(s_split, 2 * i + s + 9)
                        for t in range(NT + 1):
                            rows = P if t < NT else NS
                            n = 9 * s + t
                            pe.wait_ge(s_ev, 18 * i + n + 20)
                            product(ps[0:rows, n % 6, 0:WR], s, WR, False, (t * P, rows))
                with pe.Fori(0, 2) as j:
                    for s in range(2):
                        pe.wait_ge(s_split, 2 * j + s + 13)
                        w = (WZ, WG)[s]
                        for t in range(NT + 1):
                            rows = P if t < NT else NS
                            n = 9 * s + t
                            pe.wait_ge(s_ev, 18 * j + n + 56)
                            product(ps[0:rows, n % 6, 0:w], s, w, False, (t * P, rows))


def attend_prompt(nc, sem, ident, pres, o_nsa, kc, ps, cache_cmp_kv, page_table, w_cmp_k, w_cmp_v, new_cmp_p, new_cmp_s, new_slc_p,
                  new_slc_s, new_win_p, new_win_s):
    NB = SEQ // CB
    BR = ((C_SLC, 1), (C_WIN, 2))

    def span(u):
        i, br = u // 2, u % 2
        return (0 if br == 0 else max(0, i - WIN // P)), i

    CHT = 8
    NCH = PAGE // CHT
    ROW = NKV * HD
    HIDDEN = 2.0 ** 100
    UNITS = 2 * NT
    LAG, PTS = 2, 3
    BEHIND, PRS = 1, 3
    tiles_of = [span(u)[1] - span(u)[0] + 1 for u in range(UNITS)]
    first_tile = [sum(tiles_of[:u]) for u in range(UNITS + 1)]
    TILES = first_tile[UNITS]
    HEADS = NG * UNITS

    def schedule():
        turned, summed = [], []

        def sums(keep):
            while len(turned) > keep:
                x, t = turned.pop(0)
                yield "sum", x, t
                while summed:
                    yield "output", summed.pop(0), 0
                if t == tiles_of[x] - 1:
                    summed.append(x)

        ahead = ("query", "c_scores", "c_exp", "c_turn", "c_values")
        for what in ahead:
            yield what, 0, 0
        for h in range(HEADS + NG + BEHIND):
            u, y = h // NG, h % NG
            if u < UNITS:
                yield "scores", u, y
            x, g = (h - BEHIND) // NG - 1, (h - BEHIND) % NG
            n = tiles_of[x] if 0 <= x < UNITS else 0
            t0, t1 = -(-n * g // NG), -(-n * (g + 1) // NG)
            for t in range(t0, t1):
                yield "turn", x, t
                if u < UNITS and t == t0:
                    yield "least", u, y
                turned.append((x, t))
                yield from sums(LAG)
            if u < UNITS:
                if t0 == t1:
                    yield "least", u, y
                yield "exp", u, y
                i = (u + 1) // 2
                if u % 2 == 1 and i < NT:
                    yield ahead[y], i, 0
                elif u % 2 == 0 and y == 2 and u > 0:
                    yield ahead[NG], u // 2, 0
        yield from sums(0)
        yield "output", summed.pop(0), 0

    steps = list(schedule())
    for i in range(2, NT):
        assert steps.index(("c_values", i, 0)) > steps.index(("output", 2 * i - 3, 0))
    uses = [(k, x) for what, x, _ in steps
            for k in {"query": ("q",), "c_scores": ("cs",), "c_turn": ("ct",), "c_values": ("co",), "output": ("z",)}.get(what, ())]
    USES = len(uses)
    place = {x: n for n, x in enumerate(uses)}

    with ExitStack() as ctx:
        sb = lambda name, shape, dt=F32: ctx.enter_context(nc.sbuf_tensor(name, shape, dt))
        q_st = sb("q_st", [P, 2, NG, 2, HD])
        g_st = sb("g_st", [P, NT, NG, 3])
        kT = sb("kT", [P, 2, SEQ], F32R)
        vs = sb("vs", [P, 2, NT, 2, HD], F32R)
        kcT = sb("kcT", [P, NB], F32R)
        vc = sb("vc", [P, NG, HD])
        q_hi = sb("q_hi", [P, 2, NG * P], F32R)
        q_lo = sb("q_lo", [P, 2, NG * P], F32R)
        prob = sb("prob", [P, PRS, NG, SEQ])
        k_st = prob[:, PRS - 1, :, :].rearrange("p g n -> p (g n)")[:, 0:3 * NT * P].rearrange(
            "p (n t a d) -> p n t a d", n=3, t=NT, a=2)
        chunk = sb("chunk", [P, 2, CHT * 2 * ROW])
        wb = sb("wb", [P, 2, CB])
        pages = sb("pages", [P, 1], I32)
        page16 = sb("page16", [P, 1], I32)
        chunk_no = sb("chunk_no", [P, NCH], I32)
        rows16 = sb("rows16", [P, NCH], I32)
        pt_hi = sb("pt_hi", [P, PTS, NG * P], F32R)
        pt_lo = sb("pt_lo", [P, PTS, NG * P], F32R)
        oT = sb("oT", [P, NG * P])
        scaled = sb("scaled", [P, NG, HD])
        o_acc = sb("o_acc", [P, 2, NG, HD])
        gate = sb("gate", [P, NT + 1, 3 * NKV * NG])
        least = sb("least", [P, HEADS])
        rowsum = sb("rowsum", [P, HEADS])
        factor = sb("factor", [P, 2, NG])
        ident2 = sb("ident2", [P, HD])
        pen = sb("pen", [P, 2, P])
        pen_r = sb("pen_r", [P, 2, P], F32R)
        ident_r = sb("ident_r", [P, P], F32R)
        c_mask = sb("c_mask", [P, NT, NB])
        c_pen = sb("c_pen", [P, NT, NB])
        c_s = sb("c_s", [P, NG, NB])
        c_e = sb("c_e", [P, NG, NB])
        c_p = sb("c_p", [P, NG, 32])
        c_pT = sb("c_pT", [P, P])
        c_stat = sb("c_stat", [P, 3, NG])
        wk2 = sb("wk2", [P, 2])
        wv2 = sb("wv2", [P, 2])
        wv4 = sb("wv4", [P, NB - 2 + NG * 32])

        s_stored = sem("rows_stored")
        s_w2z, s_w2, s_const = sem("w2_zeroed"), sem("w2_loaded"), sem("consts_b")
        s_gate = sem("gates_ready")
        s_pg, s_iota, s_idx = sem("pages_loaded"), sem("chunk_numbers"), sem("indices_ready")
        s_ch = [sem("chunk_loaded_0"), sem("chunk_loaded_1")]
        s_qst = sem("q_staged")
        s_stg = sem("kv_staged")
        s_kt, s_khi, s_klo = sem("k_transposed"), sem("k_hi"), sem("k_lo")
        s_vhi, s_vlo = sem("v_hi"), sem("v_lo")
        s_sp = sem("spare_written")
        s_spr = sem("spare_read")
        s_qhi = sem("q_hi_ready")
        s_cs, s_ce, s_cp = sem("c_scores"), sem("c_exp"), sem("c_probs")
        s_qk, s_mx, s_exp = sem("scores"), sem("maxed"), sem("exped")
        s_pt, s_pth, s_ptl, s_pv = sem("p_transposed"), sem("pt_hi"), sem("pt_lo"), sem("pv_done")
        s_ot, s_otc = sem("out_summed"), sem("out_copied")
        v_done, g_done = sem("dve_done_b"), sem("pool_done_b")

        def S(g, n):
            return ps[:, 2 * (g % 2):2 * (g % 2) + 2, :].rearrange("p a b -> p (a b)")[:, 0:n]

        with nc.Block() as block:

            @block.sync
            def _(sp):
                sp.dma_start(pages[:, :], page_table.rearrange("b (j o) -> (b j) o", o=1)).then_inc(s_pg, 16)
                for n, w in enumerate((w_cmp_k, w_cmp_v)):
                    sp.dma_start(wb[:, n, :], w[0:1, :].to_broadcast([P, CB])).then_inc(s_pg, 16)
                for dst_p, dst_s, c in ((new_cmp_p, new_cmp_s, C_CMP), (new_slc_p, new_slc_s, C_SLC)):
                    sp.dma_start(dst_p[0, 0].rearrange("(t p) c h d -> p t (c h d)", p=P),
                                 pres[:, 0:NT, c:c + 256]).then_inc(s_stored, 16)
                    sp.dma_start(dst_s[0].rearrange("b t c h d -> (b t) (c h d)"),
                                 pres[0:NS, NT, c:c + 256]).then_inc(s_stored, 16)
                sp.dma_start(new_win_p[0, 0].rearrange("(t p) c h d -> p t (c h d)", p=P),
                             pres[:, NT // 2:NT, C_WIN:C_WIN + 256]).then_inc(s_stored, 16)
                for b in range(DB):
                    sp.dma_start(new_win_s[0, b, WIN - DS:WIN].rearrange("t c h d -> t (c h d)"),
                                 pres[b * DS:(b + 1) * DS, NT, C_WIN:C_WIN + 256]).then_inc(s_stored, 16)
                sp.wait_ge(s_w2z, 2)
                for w, dst in ((w_cmp_k, wk2), (w_cmp_v, wv2)):
                    for b in range(2):
                        sp.dma_start(dst[b * CB:(b + 1) * CB, b:b + 1],
                                     w[0].rearrange("(l o) -> l o", o=1)).then_inc(s_w2, 16)
                sp.wait_ge(s_stored, 16 * 13)

            @block.gpsimd
            def _(pool):
                g = Order(pool, g_done)
                nc.gpsimd.iota(chunk_no[:, :], pattern=[[1, NCH]], base=0, channel_multiplier=0).then_inc(s_iota, 1)
                nc.gpsimd.memset(wk2[:, :], 0.0).then_inc(s_w2z, 1)
                nc.gpsimd.memset(wv2[:, :], 0.0).then_inc(s_w2z, 1)
                for m, x in ((pen, 0.0), (c_pen, 0.0), (c_mask, 1.0), (wv4, 0.0), (vc, 0.0),
                             (c_p, 0.0)):
                    g.did(nc.gpsimd.memset(m[:], x))
                g.wait()
                g.did(nc.gpsimd.affine_select(out=pen[:, 0, :], in_=pen[:, 0, :], compare_op=ALU.is_ge,
                                              fill=HIDDEN, base=0, pattern=[[-1, P]], channel_multiplier=1))
                g.did(nc.gpsimd.affine_select(out=pen[:, 1, :], in_=pen[:, 1, :], compare_op=ALU.is_gt,
                                              fill=HIDDEN, base=0, pattern=[[1, P]], channel_multiplier=-1))
                g.wait()
                g.did(nc.gpsimd.tensor_copy(pen_r[:, :, :], pen[:, :, :]))
                g.did(nc.gpsimd.tensor_copy(ident_r[:, :], ident[:, :]))
                g.did(nc.gpsimd.tensor_tensor(ident2[:, :], ident[:, 0:HD], ident[:, HD:P], ALU.add))
                for m, x in ((c_pen, -NEG), (c_mask, 0.0)):
                    g.did(nc.gpsimd.affine_select(out=m[:, :, :], in_=m[:, :, :], compare_op=ALU.is_ge, fill=x,
                                                  base=-(CB - 1), pattern=[[P, NT], [-CB, NB]],
                                                  channel_multiplier=1))
                pool.wait_ge(s_w2, 64)
                for h in range(NG):
                    g.did(nc.gpsimd.tensor_copy(wv4[:, NB - 2 + 32 * h:NB + 32 * h], wv2[:, :]))
                g.wait()
                nc.gpsimd.memset(c_stat[:], 0.0).then_inc(s_const, 1)

                pool.wait_ge(s_idx, 1)
                src = cache_cmp_kv.rearrange("o n (c t) k h d -> (o n c) (t k h d)", t=CHT)

                def gather(c):
                    nc.gpsimd.indirect_dma_start(chunk[:, c % 2, :], None, src,
                                                 bass.IndirectOffsetOnAxis(ap=rows16[:, c:c + 1], axis=0)
                                                 ).then_inc(s_ch[c % 2], 16)

                def add(out, a, b):
                    g.did(nc.gpsimd.tensor_tensor(out, a, b, ALU.add))
                    g.wait()

                gather(0)
                gather(1)
                for c in range(NCH):
                    x = chunk[:, c % 2, :].rearrange("p (t k r) -> p t k r", t=CHT, k=2)
                    l0 = CHT * c % CB
                    pool.wait_ge(s_ch[c % 2], 16 * (c // 2 + 1))
                    g.did(nc.gpsimd.tensor_tensor(
                        x, x, wb[:, :, l0:l0 + CHT].rearrange("p k t -> p t k").unsqueeze(3).to_broadcast(
                            [P, CHT, 2, ROW]), ALU.mult))
                    g.wait()
                    n = CHT // 2
                    while n > 1:
                        add(x[:, 0:n], x[:, 0:n], x[:, n:2 * n])
                        n //= 2
                    blk = kc[:, CHT * c // CB, :, :]
                    if l0 == 0:
                        add(blk, x[:, 0], x[:, 1])
                    else:
                        add(x[:, 0], x[:, 0], x[:, 1])
                        add(blk, blk, x[:, 0])
                    if c + 2 < NCH:
                        gather(c + 2)

            @block.tensor
            def _(pe):
                pe.wait_ge(s_const, 1)
                with pe.Fori(0, NKV) as kv:
                    K = lambda n, per: kv * per + n

                    def spare(x):
                        if place[x] > 0:
                            pe.wait_ge(s_spr, K(place[x], USES))
                        return ps[:, 7, :]

                    pe.wait_ge(s_stg, kv + 1)
                    for b in range(4):
                        if b >= 2:
                            pe.wait_ge(s_klo, K(b - 1, 6))
                        for t in range(4):
                            mm = nc.tensor.transpose(
                                ps[:, 4 + b % 2, t * P:(t + 1) * P],
                                k_st[:, b // 2, 4 * (b % 2) + t, :, :].rearrange("p a d -> p (a d)"),
                                ident[:, :])
                        mm.then_inc(s_kt, 1)
                    pe.wait_ge(s_klo, K(3, 6))
                    for j in range(NT):
                        mm = nc.tensor.matmul(ps[:, 4, 2 * j:2 * j + 2],
                                              k_st[:, 2, j, :, :].rearrange("p a d -> p (a d)"), wk2[:, :],
                                              start=True, stop=True)
                    mm.then_inc(s_kt, 1)
                    pe.wait_ge(s_klo, K(4, 6))
                    for j in range(NT):
                        mm = nc.tensor.matmul(ps[:, 5, 0:HD], wv4[:, NB - 2 - 2 * j:NB - 2 - 2 * j + NG * 32],
                                              pres[:, j, bass.ds(kv * HD + C_CMP + P, HD)],
                                              start=(j == 0), stop=(j == NT - 1))
                    mm.then_inc(s_kt, 1)
                    pe.wait_ge(s_klo, K(6, 6))
                    pe.wait_ge(s_vlo, K(2, 2))
                    for what, x, y in steps:
                        if what == "query":
                            pe.wait_ge(s_qst, K(x + 1, NT))
                            out = spare(("q", x))
                            for g in range(NG):
                                mm = nc.tensor.transpose(
                                    out[:, g * P:(g + 1) * P],
                                    q_st[:, x % 2, g, :, :].rearrange("p a d -> p (a d)"), ident[:, :])
                            mm.then_inc(s_sp, 1)
                        elif what == "c_scores":
                            out = spare(("cs", x))
                            for g in range(NG):
                                for q in (q_hi, q_lo):
                                    mm = nc.tensor.matmul(out[:, g * NB:(g + 1) * NB],
                                                          q[:, x % 2, g * P:(g + 1) * P], kcT[:, :],
                                                          start=(q is q_hi), stop=(q is q_lo))
                            mm.then_inc(s_sp, 1)
                        elif what == "scores":
                            i, br = x // 2, x % 2
                            j0, j1 = span(x)
                            h = NG * x + y
                            if h >= 2:
                                pe.wait_ge(s_exp, K(h - 1, HEADS))
                            for c in range(j0, j1 + 1, 4):
                                n = min(4, j1 + 1 - c) * P
                                bank = 2 * (y % 2) + (c - j0) // 4
                                edges = []
                                if c + n // P > j1:
                                    edges.append((n - P, 0))
                                if c == j0 and br == 1 and i >= WIN // P:
                                    edges.append((0, 1))
                                for q in (q_hi, q_lo):
                                    mm = nc.tensor.matmul(ps[:, bank, 0:n], q[:, i % 2, y * P:(y + 1) * P],
                                                          kT[:, br, c * P:c * P + n],
                                                          start=(q is q_hi), stop=(q is q_lo and not edges))
                                for at, edge in edges:
                                    mm = nc.tensor.matmul(ps[:, bank, at:at + P], ident_r[:, :],
                                                          pen_r[:, edge, :], start=False,
                                                          stop=((at, edge) == edges[-1]))
                            mm.then_inc(s_qk, 1)
                        elif what == "turn":
                            t = first_tile[x] + y
                            if y == 0:
                                pe.wait_ge(s_exp, K(NG * (x + 1), HEADS))
                            if t >= 2:
                                pe.wait_ge(s_ptl, K(t - 1, TILES))
                            for g in range(NG):
                                mm = nc.tensor.transpose(ps[:, 4 + t % 2, g * P:(g + 1) * P],
                                                         prob[:, x % PRS, g, y * P:(y + 1) * P], ident[:, :])
                            mm.then_inc(s_pt, 1)
                        elif what == "sum":
                            t = first_tile[x] + y
                            if y == 0 and x > 0:
                                pe.wait_ge(s_otc, K(x, UNITS))
                            for s, buf in ((s_pth, pt_hi), (s_ptl, pt_lo)):
                                pe.wait_ge(s, K(t + 1, TILES))
                                mm = nc.tensor.matmul(
                                    ps[:, 6, :],
                                    vs[:, x % 2, span(x)[0] + y, :, :].rearrange("p a d -> p (a d)"),
                                    buf[:, t % PTS, :], start=(y == 0 and buf is pt_hi),
                                    stop=(y == tiles_of[x] - 1 and buf is pt_lo))
                            mm.then_inc(s_pv, 1)
                        elif what == "output":
                            out = spare(("z", x))
                            pe.wait_ge(s_otc, K(x + 1, UNITS))
                            for g in range(NG):
                                mm = nc.tensor.matmul(out[:, g * HD:(g + 1) * HD], oT[:, g * P:(g + 1) * P],
                                                      ident2[:, :], start=True, stop=True)
                            mm.then_inc(s_sp, 1)
                        elif what == "c_turn":
                            out = spare(("ct", x))
                            pe.wait_ge(s_cp, K(x + 1, NT))
                            nc.tensor.transpose(out[:, 0:P], c_p[:, :, :].rearrange("p g n -> p (g n)"),
                                                ident[:, :]).then_inc(s_sp, 1)
                        elif what == "c_values":
                            out = spare(("co", x))
                            nc.tensor.matmul(out[:, 0:NG * HD], c_pT[:, :],
                                             vc[:, :, :].rearrange("p g d -> p (g d)"),
                                             start=True, stop=True).then_inc(s_sp, 1)

            @block.scalar
            def _(act):
                nc.scalar.activation(gate[:, 0:NT, :], pres[:, 0:NT, C_GATE:C_Z], ACT.Sigmoid)
                nc.scalar.activation(gate[0:NS, NT, :], pres[0:NS, NT, C_GATE:C_Z], ACT.Sigmoid
                                     ).then_inc(s_gate, 1)
                with act.Fori(0, NKV) as kv:
                    K = lambda n, per: kv * per + n
                    act.wait_ge(s_stg, kv + 1)
                    for br, (c, _) in enumerate(BR):
                        nc.scalar.activation(vs[:, br, :, 0, :], pres[:, 0:NT, bass.ds(kv * HD + c + P, HD)],
                                             ACT.Copy).then_inc(s_vhi, 1)
                    for b in range(5):
                        act.wait_ge(s_kt, K(b + 1, 6))
                        dst = kT[:, b // 2, 512 * (b % 2):512 * (b % 2) + 512] if b < 4 else kcT[:, :]
                        nc.scalar.activation(dst, ps[:, 4 + b % 2, 0:512 if b < 4 else NB],
                                             ACT.Copy).then_inc(s_khi, 1)
                    for what, x, y in steps:
                        if what == "query":
                            act.wait_ge(s_sp, K(place["q", x] + 1, USES))
                            nc.scalar.activation(q_hi[:, x % 2, :], ps[:, 7, :], ACT.Copy).then_inc(s_qhi, 1)
                        elif what == "c_exp":
                            act.wait_ge(s_cs, K(x + 1, NT))
                            nc.scalar.activation(c_e[:, :, :], c_s[:, :, :], ACT.Exp, scale=-1.0
                                                 ).then_inc(s_ce, 1)
                        elif what == "exp":
                            h = NG * x + y
                            n = tiles_of[x] * P
                            act.wait_ge(s_mx, K(h + 1, HEADS))
                            nc.scalar.activation(prob[:, x % PRS, y, 0:n], S(y, n), ACT.Exp, scale=-1.0,
                                                 bias=least[:, h:h + 1],
                                                 accum_out=rowsum[:, h:h + 1]).then_inc(s_exp, 1)
                        elif what == "turn":
                            t = first_tile[x] + y
                            act.wait_ge(s_pt, K(t + 1, TILES))
                            if t >= PTS:
                                act.wait_ge(s_pv, K(t - PTS + 1, TILES))
                            nc.scalar.activation(pt_hi[:, t % PTS, :], ps[:, 4 + t % 2, :],
                                                 ACT.Copy).then_inc(s_pth, 1)
                        elif what == "sum":
                            t = first_tile[x] + y
                            if y == tiles_of[x] - 1:
                                act.wait_ge(s_pv, K(t + 1, TILES))
                                if x > 0:
                                    act.wait_ge(s_sp, K(place["z", x - 1] + 1, USES))
                                nc.scalar.activation(oT[:, :], ps[:, 6, :], ACT.Copy).then_inc(s_otc, 1)

            @block.vector
            def _(dve):
                v = Order(dve, v_done)
                dve.wait_ge(s_pg, 48)
                dve.wait_ge(s_iota, 1)
                v.did(nc.vector.tensor_scalar(page16[:, :], pages[:, :], float(NCH), None, ALU.mult))
                v.wait()
                nc.vector.tensor_tensor(rows16[:, :], chunk_no[:, :], page16[:, :].to_broadcast([P, NCH]),
                                        ALU.add).then_inc(s_idx, 1)
                dve.wait_ge(s_gate, 1)
                dve.wait_ge(s_const, 1)
                with dve.Fori(0, NKV) as kv:
                    K = lambda n, per: kv * per + n
                    v.loop(kv, DVE_PER_KV)
                    def stage_query(i):
                        dve_src = pres[:, i, bass.ds(kv * NG * HD, NG * HD)].rearrange("p (g d) -> p g d", g=NG)
                        return [nc.vector.tensor_scalar(q_st[:, i % 2, :, a, :], dve_src, -SCALE, None, ALU.mult)
                                for a in range(2)][-1]

                    for a in range(2):
                        for n, c in enumerate((C_SLC, C_WIN, C_CMP)):
                            v.did(nc.vector.tensor_copy(k_st[:, n, :, a, :],
                                                        pres[:, 0:NT, bass.ds(kv * HD + c, HD)]))
                    v.did(nc.vector.tensor_copy(g_st[:, :, :, :].rearrange("p i g c -> p i (g c)"),
                                                gate[:, 0:NT, bass.ds(kv * NG * 3, NG * 3)]))
                    v.wait()
                    nc.vector.memset(factor[:, 0, :], 0.0).then_inc(s_stg, 1)
                    for br, (c, _) in enumerate(BR):
                        dve.wait_ge(s_vhi, K(br + 1, 2))
                        nc.vector.tensor_tensor(vs[:, br, :, 1, :], pres[:, 0:NT, bass.ds(kv * HD + c + P, HD)],
                                                vs[:, br, :, 0, :].bitcast(F32), ALU.subtract).then_inc(s_vlo, 1)
                    for b in range(5):
                        dve.wait_ge(s_khi, K(b + 1, 5))
                        dst = kT[HD:P, b // 2, 512 * (b % 2):512 * (b % 2) + 512] if b < 4 else kcT[HD:P, :]
                        nc.vector.tensor_tensor(dst, ps[HD:P, 4 + b % 2, 0:512 if b < 4 else NB],
                                                dst.bitcast(F32), ALU.subtract).then_inc(s_klo, 1)
                    dve.wait_ge(s_kt, K(6, 6))
                    for g in range(NG):
                        last = nc.vector.tensor_copy(vc[32 * g:32 * g + NB, g, :], ps[32 * g:32 * g + NB, 5, 0:HD])
                    last.then_inc(s_klo, 1)
                    for i in range(2):
                        stage_query(i).then_inc(s_qst, 1)
                    for what, x, y in steps:
                        if what == "query":
                            dve.wait_ge(s_qhi, K(x + 1, NT))
                            nc.vector.tensor_tensor(q_lo[:, x % 2, :], ps[:, 7, :],
                                                    q_hi[:, x % 2, :].bitcast(F32), ALU.subtract
                                                    ).then_inc(s_spr, 1)
                            if x + 2 < NT:
                                stage_query(x + 2).then_inc(s_qst, 1)
                        elif what == "c_scores":
                            dve.wait_ge(s_sp, K(place["cs", x] + 1, USES))
                            nc.vector.tensor_tensor(
                                c_s[:, :, :], ps[:, 7, 0:NG * NB].rearrange("p (g n) -> p g n", g=NG),
                                c_pen[:, x, :].unsqueeze(1).to_broadcast([P, NG, NB]), ALU.add
                            ).then_inc(s_spr, 1)
                            dve.wait_ge(s_spr, K(place["cs", x] + 1, USES))
                            v.did(nc.vector.tensor_reduce(c_stat[:, 0, :], c_s[:, :, :], AX, ALU.min))
                            v.wait()
                            nc.vector.tensor_tensor(c_s[:, :, :], c_s[:, :, :],
                                                    c_stat[:, 0, :].unsqueeze(2).to_broadcast([P, NG, NB]),
                                                    ALU.subtract).then_inc(s_cs, 1)
                        elif what == "least":
                            h = NG * x + y
                            n = tiles_of[x] * P
                            dve.wait_ge(s_qk, K(h + 1, HEADS))
                            nc.vector.tensor_reduce(least[:, h:h + 1], S(y, n), AX, ALU.min).then_inc(s_mx, 1)
                        elif what == "turn":
                            t = first_tile[x] + y
                            dve.wait_ge(s_pth, K(t + 1, TILES))
                            nc.vector.tensor_tensor(pt_lo[:, t % PTS, :], ps[:, 4 + t % 2, :],
                                                    pt_hi[:, t % PTS, :].bitcast(F32), ALU.subtract
                                                    ).then_inc(s_ptl, 1)
                        elif what == "output":
                            i, br = x // 2, x % 2
                            v.did(nc.vector.reciprocal(factor[:, 0, :], rowsum[:, NG * x:NG * x + NG]))
                            v.wait()
                            v.did(nc.vector.tensor_tensor(factor[:, 0, :], factor[:, 0, :], g_st[:, i, :, br + 1],
                                                          ALU.mult))
                            v.wait()
                            dve.wait_ge(s_sp, K(place["z", x] + 1, USES))
                            nc.vector.tensor_tensor(
                                scaled[:, :, :], ps[:, 7, 0:NG * HD].rearrange("p (g e) -> p g e", g=NG),
                                factor[:, 0, :].unsqueeze(2).to_broadcast([P, NG, HD]), ALU.mult
                            ).then_inc(s_spr, 1)
                            dve.wait_ge(s_spr, K(place["z", x] + 1, USES))
                            acc = o_acc[:, i % 2, :, :]
                            out = acc if br == 0 else o_nsa[:, i, bass.ds(kv * NG * HD, NG * HD)].rearrange(
                                "p (g d) -> p g d", g=NG)
                            v.did(nc.vector.tensor_tensor(out, acc, scaled[:, :, :], ALU.add))
                            v.wait()
                        elif what == "c_exp":
                            dve.wait_ge(s_ce, K(x + 1, NT))
                            v.did(nc.vector.tensor_tensor(
                                c_e[:, :, :], c_e[:, :, :], c_mask[:, x, :].unsqueeze(1).to_broadcast([P, NG, NB]),
                                ALU.mult))
                            v.wait()
                            v.did(nc.vector.tensor_reduce(c_stat[:, 1, :], c_e[:, :, :], AX, ALU.add))
                            nc.vector.tensor_copy(c_p[:, :, 0:NB], c_e[:, :, :]).then_inc(s_cp, 1)
                            v.wait()
                            v.did(nc.vector.tensor_scalar(c_stat[:, 1, :], c_stat[:, 1, :], 0.5, None, ALU.max))
                            v.wait()
                            v.did(nc.vector.reciprocal(c_stat[:, 2, :], c_stat[:, 1, :]))
                            v.wait()
                            v.did(nc.vector.tensor_tensor(factor[:, 1, :], c_stat[:, 2, :], g_st[:, x, :, 0],
                                                          ALU.mult))
                            v.wait()
                        elif what == "c_turn":
                            dve.wait_ge(s_sp, K(place["ct", x] + 1, USES))
                            nc.vector.tensor_copy(c_pT[:, :], ps[:, 7, 0:P]).then_inc(s_spr, 1)
                        elif what == "c_values":
                            dve.wait_ge(s_sp, K(place["co", x] + 1, USES))
                            nc.vector.tensor_tensor(
                                o_acc[:, x % 2, :, :], ps[:, 7, 0:NG * HD].rearrange("p (g d) -> p g d", g=NG),
                                factor[:, 1, :].unsqueeze(2).to_broadcast([P, NG, HD]), ALU.mult
                            ).then_inc(s_spr, 1)
                            dve.wait_ge(s_spr, K(place["co", x] + 1, USES))
                v.end_loop(NKV)

def attend_sample(nc, sem, ident, pres, o_nsa, kc, ps, attn_dram, gate_dram, cache_slc_kv, cache_win_kv,
                  page_table):
    PAIRS = DB // 2
    KEEP = 16 - 1
    FORCE = 1e4
    ROW = NKV * HD
    NBAT = 2 * NPG // 4
    WT = WIN // P
    TB = [("k", b) for b in range(NBAT)] + [("p", b) for b in range(NPG // 4)] + [("pn", 0)] + \
         [("wk", 0), ("wk", 1), ("wp", 0), ("wpn", 0), ("cp", 0)]
    tb = {x: n for n, x in enumerate(TB)}
    NTB = len(TB)

    with ExitStack() as ctx:
        sb = lambda name, shape, dt=F32: ctx.enter_context(nc.sbuf_tensor(name, shape, dt))
        free = pres[:, 0:NT, :].rearrange("p a b -> p (a b)")
        same = free[:, 0:P]
        new = pres[0:NS, NT, :]
        kv = sb("kv_pages", [P, 2, 2, NPG, 2, ROW])
        wkv = sb("kv_window", [P, 2, 2, WT, 2, ROW])
        kT = sb("kT_s", [P, 2, 512])
        pT = sb("pT_s", [P, 2, 4, P])
        prob = sb("prob_s", [P, PAST + P])
        probw = sb("probw_s", [P, WIN + P])
        q_nat = sb("q_nat", [NS, NG, NKV, HD])
        q_bd = sb("q_bd", [P, DB, NKV, NG, DS])
        q_pair = sb("q_pair", [P, P])
        k_new = sb("k_new", [P, 2, NS])
        kcT = sb("kcT_s", [P, 2, P])
        gates = sb("gates_s", [P, PAIRS, 3])
        row_i = sb("row_i", [P, 1], I32)
        row_t = sb("row_t", [P, 1])
        col_i = sb("col_i", [P, P], I32)
        col_t = sb("col_t", [P, P])
        quad = sb("quad", [P, P])
        causal8 = sb("causal8", [P, DS])
        own = sb("own", [P, PAIRS, DB])
        own_pen = sb("own_pen", [P, PAIRS, DB])
        new_pen = sb("new_pen", [P, PAIRS, DB, DS])
        wpen = sb("wpen", [P, DS])
        kvsel = sb("kvsel", [P, 2])
        before = sb("before", [P, NBLK, NBLK])
        c_s = sb("cs_s", [P, 2, DB, NPG])
        c_e = sb("ce_s", [P, 2 * P])
        imp = sb("imp", [P, NBLK])
        above = sb("above", [P, NBLK, NBLK])
        ties = sb("ties", [P, NBLK, NBLK])
        rank = sb("rank", [P, NBLK])
        selpen = sb("selpen", [P, NBLK])
        st = sb("st_s", [P, 24])
        o_row = sb("o_row", [P, HD])

        s_gl = sem("gates_loaded")
        s_gst = sem("gates_stored")
        s_int = sem("int_consts")
        s_const = sem("consts_c")
        s_qn, s_qt, s_qbd = sem("q_natural"), sem("q_turned"), sem("q_blockdiag")
        s_kct, s_kce = sem("kc_turned"), sem("kc_copied")
        s_kv = [[sem(f"pages_{s}{b}") for b in range(2)] for s in range(2)]
        s_wn = [sem(f"window_{s}") for s in range(2)]
        s_qp = sem("q_pair_ready")
        s_csc, s_cmx, s_cex, s_cpn = sem("c_scored"), sem("c_maxed"), sem("c_exped"), sem("c_normed")
        s_imp = sem("importance")
        s_tb, s_tbe = sem("bank_turned"), sem("bank_copied")
        s_sc, s_mx, s_ex = sem("s_scored"), sem("s_maxed"), sem("s_exped")
        s_pv = sem("s_values")
        s_comb = sem("s_combined")
        s_ost, s_fin = sem("o_stored"), sem("o_back")
        v_done, g_done, a_done = sem("dve_done_c"), sem("pool_done_c"), sem("act_done_c")

        with nc.Block() as block:

            @block.sync
            def _(sp):
                sp.dma_start(gate_dram, new[:, C_GATE:C_Z]).then_inc(s_gst, 16)
                sp.wait_ge(s_gst, 16)
                for b in range(DB):
                    sp.dma_start(gates[(b % 2) * HD:(b % 2) * HD + HD, b // 2, :],
                                 gate_dram[b * DS:(b + 1) * DS, :].rearrange("t (k c) -> k t c", c=3)
                                 ).then_inc(s_gl, 16)

                def load_pair(it, s, first):
                    pi = 2 * it + s
                    for b in range(2):
                        for j in range(NPG):
                            if j % 4 == 0:
                                _, numbers = nc.values_load_multi_w_load_instructions(
                                    page_table[bass.ds(pi * 2 + b, 1), j:j + 4], engines=(mybir.EngineType.SP,),
                                    min_val=0, max_val=cache_slc_kv.shape[1] - 1)
                            page = numbers[j % 4]
                            if b == 0 and j == 0 and not first:
                                sp.wait_ge(s_pv, (it - 1) * 6 + 3 * s + 3)
                            sp.dma_start(kv[:, s, b, j, :, :].rearrange("p c r -> p (c r)"),
                                         cache_slc_kv[0, bass.ds(page, 1)].rearrange(
                                             "o t c h d -> t (o c h d)")).then_inc(s_kv[s][b], 16)
                    sp.dma_start(wkv[:, s, :, :, :, :].rearrange("p b w c r -> p b w (c r)"),
                                 cache_win_kv[0, bass.ds(2 * pi, 2)].rearrange(
                                     "b (w p) c h d -> p b w (c h d)", p=P)).then_inc(s_wn[s], 16)

                for s in range(2):
                    load_pair(0, s, True)
                with sp.Fori(1, PAIRS // 2) as it:
                    for s in range(2):
                        load_pair(it, s, False)
                sp.wait_ge(s_ost, 16 * PAIRS)
                for b in range(DB):
                    sp.dma_start(o_nsa[b * DS:(b + 1) * DS, NT, :].rearrange("t (k d) -> t k d", d=HD),
                                 attn_dram[b].rearrange("h g t d -> t (h g) d")).then_inc(s_fin, 16)
                sp.wait_ge(s_fin, 16 * DB)

            @block.gpsimd
            def _(pool):
                g = Order(pool, g_done)
                g.did(nc.gpsimd.iota(row_i[:, :], pattern=[[0, 1]], base=0, channel_multiplier=1))
                g.wait()
                nc.gpsimd.iota(col_i[:, :], pattern=[[0, 16], [1, 8]], base=0,
                               channel_multiplier=0).then_inc(s_int, 1)
                for m, x in ((q_bd, 0.0), (quad, 0.0), (own, 1.0), (own_pen, 0.0), (before, 1.0), (kvsel, 0.0),
                             (prob[:, PAST + NS:], 0.0), (probw[:, WIN + NS:], 0.0)):
                    g.did(nc.gpsimd.memset(m[:], x))
                g.wait()
                for n in range(4):
                    g.did(nc.gpsimd.memset(quad[32 * n:32 * n + 32, 32 * n:32 * n + 32], 1.0))
                    g.did(nc.gpsimd.memset(kvsel[32 * n:32 * n + 32, n % 2:n % 2 + 1], 1.0))
                    g.wait()
                for b2 in range(2):
                    for m, fill in ((own, 0.0), (own_pen, NEG)):
                        v = m[b2 * HD:b2 * HD + HD]
                        g.did(nc.gpsimd.affine_select(out=v, in_=v, compare_op=ALU.is_equal, fill=fill, base=-b2,
                                                      pattern=[[-2, PAIRS], [1, DB]], channel_multiplier=0))
                    g.wait()
                g.did(nc.gpsimd.affine_select(out=before[:], in_=before[:], compare_op=ALU.is_gt, fill=0.0,
                                              base=0, pattern=[[1, NBLK], [-1, NBLK]], channel_multiplier=0))
                g.wait()
                nc.gpsimd.memset(st[:, 23:24], 0.0).then_inc(s_const, 1)

            @block.tensor
            def _(pe):
                pe.wait_ge(s_qn, 1)
                for g in range(NG):
                    mm = nc.tensor.transpose(ps[:, 5, g * NS:(g + 1) * NS],
                                             q_nat[:, g, :, :].rearrange("p h d -> p (h d)"), ident[0:NS, 0:NS])
                for n, c in enumerate((C_SLC, C_WIN)):
                    mm = nc.tensor.transpose(ps[:, 5, (NG + n) * NS:(NG + n + 1) * NS], new[:, c:c + ROW],
                                             ident[0:NS, 0:NS])
                mm.then_inc(s_qt, 1)
                for half in range(2):
                    mm = nc.tensor.transpose(ps[:, 7, half * P:(half + 1) * P], kc[:, half, 0, :], ident[:, :])
                mm.then_inc(s_kct, 1)
                pe.wait_ge(s_qbd, 1)
                pe.wait_ge(s_kce, 1)
                pe.wait_ge(s_const, 2)
                with pe.Fori(0, PAIRS // 2) as it:
                    for s in range(2):
                        pi = 2 * it + s
                        K = lambda n, per: pi * per + n

                        def turn(x, ins):
                            n = tb[x]
                            if n >= 2:
                                pe.wait_ge(s_tbe, K(n - 1, NTB))
                            for k, (src, w) in enumerate(ins):
                                mm = nc.tensor.transpose(ps[0:w, 5 + n % 2, k * P:(k + 1) * P], src, ident[:, :])
                            mm.then_inc(s_tb, 1)

                        def turned(x):
                            pe.wait_ge(s_tbe, K(tb[x] + 1, NTB))

                        def turn_keys(n):
                            b, c = n % 2, n // 2
                            if c == 0:
                                pe.wait_ge(s_kv[s][b], 256 * it + 256)
                            turn(("k", n), [(kv[:, s, b, 4 * c + k, 0, :], P) for k in range(4)])

                        pe.wait_ge(s_qp, pi + 1)
                        nc.tensor.matmul(ps[:, 7, 0:2 * P], q_pair[:, :], kcT[:, :, :].rearrange("p a b -> p (a b)"),
                                         start=True, stop=True).then_inc(s_csc, 1)
                        nc.tensor.matmul(ps[:, 4, 0:NS], q_pair[:, :], k_new[:, 0, :], start=True, stop=True)
                        for n in range(NBAT):
                            b, c = n % 2, n // 2
                            if n == 0:
                                turn_keys(0)
                            if n + 1 < NBAT:
                                turn_keys(n + 1)
                            turned(("k", n))
                            mm = nc.tensor.matmul(ps[b * HD:b * HD + HD, c, :], q_pair[:, b * HD:b * HD + HD],
                                                  kT[:, tb["k", n] % 2, :], start=True, stop=True)
                            if n == 2:
                                pe.wait_ge(s_cpn, pi + 1)
                                nc.tensor.matmul(ps[:, 7, 0:2 * P], same[:, :], c_e[:, :], start=True,
                                                 stop=True).then_inc(s_imp, 1)
                        mm.then_inc(s_sc, 1)
                        pe.wait_ge(s_ex, K(1, 2))
                        turn(("p", 0), [(prob[:, k * P:(k + 1) * P], P) for k in range(4)])

                        def values(lhs, rhs, rows, first, last):
                            return nc.tensor.matmul(ps[rows, 7, 0:ROW], lhs, rhs, start=first, stop=last,
                                                    skip_group_check=True)

                        for c in range(NPG // 4):
                            if c + 1 < NPG // 4:
                                turn(("p", c + 1), [(prob[:, (4 * c + 4 + k) * P:(4 * c + 5 + k) * P], P)
                                                    for k in range(4)])
                            else:
                                turn(("pn", 0), [(prob[:, PAST:PAST + P], P)])
                            turned(("p", c))
                            for k in range(4):
                                for b in range(2):
                                    values(pT[:, tb["p", c] % 2, k, b * HD:b * HD + HD],
                                           kv[:, s, b, 4 * c + k, 1, :], slice(b * HD, b * HD + HD),
                                           c == 0 and k == 0, False)
                        turned(("pn", 0))
                        values(pT[0:NS, tb["pn", 0] % 2, 0, :], new[:, C_SLC + ROW:C_SLC + 2 * ROW], slice(0, P),
                               False, True).then_inc(s_pv, 1)
                        pe.wait_ge(s_wn[s], 16 * it + 16)
                        for b in range(2):
                            turn(("wk", b), [(wkv[:, s, b, k, 0, :], P) for k in range(WT)])
                            turned(("wk", b))
                            nc.tensor.matmul(ps[b * HD:b * HD + HD, 0, :], q_pair[:, b * HD:b * HD + HD],
                                             kT[:, tb["wk", b] % 2, :], start=True, stop=True)
                        nc.tensor.matmul(ps[:, 1, 0:NS], q_pair[:, :], k_new[:, 1, :], start=True,
                                         stop=True).then_inc(s_sc, 1)
                        pe.wait_ge(s_ex, K(2, 2))
                        turn(("wp", 0), [(probw[:, k * P:(k + 1) * P], P) for k in range(WT)])
                        turn(("wpn", 0), [(probw[:, WIN:WIN + P], P)])
                        turned(("wp", 0))
                        pe.wait_ge(s_comb, K(1, 3))
                        for k in range(WT):
                            for b in range(2):
                                values(pT[:, tb["wp", 0] % 2, k, b * HD:b * HD + HD], wkv[:, s, b, k, 1, :],
                                       slice(b * HD, b * HD + HD), k == 0, False)
                        turned(("wpn", 0))
                        values(pT[0:NS, tb["wpn", 0] % 2, 0, :], new[:, C_WIN + ROW:C_WIN + 2 * ROW], slice(0, P),
                               False, True).then_inc(s_pv, 1)
                        turn(("cp", 0), [(c_e[:, k * P:(k + 1) * P], P) for k in range(2)])
                        turned(("cp", 0))
                        pe.wait_ge(s_comb, K(2, 3))
                        for half in range(2):
                            mm = nc.tensor.matmul(ps[:, 7, 0:ROW], pT[:, tb["cp", 0] % 2, half, :],
                                                  kc[:, half, 1, :], start=(half == 0), stop=(half == 1))
                        mm.then_inc(s_pv, 1)

            @block.scalar
            def _(act):
                a = Order(act, a_done)
                act.wait_ge(s_gl, 16 * DB)
                a.did(nc.scalar.activation(gates[:, :, :], gates[:, :, :], ACT.Sigmoid))
                with act.Fori(0, PAIRS // 2) as it:
                    for s in range(2):
                        pi = 2 * it + s
                        K = lambda n, per: pi * per + n

                        def copy(x, w, n, rows=P):
                            act.wait_ge(s_tb, K(tb[x] + 1, NTB))
                            dst = (kT[:, tb[x] % 2, :] if x[0] in ("k", "wk") else
                                   pT[0:rows, tb[x] % 2, :, :].rearrange("p k r -> p (k r)")[:, 0:n])
                            nc.scalar.activation(dst, ps[0:rows, 5 + tb[x] % 2, 0:n], ACT.Copy).then_inc(s_tbe, 1)

                        act.wait_ge(s_cmx, pi + 1)
                        nc.scalar.activation(c_e[:, :], c_s[:].rearrange("p a b c -> p (a b c)"), ACT.Exp,
                                             scale=SCALE, bias=st[:, 1:2], accum_out=st[:, 2:3]
                                             ).then_inc(s_cex, 1)
                        for n in range(NBAT):
                            copy(("k", n), P, 512)
                        act.wait_ge(s_mx, K(1, 2))
                        nc.scalar.activation(prob[:, 0:PAST], ps[:, 0:4, :].rearrange("p a b -> p (a b)"), ACT.Exp,
                                             scale=SCALE, bias=st[:, 6:7], accum_out=st[:, 7:8])
                        nc.scalar.activation(prob[:, PAST:PAST + NS], ps[:, 4, 0:NS], ACT.Exp, scale=SCALE,
                                             bias=st[:, 6:7], accum_out=st[:, 8:9]).then_inc(s_ex, 1)
                        for c in range(NPG // 4):
                            copy(("p", c), P, 512)
                        copy(("pn", 0), NS, P, NS)
                        for b in range(2):
                            copy(("wk", b), P, 512)
                        act.wait_ge(s_mx, K(2, 2))
                        nc.scalar.activation(probw[:, 0:WIN], ps[:, 0, :], ACT.Exp, scale=SCALE, bias=st[:, 12:13],
                                             accum_out=st[:, 13:14])
                        nc.scalar.activation(probw[:, WIN:WIN + NS], ps[:, 1, 0:NS], ACT.Exp, scale=SCALE,
                                             bias=st[:, 12:13], accum_out=st[:, 14:15]).then_inc(s_ex, 1)
                        copy(("wp", 0), P, 512)
                        copy(("wpn", 0), NS, P, NS)
                        copy(("cp", 0), P, 2 * P)
                        act.wait_ge(s_comb, K(3, 3))
                        act.dma_start(attn_dram.rearrange("b h g t d -> (b h g t) d")[bass.ds(pi * P, P), :],
                                      o_row[:, :]).then_inc(s_ost, 16)
                        act.wait_ge(s_ost, 16 * pi + 16)

            @block.vector
            def _(dve):
                v = Order(dve, v_done)
                dve.wait_ge(s_int, 1)
                v.did(nc.vector.tensor_single_scalar(row_i[:, :], row_i[:, :], 7, ALU.bitwise_and))
                v.wait()
                v.did(nc.vector.tensor_copy(row_t[:, :], row_i[:, :]))
                v.did(nc.vector.tensor_copy(col_t[:, :], col_i[:, :]))
                v.wait()
                v.did(nc.vector.tensor_scalar(same[:, :], col_t[:, :], row_t[:, :], None, ALU.is_equal))
                v.did(nc.vector.tensor_scalar(causal8[:, :], col_t[:, 0:DS], row_t[:, :], None, ALU.is_le))
                v.wait()
                dve.wait_ge(s_const, 1)
                v.did(nc.vector.tensor_tensor(same[:, :], same[:, :], quad[:, :], ALU.mult))
                v.did(nc.vector.tensor_scalar(wpen[:, :], causal8[:, :], NEG, None, ALU.mult))
                v.did(nc.vector.tensor_tensor(
                    new_pen[:], own[:].unsqueeze(3).to_broadcast([P, PAIRS, DB, DS]),
                    causal8[:].unsqueeze(1).unsqueeze(1).to_broadcast([P, PAIRS, DB, DS]), ALU.mult))
                v.wait()
                v.did(nc.vector.tensor_scalar(new_pen[:], new_pen[:], -NEG, NEG, ALU.mult, ALU.add))
                for g in range(NG):
                    last = nc.vector.tensor_copy(q_nat[:, g, :, :],
                                                 new[:, 0:512].rearrange("p (h g d) -> p h g d", h=NKV, g=NG)[:, :, g, :])
                last.then_inc(s_qn, 1)
                dve.wait_ge(s_qt, 1)
                for h in range(NKV):
                    r = slice(h * HD, (h + 1) * HD)
                    nc.vector.tensor_copy(q_bd[r, :, h, :, :],
                                          ps[r, 5, 0:NG * NS].rearrange("p (g b t) -> p b g t", g=NG, b=DB))
                nc.vector.tensor_copy(k_new[:], ps[:, 5, NG * NS:(NG + 2) * NS].rearrange("p (n c) -> p n c", n=2)
                                      ).then_inc(s_qbd, 1)
                dve.wait_ge(s_qbd, 1)
                v.wait()
                nc.vector.memset(st[:, 22:23], 0.0).then_inc(s_const, 1)
                dve.wait_ge(s_kct, 1)
                nc.vector.tensor_copy(kcT[:], ps[:, 7, 0:2 * P].rearrange("p (a b) -> p a b", a=2)
                                      ).then_inc(s_kce, 1)
                with dve.Fori(0, PAIRS // 2) as it:
                    v.loop(it, DVE_PER_PAIRS)
                    for s in range(2):
                        pi = 2 * it + s
                        K = lambda n, per: pi * per + n
                        S4 = ps[:, 0:4, :].rearrange("p a b -> p (a b)")

                        def did(ins):
                            v.did(ins)
                            v.wait()

                        nc.vector.tensor_copy(q_pair[:, :], q_bd[:].rearrange("p b h g t -> p (b h g t)")[
                            :, bass.ds(pi * P, P)]).then_inc(s_qp, 1)
                        dve.wait_ge(s_csc, pi + 1)
                        did(nc.vector.tensor_tensor(
                            c_s[:],
                            ps[:, 7, 0:2 * P].rearrange("p (a b j) -> p a b j", a=2, b=DB),
                            own_pen[:, bass.ds(pi, 1), :].rearrange("p o b -> p (o b)").unsqueeze(1).unsqueeze(3)
                            .to_broadcast([P, 2, DB, NPG]), ALU.add))
                        did(nc.vector.tensor_reduce(st[:, 0:1], c_s[:].rearrange("p a b j -> p (a b j)"), AX, ALU.max))
                        nc.vector.tensor_scalar(st[:, 1:2], st[:, 0:1], -SCALE, None, ALU.mult).then_inc(s_cmx, 1)
                        dve.wait_ge(s_cex, pi + 1)
                        did(nc.vector.reciprocal(st[:, 3:4], st[:, 2:3]))
                        nc.vector.tensor_scalar(c_e[:, :], c_e[:, :], st[:, 3:4], None, ALU.mult).then_inc(s_cpn, 1)
                        dve.wait_ge(s_imp, pi + 1)
                        did(nc.vector.tensor_reduce(
                            imp[:, :].rearrange("p (j a) -> p a j", a=2),
                            ps[:, 7, 0:2 * P].rearrange("p (a b j) -> p a j b", a=2, b=DB), AX, ALU.add))
                        did(nc.vector.memset(imp[:, 0:1], FORCE))
                        did(nc.vector.memset(imp[:, NBLK - 1:NBLK], FORCE))
                        i_m = imp[:, :].unsqueeze(1).to_broadcast([P, NBLK, NBLK])
                        i_n = imp[:, :].unsqueeze(2).to_broadcast([P, NBLK, NBLK])
                        v.did(nc.vector.tensor_tensor(above[:], i_m, i_n, ALU.is_gt))
                        did(nc.vector.tensor_tensor(ties[:], i_m, i_n, ALU.is_equal))
                        did(nc.vector.tensor_tensor(ties[:], ties[:], before[:], ALU.mult))
                        did(nc.vector.tensor_tensor(above[:], above[:], ties[:], ALU.add))
                        did(nc.vector.tensor_reduce(rank[:, :], above[:], AX, ALU.add))
                        did(nc.vector.tensor_scalar(selpen[:, :], rank[:, :], KEEP - 0.5, NEG, ALU.is_gt, ALU.mult))
                        dve.wait_ge(s_sc, K(1, 2))
                        v.did(nc.vector.tensor_tensor(S4.rearrange("p (n l) -> p n l", l=CB),
                                                      S4.rearrange("p (n l) -> p n l", l=CB),
                                                      selpen[:, :].unsqueeze(2).to_broadcast([P, NBLK, CB]), ALU.add))
                        did(nc.vector.tensor_tensor(ps[:, 4, 0:NS], ps[:, 4, 0:NS],
                                                    new_pen[:, bass.ds(pi, 1)].rearrange("p o b t -> p (o b t)"),
                                                    ALU.add))
                        v.did(nc.vector.tensor_reduce(st[:, 4:5], S4, AX, ALU.max))
                        did(nc.vector.tensor_reduce(st[:, 5:6], ps[:, 4, 0:NS], AX, ALU.max))
                        did(nc.vector.tensor_tensor(st[:, 4:5], st[:, 4:5], st[:, 5:6], ALU.max))
                        nc.vector.tensor_scalar(st[:, 6:7], st[:, 4:5], -SCALE, None, ALU.mult).then_inc(s_mx, 1)

                        def factors(branch, sums):
                            if len(sums) == 2:
                                did(nc.vector.tensor_tensor(st[:, 16:17], st[:, sums[0]:sums[0] + 1],
                                                            st[:, sums[1]:sums[1] + 1], ALU.add))
                                did(nc.vector.reciprocal(st[:, 17:18], st[:, 16:17]))
                            else:
                                did(nc.vector.memset(st[:, 17:18], 1.0))
                            did(nc.vector.tensor_tensor(st[:, 17:18], st[:, 17:18],
                                                        gates[:, bass.ds(pi, 1), branch], ALU.mult))
                            did(nc.vector.tensor_scalar(st[:, 18:20], kvsel[:, :], st[:, 17:18], None, ALU.mult))

                        def combine(n):
                            if n == 0:
                                did(nc.vector.tensor_scalar(o_row[:, :], ps[:, 7, 0:HD], st[:, 18:19], None,
                                                            ALU.mult))
                            else:
                                did(nc.vector.scalar_tensor_tensor(o_row[:, :], ps[:, 7, 0:HD], st[:, 18:19],
                                                                   o_row[:, :], ALU.mult, ALU.add))
                            nc.vector.scalar_tensor_tensor(o_row[:, :], ps[:, 7, HD:ROW], st[:, 19:20],
                                                           o_row[:, :], ALU.mult, ALU.add).then_inc(s_comb, 1)
                            dve.wait_ge(s_comb, K(n + 1, 3))

                        dve.wait_ge(s_ex, K(1, 2))
                        factors(1, (7, 8))
                        dve.wait_ge(s_pv, K(1, 3))
                        combine(0)
                        dve.wait_ge(s_sc, K(2, 2))
                        v.did(nc.vector.tensor_tensor(ps[:, 0, 0:DS], ps[:, 0, 0:DS], wpen[:, :], ALU.add))
                        did(nc.vector.tensor_tensor(ps[:, 1, 0:NS], ps[:, 1, 0:NS],
                                                    new_pen[:, bass.ds(pi, 1)].rearrange("p o b t -> p (o b t)"),
                                                    ALU.add))
                        v.did(nc.vector.tensor_reduce(st[:, 10:11], ps[:, 0, :], AX, ALU.max))
                        did(nc.vector.tensor_reduce(st[:, 11:12], ps[:, 1, 0:NS], AX, ALU.max))
                        did(nc.vector.tensor_tensor(st[:, 10:11], st[:, 10:11], st[:, 11:12], ALU.max))
                        nc.vector.tensor_scalar(st[:, 12:13], st[:, 10:11], -SCALE, None, ALU.mult).then_inc(s_mx, 1)
                        dve.wait_ge(s_ex, K(2, 2))
                        factors(2, (13, 14))
                        dve.wait_ge(s_pv, K(2, 3))
                        combine(1)
                        factors(0, ())
                        dve.wait_ge(s_pv, K(3, 3))
                        combine(2)
                v.end_loop(PAIRS // 2)

def finish_rows(nc, sem, ident, pres, cmix_hi, cmix_lo, o_nsa, ps, z_dram, gla_dram, x_prompt, x_sample, norm_post,
                w_out, gla_a2, gla_ab, gla_norm, state_gla, y_prompt, y_sample, new_gla_p, new_gla_s):
    LEVELS = (64, 32, 16, 8)
    NL = len(LEVELS)
    BASE = 8
    LOG_A_MIN = -21.0
    E_BK, E_KD, E_BQ, E_IN = NL, NL + 1, NL + 2, NL + 3
    NE = NL + 4
    CHN = GH * GK
    LAST = NT

    with ExitStack() as ctx:
        sb = lambda name, shape, dt=F32: ctx.enter_context(nc.sbuf_tensor(name, shape, dt))
        flat = pres[:, :, :].rearrange("p a b -> p (a b)")
        at = [0]

        def part(*dims):
            n = int(np.prod(dims))
            at[0] += n
            assert at[0] <= (NT + 1) * NRES
            v = flat[:, at[0] - n:at[0]]
            if len(dims) == 2:
                v = v.rearrange("p (a b) -> p a b", a=dims[0])
            elif len(dims) == 3:
                v = v.rearrange("p (a b c) -> p a b c", a=dims[0], b=dims[1])
            return v

        s0 = part(DB, GH * GV)
        qE = [part(NL + 1, GH, P), part(NL + 1, GH, P)]
        kE = [part(NL + 2, P), sb("kE_1", [P, NL + 2, P])]
        post, yt = part(D), part(D)
        xr = [part(D), sb("xr_1", [P, D])]
        wo_raw = sb("wo_raw", [P, 2, D])
        wo_hi = sb("wo_hi", [P, KD, D], F32R)
        wo_lo = sb("wo_lo", [P, KD, D], F32R)
        gnorm = sb("gnorm", [P, GV])
        a2 = sb("a2", [GR, CHN])
        a_bias = sb("a_bias", [1, CHN])
        ones = sb("ones", [1, P])
        qka = sb("qka", [P, 2 * CHN + GR])
        vt = sb("vt", [P, GH * GV])
        zt = sb("zt", [P, 2, WZ])
        qT = sb("qT_g", [P, P])
        q_bd = sb("q_bd_g", [P, GH, P])
        kT = sb("kT_g", [P, P])
        aT = sb("aT_g", [GR, P])
        lg = sb("lg", [P, CHN])
        lneg = sb("lneg", [P, CHN])
        lu = sb("lu", [P, CHN])
        log_a = sb("log_a", [P, CHN])
        bT = sb("bT", [P, P])
        dec = [sb(f"dec_{n}", [P, NE, P]) for n in range(2)]
        qi = [sb(f"qi_{n}", [P, P]) for n in range(2)]
        att = sb("att", [P, GH, P])
        kd = sb("kd", [P, CHN])
        state = sb("state", [P, GH * GV])
        upd = sb("upd", [P, GH * GV])
        bdm = sb("bdm", [P, GH, GV])
        o_g = sb("o_g", [P, GH, GV])
        o_sq = sb("o_sq", [P, GH, GV])
        st = sb("st_d", [P, 16])
        mix = sb("mix", [P, 6 * P])
        m_hi = sb("m_hi", [P, KD, P], F32R)
        m_lo = sb("m_lo", [P, KD, P], F32R)
        eps = sb("eps_d", [P, 1])
        one = sb("one_d", [P, 1])
        upper = sb("upper", [P, P])
        masks = sb("masks", [P, NL, P], I32)
        base_m = sb("base_m", [P, P])
        mk = sb("mk", [P, P])
        ri = sb("ri", [P, 1], I32)
        rj = sb("rj", [P, 2], I32)
        rf = sb("rf", [P, 3])
        ci = sb("ci", [P, P], I32)
        cj = sb("cj", [P, P], I32)
        cf = sb("cf", [P, P])
        qi_b = part(DB * (NS + DS))
        kd_b = qE[1].rearrange("p e h t -> p (e h t)")[0:NS, 0:DB * CHN].rearrange("p (b k) -> p b k", b=DB)
        seq_m = sb("seq_m", [NS, DB])

        s_wr = [sem("wo_loaded_0"), sem("wo_loaded_1")]
        s_wh, s_wl = sem("wo_hi_ready"), sem("wo_lo_ready")
        s_cst = sem("small_loaded_d")
        s_s0z, s_s0 = sem("s0_zeroed"), sem("s0_loaded")
        s_qka, s_v, s_z, s_x = sem("qka_loaded"), sem("v_loaded"), sem("z_loaded"), [
            sem("x_loaded_d0"), sem("x_loaded_d1")]
        s_int, s_mask = sem("int_consts_d"), sem("masks_ready")
        s_t1, s_aT, s_qT = sem("qka_turned"), sem("a_turned"), sem("q_turned_d")
        s_lg, s_lgc, s_ls, s_la = sem("logits"), sem("logits_copied"), sem("log1p_done"), sem("log_a_ready")
        s_cs, s_bT, s_D, s_E, s_kq = sem("b_summed"), sem("b_copied"), sem("exponents"), sem("decays"), \
            sem("kq_decayed")
        s_at, s_atr = sem("att_product"), sem("att_taken")
        s_kd, s_kdc, s_o, s_on = sem("kd_turned"), sem("kd_copied"), sem("o_summed"), sem("o_taken")
        s_up, s_st = sem("update_product"), sem("state_ready")
        s_sq, s_ms, s_r4 = sem("o_squared"), sem("o_mean"), sem("o_rms")
        s_mix, s_mt, s_mh, s_ml, s_cm = sem("mix_ready"), sem("mix_turned"), sem("mix_hi"), sem("mix_lo"), \
            sem("conv_mixed")
        s_op, s_rr, s_y, s_ys = sem("out_product"), sem("out_rms"), sem("y_ready"), sem("y_stored")
        s_new = sem("states_stored")
        s_kdm = sem("kd_masked")
        v_done, a_done, g_done = sem("dve_done_d"), sem("act_done_d"), sem("pool_done_d")

        OUT_PARTS = {"out0": (0, 0, 2), "out1": (0, 2, KD), "out2": (1, 0, KD)}
        MIX = [n * P for n in (0, 1, 2, 3, 0, 1)]

        def ge(eng, s, n):
            if not isinstance(n, int) or n > 0:
                eng.wait_ge(s, n)

        LAG = {"att": 1, "kd": 1, "o": 1, "update": 1, "rms": 1, "mixturn": 1, "mixhi": 1, "mixlo": 1, "conv": 1,
               "z": 1, "out": 2, "out0": 2, "out1": 2, "out2": 2, "resid": 2, "store": 2}

        def rounds(eng, order, run, own=None, per=0):
            def one(r, parity):
                for x in order:
                    lag = LAG.get(x, 0)
                    t = r - lag
                    if not isinstance(r, int):
                        run(x, t, (parity - lag) % 2, P, False)
                    elif 0 <= t <= LAST:
                        run(x, t, t % 2, NS if t == LAST else P, t == LAST)

            one(0, 0)
            one(1, 1)
            with eng.Fori(1, NT // 2) as it:
                if own:
                    own.loop(it, per, 1)
                for parity in range(2):
                    one(2 * it + parity, parity)
            if own:
                own.end_loop(NT // 2 - 1)
            for r in range(NT, NT + 3):
                one(r, r % 2)

        with nc.Block() as block:

            @block.sync
            def _(sp):
                sp.dma_start(wo_raw[:, 0, :], w_out[0, 0:P, :]).then_inc(s_wr[0], 16)
                sp.dma_start(wo_raw[:, 1, :], w_out[0, P:2 * P, :]).then_inc(s_wr[1], 16)
                sp.dma_start(a2[:, :], gla_a2[0]).then_inc(s_cst, 16)
                sp.dma_start(a_bias[:, :], gla_ab[0:1, :]).then_inc(s_cst, 16)
                sp.dma_start(gnorm[:, :], gla_norm[0:1, :].to_broadcast([P, GV])).then_inc(s_cst, 16)
                sp.dma_start(post[:, :], norm_post[0:1, :].to_broadcast([P, D])).then_inc(s_cst, 16)

                def run(x, t, slot, rows, sample):
                    g = gla_dram.rearrange("r a c -> r (a c)")[bass.ds(t * P, rows), :]
                    if x == "qk":
                        ge(sp, s_t1, t)
                        sp.dma_start(qka[0:rows, 0:2 * CHN], g[:, 0:2 * CHN]).then_inc(s_qka, 16)
                        sp.dma_start(qka[0:rows, 2 * CHN:], g[:, C_GA - C_GQ:NGL]).then_inc(s_qka, 16)
                    elif x == "v":
                        ge(sp, s_up, t)
                        sp.dma_start(vt[0:rows, :], g[:, 2 * CHN:2 * CHN + GH * GV]).then_inc(s_v, 16)
                    elif x == "resid":
                        ge(sp, s_y, t + 1)
                        src = x_sample.rearrange("b t d -> (b t) d") if sample else x_prompt[0, bass.ds(t * P, P), :]
                        sp.dma_start(xr[slot][0:rows, :], src).then_inc(s_x[slot], 16)
                    elif x == "weights" and isinstance(t, int) and t == 0:
                        for k in range(2, KD):
                            sp.wait_ge(s_wl, k - 1)
                            sp.dma_start(wo_raw[:, k % 2, :], w_out[0, k * P:(k + 1) * P, :]
                                         ).then_inc(s_wr[k % 2], 16)
                        sp.wait_ge(s_s0z, 1)
                        for h in range(GH):
                            sp.dma_start(s0[h * GK:(h + 1) * GK, :, h * GV:(h + 1) * GV],
                                         state_gla[0, :, h].rearrange("b k v -> k b v")).then_inc(s_s0, 16)

                rounds(sp, ("qk", "resid", "v", "weights"), run)
                sp.wait_ge(s_st, NT + DB)
                for h in range(GH):
                    r, c = slice(h * GK, (h + 1) * GK), slice(h * GV, (h + 1) * GV)
                    sp.dma_start(new_gla_p[0, 0, h], state[r, c]).then_inc(s_new, 16)
                    sp.dma_start(new_gla_s[0, :, h].rearrange("b k v -> k b v"), s0[r, :, c]).then_inc(s_new, 16)
                sp.wait_ge(s_new, 16 * 2 * GH)

            @block.gpsimd
            def _(pool):
                g = Order(pool, g_done)
                g.did(nc.gpsimd.memset(s0, 0.0))
                g.wait()
                g.did(nc.gpsimd.iota(ri[:, :], pattern=[[0, 1]], base=0, channel_multiplier=1))
                g.did(nc.gpsimd.iota(ci[:, :], pattern=[[1, P]], base=0, channel_multiplier=0))
                for m, x in ((upper, 1.0), (q_bd, 0.0), (bdm, 0.0), (state, 0.0), (ones, 1.0), (qi_b, 0.0),
                             (seq_m, 1.0)):
                    g.did(nc.gpsimd.memset(m if m is qi_b else m[:], x))
                g.wait()
                nc.gpsimd.memset(one[:, :], 1.0).then_inc(s_s0z, 1)
                g.did(nc.gpsimd.affine_select(out=upper[:, :], in_=upper[:, :], compare_op=ALU.is_ge, fill=0.0,
                                              base=0, pattern=[[1, P]], channel_multiplier=-1))
                g.did(nc.gpsimd.affine_select(out=seq_m[:, :], in_=seq_m[:, :], compare_op=ALU.is_ge, fill=0.0,
                                              base=0, pattern=[[-DS, DB]], channel_multiplier=1))
                g.wait()
                g.did(nc.gpsimd.affine_select(out=seq_m[:, :], in_=seq_m[:, :], compare_op=ALU.is_ge, fill=0.0,
                                              base=DS - 1, pattern=[[DS, DB]], channel_multiplier=-1))
                for h in range(GH):
                    g.did(nc.gpsimd.memset(bdm[h * GK:(h + 1) * GK, h, :], 1.0))
                    g.wait()
                nc.gpsimd.memset(eps[:, :], EPS).then_inc(s_int, 1)

                def run(x, t, slot, rows, sample):
                    if x == "conv":
                        ge(pool, s_op, 2 * t)
                        for src, dst in ((cmix_hi, m_hi), (cmix_lo, m_lo)):
                            nc.gpsimd.tensor_copy(dst[:, 6:KD, 0:rows],
                                                  src[:, :, bass.ds(t * P, rows)].bitcast(F32)).then_inc(s_cm, 1)
                    elif x == "weights" and isinstance(t, int) and t == 0:
                        for k in range(KD):
                            pool.wait_ge(s_wr[k % 2], 16 * (k // 2) + 16)
                            nc.gpsimd.tensor_copy(wo_hi[:, k, :], wo_raw[:, k % 2, :]).then_inc(s_wh, 1)
                            pool.wait_ge(s_wh, k + 1)
                            nc.gpsimd.tensor_tensor(wo_lo[:, k, :], wo_raw[:, k % 2, :], wo_hi[:, k, :].bitcast(F32),
                                                    ALU.subtract).then_inc(s_wl, 1)
                    elif x == "z":
                        ge(pool, s_mix, t)
                        pool.dma_start(zt[0:rows, :, :], z_dram[bass.ds(t * P, rows), :, :]).then_inc(s_z, 16)

                rounds(pool, ("z", "weights", "conv"), run)

            @block.tensor
            def _(pe):
                def run(x, t, slot, rows, sample):
                    R = rows
                    if x == "turn":
                        pe.wait_ge(s_qka, 32 * t + 32)
                        ge(pe, s_bT, t)
                        for n, (c, w) in enumerate(((0, CHN), (CHN, CHN), (2 * CHN, GR))):
                            mm = nc.tensor.transpose(ps[0:w, 0, n * P:n * P + R], qka[0:R, c:c + w], ident[0:R, 0:R])
                        mm.then_inc(s_t1, 1)
                    elif x == "logits":
                        pe.wait_ge(s_aT, t + 1)
                        pe.wait_ge(s_qT, t + 1)
                        nc.tensor.matmul(ps[0:R, 0, 3 * P:3 * P + CHN], aT[:, 0:R], a2[:, :], start=True, stop=False)
                        nc.tensor.matmul(ps[0:R, 0, 3 * P:3 * P + CHN], ones[:, 0:R], a_bias[:, :], start=False,
                                         stop=True).then_inc(s_lg, 1)
                    elif x in OUT_PARTS:
                        half, k0, k1 = OUT_PARTS[x]
                        if x == "out0":
                            pe.wait_ge(s_wl, KD)
                            pe.wait_ge(s_ml, t + 1)
                            pe.wait_ge(s_cm, 2 * t + 2)
                            ge(pe, s_y, t + 2)
                        for k in range(k0, k1):
                            for n, (l, w) in enumerate(((m_hi, wo_hi), (m_hi, wo_lo), (m_lo, wo_hi))):
                                mm = nc.tensor.matmul(ps[0:R, 2 + half, :], l[:, k, 0:R],
                                                      w[:, k, half * 512:(half + 1) * 512],
                                                      start=(k == 0 and n == 0), stop=(k == KD - 1 and n == 2))
                        if k1 == KD:
                            mm.then_inc(s_op, 1)
                    elif x == "sum":
                        pe.wait_ge(s_la, t + 1)
                        nc.tensor.matmul(ps[:, 0, 3 * P:3 * P + R], log_a[0:R, :], (base_m if sample else upper)[0:R, 0:R],
                                         start=True, stop=True).then_inc(s_cs, 1)
                    elif x == "att":
                        pe.wait_ge(s_kq, t + 1)
                        base = (NL + 1) * t
                        for e in range(1 if sample else NL + 1):
                            ge(pe, s_atr, base + e - 1 if not isinstance(t, int) or t > 0 or e > 1 else 0)
                            if e == 1:
                                ge(pe, s_kdc, t)
                            k = E_BK if e == 0 else e - 1
                            mm = nc.tensor.matmul(ps[0:R, 4 + e % 2, :].rearrange("p (h t) -> p h t", h=GH)[:, :, 0:R],
                                                  kE[slot][:, k, 0:R], qE[slot][:, e, :, 0:R], start=True, stop=True)
                            mm.then_inc(s_at, 1)
                    elif x == "kd":
                        ge(pe, s_kdc, t)
                        if not sample:
                            pe.wait_ge(s_atr, (NL + 1) * t + 4)
                        nc.tensor.transpose(ps[0:R, 5, 0:CHN], kE[slot][:, E_KD, 0:R], ident[:, :]
                                            ).then_inc(s_kd, 1)
                    elif x == "o":
                        pe.wait_ge(s_atr, (NL + 1) * t + (1 if sample else NL + 1))
                        ge(pe, s_on, t)
                        pe.wait_ge(s_v, 16 * t + 16)
                        if sample:
                            pe.wait_ge(s_s0, 16 * GH)
                            pe.wait_ge(s_st, NT)
                            for b in range(DB):
                                nc.tensor.matmul(ps[0:R, 6, 0:GH * GV], qi_b[:, b * NS:(b + 1) * NS], s0[:, b, :],
                                                 start=(b == 0), stop=False, skip_group_check=True)
                        else:
                            ge(pe, s_st, t)
                            nc.tensor.matmul(ps[0:R, 6, 0:GH * GV], qi[slot][:, 0:R], state[:, :], start=True,
                                             stop=False, skip_group_check=True)
                        for h in range(GH):
                            mm = nc.tensor.matmul(ps[0:R, 6, h * GV:(h + 1) * GV], att[0:R, h, 0:R],
                                                  vt[0:R, h * GV:(h + 1) * GV], start=False, stop=(h == GH - 1),
                                                  skip_group_check=True)
                        mm.then_inc(s_o, 1)
                    elif x == "update":
                        pe.wait_ge(s_kdc, t + 1)
                        ge(pe, s_ml, t)
                        if not sample:
                            nc.tensor.matmul(ps[:, 7, 0:GH * GV], kd[0:R, :], vt[0:R, :], start=True,
                                             stop=True).then_inc(s_up, 1)
                        else:
                            pe.wait_ge(s_kdm, 1)
                            for b in range(DB):
                                if b > 0:
                                    pe.wait_ge(s_st, NT + b)
                                nc.tensor.matmul(ps[:, 7, 0:GH * GV], kd_b[:, b, :], vt[0:R, :], start=True,
                                                 stop=True).then_inc(s_up, 1)
                    elif x == "mixturn":
                        pe.wait_ge(s_mix, t + 1)
                        pe.wait_ge(s_st, t + (DB if sample else 1))
                        for n in range(6):
                            mm = nc.tensor.transpose(ps[:, 7 if n < 4 else 1, MIX[n]:MIX[n] + R],
                                                     mix[0:R, n * P:(n + 1) * P], ident[0:R, 0:R])
                        mm.then_inc(s_mt, 1)

                pe.wait_ge(s_int, 1)
                pe.wait_ge(s_cst, 64)
                rounds(pe, ("turn", "att", "logits", "out0", "sum", "kd", "o", "update", "out1", "out2", "mixturn"), run)

            @block.scalar
            def _(act):
                a = Order(act, a_done)

                def did(ins):
                    a.did(ins)
                    a.wait()

                def run(x, t, slot, rows, sample):
                    R = rows
                    if x == "turn":
                        act.wait_ge(s_t1, t + 1)
                        ge(act, s_kq, t)
                        nc.scalar.activation(kT[:, 0:R], ps[:, 0, P:P + R], ACT.Copy)
                        nc.scalar.activation(aT[:, 0:R], ps[0:GR, 0, 2 * P:2 * P + R], ACT.Copy).then_inc(s_aT, 1)
                    elif x == "softplus":
                        act.wait_ge(s_lgc, t + 1)
                        did(nc.scalar.activation(lu[0:R, :], lg[0:R, :], ACT.Abs))
                        did(nc.scalar.activation(lu[0:R, :], lu[0:R, :], ACT.Exp, scale=-1.0))
                        nc.scalar.activation(lu[0:R, :], lu[0:R, :], ACT.Ln, bias=one[0:R, :]).then_inc(s_ls, 1)
                    elif x == "decay":
                        act.wait_ge(s_D, t + 1)
                        n0 = E_BK if sample else 0
                        nc.scalar.activation(dec[slot][:, n0:NE, 0:R], dec[slot][:, n0:NE, 0:R], ACT.Exp).then_inc(s_E, 1)
                    elif x == "out":
                        act.wait_ge(s_op, 2 * t + 2)
                        act.wait_ge(s_ys, 16 * t + 1)
                        did(nc.scalar.activation(yt[0:R, :], ps[0:R, 2:4, :].rearrange("p a b -> p (a b)"),
                                                 ACT.Square, accum_out=st[0:R, 8:9]))
                        did(nc.scalar.activation(st[0:R, 9:10], st[0:R, 8:9], ACT.Ln, scale=1.0 / D,
                                                 bias=eps[0:R, :]))
                        nc.scalar.activation(st[0:R, 10:11], st[0:R, 9:10], ACT.Exp, scale=-0.5).then_inc(s_rr, 1)
                    elif x == "kd":
                        act.wait_ge(s_kd, t + 1)
                        nc.scalar.activation(kd[0:R, :], ps[0:R, 5, 0:CHN], ACT.Copy).then_inc(s_kdc, 1)
                    elif x == "rms":
                        act.wait_ge(s_on, t + 1)
                        nc.scalar.activation(o_sq[0:R], o_g[0:R], ACT.Square).then_inc(s_sq, 1)
                        act.wait_ge(s_ms, t + 1)
                        did(nc.scalar.activation(st[0:R, 4:8], st[0:R, 0:4], ACT.Ln, scale=1.0 / GV,
                                                 bias=eps[0:R, :]))
                        nc.scalar.activation(st[0:R, 4:8], st[0:R, 4:8], ACT.Exp, scale=-0.5).then_inc(s_r4, 1)
                    elif x == "mixhi":
                        act.wait_ge(s_mt, t + 1)
                        ge(act, s_op, 2 * t)
                        for bank, k0, k1 in ((7, 0, 4), (1, 4, 6)):
                            last = nc.scalar.activation(
                                m_hi[:, k0:k1, 0:R],
                                ps[:, bank, MIX[k0]:MIX[k0] + (k1 - k0) * P].rearrange("p (k c) -> p k c", c=P)[:, :, 0:R], ACT.Copy)
                        last.then_inc(s_mh, 1)
                    elif x == "store":
                        act.wait_ge(s_y, t + 3)
                        dst = (y_sample.rearrange("b t d -> (b t) d") if sample else
                               y_prompt[0, bass.ds(t * P, P), :])
                        act.dma_start(dst, yt[0:rows, :]).then_inc(s_ys, 16)

                nc.scalar.preload_act_table_set("natural_log_exp_and_others")
                act.wait_ge(s_int, 1)
                act.wait_ge(s_cst, 64)
                rounds(act, ("turn", "softplus", "kd", "decay", "rms", "out", "mixhi", "store"), run, a, 2 * 5)
                act.wait_ge(s_ys, 16 * (NT + 1) + 1)

            @block.vector
            def _(dve):
                v = Order(dve, v_done)

                def did(ins):
                    v.did(ins)
                    v.wait()

                def run(x, t, slot, rows, sample):
                    R = rows
                    if x == "turn":
                        dve.wait_ge(s_aT, t + 1)
                        for h in range(GH):
                            r = slice(h * GK, (h + 1) * GK)
                            nc.vector.tensor_scalar(q_bd[r, h, 0:R], ps[r, 0, 0:R], GK ** -0.5, None, ALU.mult)
                        nc.vector.tensor_scalar(qT[:, 0:R], ps[:, 0, 0:R], GK ** -0.5, None,
                                                ALU.mult).then_inc(s_qT, 1)
                    elif x == "softplus":
                        dve.wait_ge(s_lg, t + 1)
                        nc.vector.tensor_copy(lg[0:R, :], ps[0:R, 0, 3 * P:3 * P + CHN]).then_inc(s_lgc, 1)
                        dve.wait_ge(s_lgc, t + 1)
                        v.did(nc.vector.tensor_scalar(lneg[0:R, :], lg[0:R, :], 0.0, None, ALU.min))
                    elif x == "log_a":
                        v.wait()
                        dve.wait_ge(s_ls, t + 1)
                        did(nc.vector.tensor_tensor(lneg[0:R, :], lneg[0:R, :], lu[0:R, :], ALU.subtract))
                        nc.vector.tensor_scalar(log_a[0:R, :], lneg[0:R, :], 1.0 / TAU, LOG_A_MIN, ALU.mult,
                                                ALU.max).then_inc(s_la, 1)
                    elif x == "decay":
                        dve.wait_ge(s_cs, t + 1)
                        nc.vector.tensor_copy(bT[:, 0:R], ps[:, 0, 3 * P:3 * P + R]).then_inc(s_bT, 1)
                        dve.wait_ge(s_bT, t + 1)
                        if not sample:
                            for e, L in enumerate(LEVELS):
                                b = bT[:, :].rearrange("p (n a l) -> p n a l", a=2, l=L)
                                d = dec[slot][:, e, :].rearrange("p (n a l) -> p n a l", a=2, l=L)
                                n = P // (2 * L)
                                r = b[:, :, 0, L - 1:L].to_broadcast([P, n, L])
                                nc.vector.tensor_tensor(d[:, :, 0, :], r, b[:, :, 0, :], ALU.subtract)
                                nc.vector.tensor_tensor(d[:, :, 1, :], b[:, :, 1, :], r, ALU.subtract)
                        b8 = bT[:, 0:R].rearrange("p (n l) -> p n l", l=BASE)
                        c8 = b8[:, :, BASE // 2 - 1:BASE // 2].to_broadcast([P, R // BASE, BASE])
                        v8 = lambda e: dec[slot][:, e, 0:R].rearrange("p (n l) -> p n l", l=BASE)
                        nc.vector.tensor_tensor(v8(E_BK), c8, b8, ALU.subtract)
                        nc.vector.tensor_tensor(v8(E_BQ), b8, c8, ALU.subtract)
                        nc.vector.tensor_copy(dec[slot][:, E_IN, 0:R], bT[:, 0:R])
                        end = (b8[:, :, BASE - 1:BASE].to_broadcast([P, R // BASE, BASE]) if sample else
                               bT[:, P - 1:P].to_broadcast([P, P]))
                        nc.vector.tensor_tensor(v8(E_KD) if sample else dec[slot][:, E_KD, :], end,
                                                b8 if sample else bT[:, :], ALU.subtract).then_inc(s_D, 1)
                    elif x == "decayed":
                        dve.wait_ge(s_E, t + 1)
                        dve.wait_ge(s_qT, t + 1)
                        if not isinstance(t, int) or t >= 2:
                            dve.wait_ge(s_up, t - 1)
                        n0 = E_BK if sample else 0
                        nc.vector.tensor_tensor(kE[slot][:, n0:NL + 2, 0:R], dec[slot][:, n0:NL + 2, 0:R],
                                                kT[:, 0:R].unsqueeze(1).to_broadcast([P, NL + 2 - n0, R]), ALU.mult)
                        for e in range(1 if sample else NL + 1):
                            nc.vector.tensor_tensor(
                                qE[slot][:, e, :, 0:R], q_bd[:, :, 0:R],
                                dec[slot][:, E_BQ if e == 0 else e - 1, 0:R].unsqueeze(1).to_broadcast([P, GH, R]),
                                ALU.mult)
                        if sample:
                            nc.vector.tensor_tensor(
                                qi_b[:, :].rearrange("p (b x) -> p b x", b=DB)[:, :, 0:DS],
                                qT[:, 0:R].rearrange("p (b t) -> p b t", b=DB),
                                dec[slot][:, E_IN, 0:R].rearrange("p (b t) -> p b t", b=DB), ALU.mult).then_inc(s_kq, 1)
                        else:
                            nc.vector.tensor_tensor(qi[slot][:, 0:R], qT[:, 0:R], dec[slot][:, E_IN, 0:R],
                                                    ALU.mult).then_inc(s_kq, 1)
                    elif x == "out":
                        dve.wait_ge(s_rr, t + 1)
                        dve.wait_ge(s_x[slot], 8 * (t - slot) + 16)
                        dve.wait_ge(s_ys, 16 * t + 1)
                        did(nc.vector.scalar_tensor_tensor(
                            yt[0:R, :], ps[0:R, 2:4, :].rearrange("p a b -> p (a b)"), st[0:R, 10:11],
                            post[0:R, :], ALU.mult, ALU.mult))
                        nc.vector.tensor_tensor(yt[0:R, :], yt[0:R, :], xr[slot][0:R, :], ALU.add).then_inc(s_y, 1)
                    elif x == "att":
                        base = (NL + 1) * t
                        for e in range(1 if sample else NL + 1):
                            dve.wait_ge(s_at, base + e + 1)
                            src = ps[0:R, 4 + e % 2, :].rearrange("p (h t) -> p h t", h=GH)[:, :, 0:R]
                            if e == 0:
                                ins = nc.vector.tensor_tensor(att[0:R, :, 0:R], src, base_m[0:R, 0:R].unsqueeze(
                                    1).to_broadcast([R, GH, R]), ALU.mult)
                            else:
                                dve.wait_ge(s_atr, base + e)
                                nc.vector.memset(st[:, 11:12], 0.0)
                                ins = nc.vector.copy_predicated(
                                    att[:, :, :], masks[:, e - 1, :].unsqueeze(1).to_broadcast([P, GH, P]), src)
                            ins.then_inc(s_atr, 1)
                    elif x == "o":
                        dve.wait_ge(s_o, t + 1)
                        nc.vector.tensor_copy(o_g[0:R], ps[0:R, 6, 0:GH * GV].rearrange("p (h v) -> p h v", h=GH)
                                              ).then_inc(s_on, 1)
                    elif x == "update":
                        if not sample:
                            dve.wait_ge(s_up, t + 1)
                            did(nc.vector.tensor_tensor(upd[:, :], ps[:, 7, 0:GH * GV],
                                                        bdm[:].rearrange("p h v -> p (h v)"), ALU.mult))
                            nc.vector.scalar_tensor_tensor(state[:, :], state[:, :], dec[slot][:, E_IN, P - 1:P],
                                                           upd[:, :], ALU.mult, ALU.add).then_inc(s_st, 1)
                        else:
                            dve.wait_ge(s_kdc, t + 1)
                            nc.vector.tensor_tensor(
                                kd_b, kd[0:NS, :].unsqueeze(1).to_broadcast([NS, DB, CHN]),
                                seq_m[:, :].unsqueeze(2).to_broadcast([NS, DB, CHN]), ALU.mult).then_inc(s_kdm, 1)
                            for b in range(DB):
                                dve.wait_ge(s_up, NT + b + 1)
                                nc.vector.scalar_tensor_tensor(
                                    s0[:, b, :], s0[:, b, :], dec[slot][:, E_IN, b * DS + DS - 1:b * DS + DS],
                                    ps[:, 7, 0:GH * GV], ALU.mult, ALU.add).then_inc(s_st, 1)
                    elif x == "rms":
                        dve.wait_ge(s_sq, t + 1)
                        nc.vector.tensor_reduce(st[0:R, 0:4], o_sq[0:R], AX, ALU.add).then_inc(s_ms, 1)
                        dve.wait_ge(s_z, 16 * t + 16)
                        nc.vector.tensor_tensor(
                            mix[0:R, 0:512].rearrange("p (a c) -> p a c", a=2),
                            o_nsa[0:R, bass.ds(t, 1), :].rearrange("p o (a c) -> p (o a) c", a=2),
                            zt[0:R, :, 0:256], ALU.mult)
                        dve.wait_ge(s_r4, t + 1)
                        did(nc.vector.tensor_tensor(o_g[0:R], o_g[0:R],
                                                    st[0:R, 4:8].unsqueeze(2).to_broadcast([R, GH, GV]), ALU.mult))
                        did(nc.vector.tensor_tensor(o_g[0:R], o_g[0:R],
                                                    gnorm[0:R, :].unsqueeze(1).to_broadcast([R, GH, GV]), ALU.mult))
                        nc.vector.tensor_tensor(
                            mix[0:R, 512:768].rearrange("p (a c) -> p a c", a=2),
                            o_g[0:R].rearrange("p (a h) v -> p a (h v)", a=2), zt[0:R, :, 256:WZ],
                            ALU.mult).then_inc(s_mix, 1)
                    elif x == "mixlo":
                        dve.wait_ge(s_mh, t + 1)
                        for bank, k0, k1 in ((7, 0, 4), (1, 4, 6)):
                            last = nc.vector.tensor_tensor(
                                m_lo[:, k0:k1, 0:R],
                                ps[:, bank, MIX[k0]:MIX[k0] + (k1 - k0) * P].rearrange("p (k c) -> p k c", c=P)[:, :, 0:R],
                                m_hi[:, k0:k1, 0:R].bitcast(F32), ALU.subtract)
                        last.then_inc(s_ml, 1)

                for s, n in ((s_y, 2), (s_ys, 1)):
                    nc.vector.memset(st[:, 11:12], 0.0).then_inc(s, n)
                    dve.wait_ge(s, n)
                dve.wait_ge(s_int, 1)
                for e, L in enumerate(LEVELS + (BASE,)):
                    sh = L.bit_length() - 1
                    v.did(nc.vector.tensor_single_scalar(rj[:, 0:1], ri[:, :], sh, ALU.logical_shift_right))
                    did(nc.vector.tensor_single_scalar(cj[:, :], ci[:, :], sh, ALU.logical_shift_right))
                    v.did(nc.vector.tensor_single_scalar(rj[:, 1:2], rj[:, 0:1], 1, ALU.bitwise_and))
                    did(nc.vector.tensor_copy(cf[:, :], cj[:, :]))
                    v.did(nc.vector.tensor_scalar(rf[:, 0:1], rj[:, 0:1], 0.0 if e == NL else 1.0, None, ALU.add))
                    did(nc.vector.tensor_scalar(rf[:, 1:2], rj[:, 1:2], -1.0, 1.0, ALU.mult, ALU.add))
                    if e < NL:
                        did(nc.vector.tensor_scalar(mk[:, :], cf[:, :], rf[:, 0:1], rf[:, 1:2], ALU.is_equal,
                                                    ALU.mult))
                        did(nc.vector.tensor_copy(masks[:, e, :], mk[:, :]))
                    else:
                        did(nc.vector.tensor_scalar(mk[:, :], cf[:, :], rf[:, 0:1], None, ALU.is_equal))
                        nc.vector.tensor_tensor(base_m[:, :], mk[:, :], upper[:, :], ALU.mult).then_inc(s_mask, 1)
                dve.wait_ge(s_mask, 1)
                dve.wait_ge(s_cst, 64)
                rounds(dve, ("turn", "att", "softplus", "log_a", "o", "decay", "update", "decayed", "rms", "out",
                             "mixlo"), run, v, 2 * 6)


_INS = ["x_prompt", "x_sample", "cache_cmp_kv", "cache_slc_kv", "cache_win_kv", "state_gla", "state_conv",
        "page_table", "norm_pre", "norm_post", "w_in", "w_out", "w_cmp_k", "w_cmp_v", "gla_a2", "gla_ab",
        "gla_norm", "conv_w"]
_OUTS = [(1, SEQ, D), (DB, DS, D), (1, 1, SEQ, 2, NKV, HD), (1, DB, DS, 2, NKV, HD), (1, 1, SEQ, 2, NKV, HD),
         (1, DB, DS, 2, NKV, HD), (1, 1, WIN, 2, NKV, HD), (1, DB, WIN, 2, NKV, HD), (1, 1, GH, GK, GV),
         (1, DB, GH, GK, GV), (1, 1, CK - 1, CW), (1, DB, CK - 1, CW)]


def kernel(**inputs):
    import concourse.bacc as bacc
    from concourse.bass_utils import run_bass_kernel_spmd

    nc = bacc.Bacc("TRN2", target_bir_lowering=False, num_devices=1)
    arrays, args = {}, []
    for name in _INS:
        a = np.ascontiguousarray(inputs[name])
        arrays[f"in_{name}"] = a
        args.append(nc.dram_tensor(f"in_{name}", a.shape, mybir.dt.from_np(a.dtype), kind="ExternalInput").ap())
    for i, shape in enumerate(_OUTS):
        args.append(nc.dram_tensor(f"out_{i}", shape, F32, kind="ExternalOutput").ap())
    with nc.allow_non_contiguous_dma(reason="small columns of weights and states"):
        hybrid_step(nc, *args)
    r = run_bass_kernel_spmd(nc, [arrays], core_ids=[0])
    return tuple(r.results[0][f"out_{i}"] for i in range(len(_OUTS)))
```
